# Optimizing a Trainium2 kernel written in Bass

```python
import jax, jax.numpy as jnp
from jax import lax
import numpy as np

D_MODEL = 1024
BATCH = 1
SEQ = 1024
DEPTH = 1

N_META = 16
HEAD_DIM = 64
ATTN_HEADS = 8
ATTN_WIDTH = ATTN_HEADS * HEAD_DIM
CONV_WIDTH = D_MODEL - ATTN_WIDTH
CONV_GROUPS = CONV_WIDTH // HEAD_DIM
CONV_K = 3
BLOCK_Q = 128
N_EXPERT_GROUPS = 4
EXPERTS_PER_GROUP = 8
N_EXPERTS = N_EXPERT_GROUPS * EXPERTS_PER_GROUP
TOP_K = 2
D_EXPERT = 512
EXPERT_BLOCK = 128
EPS = 1e-6
MASK_VALUE = -1e30
SPLIT_SIZES = (ATTN_WIDTH, ATTN_WIDTH, ATTN_WIDTH, ATTN_HEADS, CONV_WIDTH, CONV_WIDTH, CONV_WIDTH)
PROJ_COLS = sum(SPLIT_SIZES)
SPLIT_POINTS = tuple(int(p) for p in np.cumsum(SPLIT_SIZES)[:-1])

kernel_name = "hymba_fox_shortconv_hiermoe_block"

def rms_norm(x, g):
    xf = x.astype(jnp.float32)
    y = xf * lax.rsqrt(jnp.mean(xf * xf, axis=-1, keepdims=True) + EPS)
    return (y * g.astype(jnp.float32)).astype(x.dtype)

def forgetting_attention(q, k, v, log_f):
    Bsz, T, H, Dh = q.shape
    pad = (-T) % BLOCK_Q
    pw = ((0, 0), (pad, 0), (0, 0), (0, 0))
    q = jnp.pad(q, pw)
    k = jnp.pad(k, pw)
    v = jnp.pad(v, pw)
    log_f = jnp.pad(log_f, ((0, 0), (pad, 0), (0, 0)))
    Tp = T + pad
    nb = Tp // BLOCK_Q
    cum = jnp.cumsum(log_f, axis=1)
    cum_k = cum.transpose(0, 2, 1)
    k_pos = jnp.arange(Tp)
    k_valid = k_pos >= pad
    qb = q.reshape(Bsz, nb, BLOCK_Q, H, Dh).transpose(1, 0, 3, 2, 4)
    cq = cum.reshape(Bsz, nb, BLOCK_Q, H).transpose(1, 0, 3, 2)
    scale = Dh ** -0.5

    def block(args):
        i, qi, ci = args
        s = jnp.einsum('bhqd,bkhd->bhqk', qi, k).astype(jnp.float32) * scale
        s = s + ci[..., None] - cum_k[:, :, None, :]
        q_pos = i * BLOCK_Q + jnp.arange(BLOCK_Q)
        allowed = (k_pos[None, :] <= q_pos[:, None]) & k_valid[None, :]
        s = jnp.where(allowed, s, MASK_VALUE)
        p = jax.nn.softmax(s, axis=-1)
        return jnp.einsum('bhqk,bkhd->bqhd', p.astype(v.dtype), v)

    out = lax.map(block, (jnp.arange(nb), qb, cq))
    out = out.transpose(1, 0, 2, 3, 4).reshape(Bsz, Tp, H, Dh)
    return out[:, pad:]

def short_conv_mixer(b_gate, c_gate, hc, conv_w):
    u = c_gate * hc
    ch = u.shape[-1]
    y = lax.conv_general_dilated(
        u, conv_w[:, None, :].astype(u.dtype), window_strides=(1,),
        padding=[(CONV_K - 1, 0)], dimension_numbers=('NWC', 'WIO', 'NWC'),
        feature_group_count=ch)
    return b_gate * y

def hierarchical_moe(u, w_rg, b_rg, w_re, b_re, w_gate, w_up, w_down):
    Bsz, T, D = u.shape
    N = Bsz * T
    xt = u.reshape(N, D)
    g_prob = jax.nn.softmax((xt @ w_rg).astype(jnp.float32) + b_rg.astype(jnp.float32), axis=-1)
    g_p, g_idx = lax.top_k(g_prob, 1)
    e_logits = ((xt @ w_re).astype(jnp.float32) + b_re.astype(jnp.float32)).reshape(
        N, N_EXPERT_GROUPS, EXPERTS_PER_GROUP)
    e_logits = jnp.take_along_axis(e_logits, g_idx[:, :, None], axis=1)[:, 0]
    e_prob = jax.nn.softmax(e_logits, axis=-1)
    e_p, e_idx = lax.top_k(e_prob, TOP_K)
    gates = g_p * e_p / jnp.sum(e_p, axis=-1, keepdims=True)
    expert_ids = g_idx * EXPERTS_PER_GROUP + e_idx

    A = N * TOP_K
    flat_e = expert_ids.reshape(A)
    flat_tok = jnp.repeat(jnp.arange(N, dtype=jnp.int32), TOP_K)
    flat_w = gates.reshape(A)
    order = jnp.argsort(flat_e)
    se, stok, sw = flat_e[order], flat_tok[order], flat_w[order]
    counts = jnp.bincount(flat_e, length=N_EXPERTS)
    padded = (counts + EXPERT_BLOCK - 1) // EXPERT_BLOCK * EXPERT_BLOCK
    pad_end = jnp.cumsum(padded)
    pad_start = pad_end - padded
    start = jnp.cumsum(counts) - counts
    dest = pad_start[se] + jnp.arange(A) - start[se]
    n_blocks = -(-A // EXPERT_BLOCK) + N_EXPERTS
    R = n_blocks * EXPERT_BLOCK
    buf_tok = jnp.zeros((R,), jnp.int32).at[dest].set(stok)
    buf_w = jnp.zeros((R,), jnp.float32).at[dest].set(sw)
    block_e = jnp.minimum(
        jnp.searchsorted(pad_end, jnp.arange(n_blocks) * EXPERT_BLOCK, side='right'),
        N_EXPERTS - 1)
    xs = xt[buf_tok].reshape(n_blocks, EXPERT_BLOCK, D)

    def expert_block(args):
        xb, e = args
        hdn = jax.nn.silu(xb @ w_gate[e]) * (xb @ w_up[e])
        return hdn @ w_down[e]

    ys = lax.map(expert_block, (xs, block_e)).reshape(R, D)
    out = jax.ops.segment_sum(ys * buf_w[:, None].astype(ys.dtype), buf_tok, num_segments=N)
    return out.reshape(Bsz, T, D)

def hybrid_layer(h, g_mix, w_in, b_forget, q_norm_g, k_norm_g, conv_w, attn_out_g,
                 conv_out_g, w_out, g_ffn, w_rg, b_rg, w_re, b_re, w_gate, w_up, w_down):
    Bsz, T, _ = h.shape
    u = rms_norm(h, g_mix)
    proj = u @ w_in
    q, k, v, f_logit, b_gate, c_gate, hc = jnp.split(proj, SPLIT_POINTS, axis=-1)
    q = rms_norm(q.reshape(Bsz, T, ATTN_HEADS, HEAD_DIM), q_norm_g)
    k = rms_norm(k.reshape(Bsz, T, ATTN_HEADS, HEAD_DIM), k_norm_g)
    v = v.reshape(Bsz, T, ATTN_HEADS, HEAD_DIM)
    log_f = jax.nn.log_sigmoid(f_logit.astype(jnp.float32) + b_forget.astype(jnp.float32))
    attn = forgetting_attention(q, k, v, log_f)
    attn = rms_norm(attn, attn_out_g.reshape(ATTN_HEADS, HEAD_DIM)).reshape(Bsz, T, ATTN_WIDTH)
    conv = short_conv_mixer(b_gate, c_gate, hc, conv_w)
    conv = rms_norm(conv.reshape(Bsz, T, CONV_GROUPS, HEAD_DIM),
                    conv_out_g.reshape(CONV_GROUPS, HEAD_DIM)).reshape(Bsz, T, CONV_WIDTH)
    h = h + jnp.concatenate([attn, conv], axis=-1) @ w_out
    h = h + hierarchical_moe(rms_norm(h, g_ffn), w_rg, b_rg, w_re, b_re, w_gate, w_up, w_down)
    return h

def setup_inputs(seed: int = 0) -> dict:
    key = jax.random.key(seed)
    ks = jax.random.split(key, 20)

    def nrm(k, shape, scale):
        return jax.random.normal(k, shape, jnp.float32) * scale

    return {
        "x": nrm(ks[0], (BATCH, SEQ, D_MODEL), 1.0),
        "meta_tokens": nrm(ks[1], (N_META, D_MODEL), 1.0),
        "norm_mix_g": 1.0 + nrm(ks[2], (DEPTH, D_MODEL), 0.02),
        "w_in": nrm(ks[3], (DEPTH, D_MODEL, PROJ_COLS), D_MODEL ** -0.5),
        "b_forget": jax.random.uniform(ks[4], (DEPTH, ATTN_HEADS), jnp.float32, 1.0, 5.0),
        "q_norm_g": 1.0 + nrm(ks[5], (DEPTH, HEAD_DIM), 0.02),
        "k_norm_g": 1.0 + nrm(ks[6], (DEPTH, HEAD_DIM), 0.02),
        "conv_w": nrm(ks[7], (DEPTH, CONV_K, CONV_WIDTH), CONV_K ** -0.5),
        "attn_out_g": 1.0 + nrm(ks[8], (DEPTH, ATTN_WIDTH), 0.02),
        "conv_out_g": 1.0 + nrm(ks[9], (DEPTH, CONV_WIDTH), 0.02),
        "w_out": nrm(ks[10], (DEPTH, D_MODEL, D_MODEL), D_MODEL ** -0.5),
        "norm_ffn_g": 1.0 + nrm(ks[11], (DEPTH, D_MODEL), 0.02),
        "w_router_group": nrm(ks[12], (DEPTH, D_MODEL, N_EXPERT_GROUPS), D_MODEL ** -0.5),
        "b_router_group": nrm(ks[13], (DEPTH, N_EXPERT_GROUPS), 0.01),
        "w_router_expert": nrm(ks[14], (DEPTH, D_MODEL, N_EXPERTS), D_MODEL ** -0.5),
        "b_router_expert": nrm(ks[15], (DEPTH, N_EXPERTS), 0.01),
        "w_gate": nrm(ks[16], (DEPTH, N_EXPERTS, D_MODEL, D_EXPERT), D_MODEL ** -0.5),
        "w_up": nrm(ks[17], (DEPTH, N_EXPERTS, D_MODEL, D_EXPERT), D_MODEL ** -0.5),
        "w_down": nrm(ks[18], (DEPTH, N_EXPERTS, D_EXPERT, D_MODEL), D_EXPERT ** -0.5),
    }

def reference(x, meta_tokens, norm_mix_g, w_in, b_forget, q_norm_g, k_norm_g, conv_w,
              attn_out_g, conv_out_g, w_out, norm_ffn_g, w_router_group, b_router_group,
              w_router_expert, b_router_expert, w_gate, w_up, w_down):
    Bsz = x.shape[0]
    meta = jnp.broadcast_to(meta_tokens[None].astype(x.dtype), (Bsz, N_META, D_MODEL))
    h = jnp.concatenate([meta, x], axis=1)
    for layer in range(DEPTH):
        h = hybrid_layer(
            h, norm_mix_g[layer], w_in[layer], b_forget[layer], q_norm_g[layer],
            k_norm_g[layer], conv_w[layer], attn_out_g[layer], conv_out_g[layer],
            w_out[layer], norm_ffn_g[layer], w_router_group[layer], b_router_group[layer],
            w_router_expert[layer], b_router_expert[layer], w_gate[layer], w_up[layer],
            w_down[layer])
    return h[:, N_META:]


_drawn_inputs = setup_inputs


def setup_inputs(seed=0):
    import zlib

    import numpy as np

    out = dict(_drawn_inputs(seed))
    spreads = {}
    factors = {'q_norm_g': 3.452,
     'k_norm_g': 3.147,
     'attn_out_g': 3.227,
     'conv_out_g': 3.105,
     'norm_ffn_g': 2.898,
     'b_router_group': 6.689,
     'b_router_expert': 5.342}
    for name, (base, spread) in spreads.items():
        noise = np.random.default_rng([zlib.crc32(name.encode()), seed]).standard_normal(out[name].shape)
        drawn = base * np.exp(spread * noise) if base else spread * noise
        out[name] = __import__('jax').numpy.asarray(drawn.astype(out[name].dtype))
    for name, factor in factors.items():
        out[name] = (out[name] * factor).astype(out[name].dtype)
    return out
```

```python
import concourse.bass as bass
from concourse import mybir
from contextlib import ExitStack

F32 = mybir.dt.float32
BF16 = mybir.dt.bfloat16
I32 = mybir.dt.int32
U32 = mybir.dt.uint32
ALU = mybir.AluOpType
ACT = mybir.ActivationFunctionType
AX = mybir.AxisListType

P = 128
D = 1024
KT = D // P
T = 1024
NT = T // P
META = 16
KEYS = T + META
H = 8
HD = 64
AW = H * HD
CW = D - AW
CT = CW // P
AUG = HD + 2
NG = 4
NE = 32
EG = NE // NG
F = 512
FT = F // P
EPS = 1e-6
NEG = -1e30
MAX_OVER = 2 * T // P - 1
COLS = NE + MAX_OVER + 3
NOWHERE = 1 << 20

COL_V, COL_F = 2 * AW, 3 * AW
COL_B = 3 * AW + H
COL_C, COL_H = COL_B + CW, COL_B + 2 * CW

BASE = 16512


class Plan:

    def __init__(self, nc, at, end):
        self.nc, self.at, self.end = nc, at, end

    def __call__(self, name, shape, dt=F32):
        n = 1
        for s in shape[1:]:
            n *= s
        size = n * (2 if dt == BF16 else 4)
        t = self.nc.alloc_sbuf_tensor_at(name, list(shape), dt, offset=self.at)
        self.at += -(-size // 32) * 32
        assert self.at <= self.end, (name, self.at, self.end)
        return t


EXTRA = {3: "M", 4: "W", 6: "U", 7: "L"}


def ring_jobs():
    jobs = [("T", NT)] + [("T", t) for t in range(NT)]
    for c in range(CT):
        jobs += [("C", c), ("H", c), ("B", c)]
        if c:
            jobs.append(("R", c - 1))
    jobs += [("V", NT), ("V", 0), ("R", CT - 1)] + [("V", t) for t in range(1, NT)]
    jobs.append(("CUM", 0))
    toks = [NT] + list(range(NT))
    jobs += [("K", NT), ("K", 0)]
    for n in range(1, len(toks)):
        jobs.append(("KT", toks[n - 1]))
        jobs.append(("K", toks[n + 1]) if n + 1 < len(toks) else ("Q", 0))
    jobs += [("KT", NT - 1), ("Q", 1)]
    for t in range(NT):
        jobs.append(("QT", t))
        if t + 2 < NT:
            jobs.append(("Q", t + 2))
    for i in range(NT):
        for h in range(H):
            jobs.append(("S", i, h))
            if i and h in EXTRA:
                jobs.append((EXTRA[h], i - 1))
    jobs += [(k, NT - 1) for k in ("M", "W", "U", "L")]
    jobs += [("RANK", 0), ("TABLE", 0)]
    return jobs


JOBS = ring_jobs()
TURN = {job: n for n, job in enumerate(JOBS)}


def side(job):
    return TURN[job] % 2


def uses(job):
    return TURN[job] // 2 + 1


def groups(i):
    blocks = list(range(i + 2))
    return [blocks[j:j + 2] for j in range(0, i + 2, 2)]


GROUPS = {}
for _i in range(NT):
    for _h in range(H):
        for _g in range(len(groups(_i))):
            GROUPS[(_i, _h, _g)] = len(GROUPS)


def build(nc, x, meta, g_mix, w_in, b_forget, gq, gk, conv_w, g_attn, g_conv, w_out, g_ffn,
          w_rg, b_rg, w_re, b_re, w_gate, w_up, w_down, out):
    ctx = ExitStack()
    with ctx:
        def sem(name):
            return ctx.enter_context(nc.semaphore(name))

        top = BASE + 212800
        small = Plan(nc, BASE, BASE + 20000)
        ident = small("ident", [P, P])
        identb = small("identb", [P, P], BF16)
        maskb = small("maskb", [P, P], BF16)
        tri = small("tri", [P, P])
        tris = small("tris", [P, P])
        ones = small("ones", [P, P])
        blockones = small("blockones", [P, P])
        iota128 = small("iota128", [P, P])
        wf = small("wf", [P, KT, H])
        wr = small("wr", [P, KT, NG + NE])
        gmixT = small("gmixT", [P, KT])
        gattnT = small("gattnT", [P, CT])
        gconvT = small("gconvT", [P, CT])
        convwT = small("convwT", [P, 3, CT])
        bf_b = small("bf_b", [P, H])
        gqk_b = small("gqk_b", [P, 2, HD])
        br_b = small("br_b", [P, NG + NE])
        stat = small("stat", [P, 2, H])
        ms = small("ms", [P, 4])
        negmax = small("negmax", [P, 2])
        rowsum = small("rowsum", [P, 2, H])
        logits = small("logits", [P, NT, NG + NE])
        tokcode = small("tokcode", [P, NT])
        gates = small("gates", [P, 2, NT])
        eps_b = small("eps_b", [P, 1])
        one_b = small("one_b", [P, 1])
        gtab = small("gtab", [P, COLS], I32)
        stab = small("stab", [P, COLS], I32)
        bexp = small("bexp", [P, COLS], I32)
        nblocks = small("nblocks", [P, 1], I32)
        idxg = small("idxg", [P, 2], I32)
        idxs = small("idxs", [P, 2], I32)

        A0 = small.at

        p = Plan(nc, A0, top)
        uT = p("uT", [P, KT, KEYS])
        ring_at = p.at
        win = p("win", [P, 3, KT, 512])
        conv = p("conv", [P, CT, T])
        v_at = p.at
        v = p("v", [P, NT + 1, AW])
        qT_at = p.at
        qT = p("qT", [P, H, T])
        kT = p("kT", [P, H, KEYS])
        kn_at = p.at
        c_ = Plan(nc, qT_at, kn_at)
        xin = c_("xin", [P, 2, D])
        hn = c_("hn", [P, 2, D])
        sqj = c_("sqj", [P, D])
        csb = c_("csb", [P, T + 2])
        uc = c_("uc", [P, T + 2])
        ysq = c_("ysq", [P, T])
        rsb = c_("rsb", [P, T])
        m_ = Plan(nc, kn_at, top)
        kn = m_("kn", [P, 2, H, AUG])
        qn = m_("qn", [P, 2, H, AUG])
        fz = m_("fz", [P, NT + 1, H])
        fe = m_("fe", [P, NT + 1, H])
        lf = m_("lf", [P, NT + 1, H])
        facc = m_("facc", [P, NT + 1, H])
        cum = m_("cum", [P, NT + 1, H])
        sq = m_("sq", [P, AW])
        a_ = Plan(nc, A0, ring_at)
        probs = a_("probs", [P, 2, T + P])
        pT = a_("pT", [P, 2, 2 * P])
        atok = a_("atok", [P, 2, AW])
        asq = a_("asq", [P, AW])
        aT = a_("aT", [P, CT, P])
        xr = a_("xr", [P, D])
        u2T = a_("u2T", [P, KT, P])
        r_ = Plan(nc, ring_at, v_at - 4 * CT * T)
        wo = r_("wo", [P, KT, D])
        h1b = r_("h1b", [P, D])
        u2 = r_("u2", [P, D])
        gffn_b = r_("gffn_b", [P, D])
        u2sq = r_("u2sq", [P, D])
        q_ = Plan(nc, A0, ring_at)
        one0 = q_("one0", [P, NT, NE])
        one1 = q_("one1", [P, NT, NE])
        both = q_("both", [P, NT, NE])
        prev = q_("prev", [P, NT + 1, NE])
        ranks = q_("ranks", [P, NT, NE])
        el = q_("el", [P, NT, NE])
        et = q_("et", [P, NT, NE])
        cmp7 = q_("cmp7", [P, NE, 8])
        t256 = q_("t256", [P, 16, 16])
        oc = Plan(nc, ring_at, v_at)
        rowhot = oc("rowhot", [P, 2 * NT, P])
        colhot = oc("colhot", [P, 2 * NT, COLS])
        over = oc("over", [P, 2, NE])
        nover = oc("nover", [P, NE])
        cnt = oc("cnt", [P, NE])
        bcmp = oc("bcmp", [P, MAX_OVER + 3, NE])
        r8 = [oc(f"r8_{n}", [P, 2, NT]) for n in range(10)]
        r4 = [oc(f"r4_{n}", [P, NT, NG]) for n in range(2)]
        tabf = [oc(f"tabf_{n}", [P, COLS]) for n in range(3)]
        iotag = oc("iotag", [P, NG])
        w_ = Plan(nc, v_at, top)
        wg = w_("wg", [P, 2, KT, F])
        wu = w_("wu", [P, 2, KT, F])
        wd = w_("wd", [P, 2, FT, D])
        e_ = Plan(nc, oc.at, v_at)
        xg = e_("xg", [P, 2, D])
        yb = e_("yb", [P, 2, D])
        f_ = Plan(nc, A0, ring_at)
        xT = f_("xT", [P, KT, P])
        sil = f_("sil", [P, F])
        hid = f_("hid", [P, F])
        hidT = f_("hidT", [P, FT, P])
        g_ = Plan(nc, f_.at, ring_at)
        h1t = g_("h1t", [P, 2, D])
        l_ = Plan(nc, v_at, top)
        y0 = l_("y0", [P, 2, D])
        y1 = l_("y1", [P, 2, D])

        ps = ctx.enter_context(nc.psum_tensor("ps", [P, 8, 512], F32))
        OB = 7

        def pt_bank(n, no):
            return 6 if no % 2 == 0 or n >= H * (NT - 1) - 1 else 2
        big = ps[:, :, :].rearrange("p b n -> p (b n)")

        def buf(job, width, rows=P):
            at = 3 * 512 * side(job)
            return big[0:rows, at:at + width]

        dram_u2 = nc.dram_tensor("u2_rows", [T, D], F32).ap()
        dram_h1 = nc.dram_tensor("h1_rows", [T, D], F32).ap()
        ys = nc.dram_tensor("expert_rows", [2 * T, D], F32).ap()

        made = [sem("ring_made_0"), sem("ring_made_1")]
        used = [sem("ring_used_0"), sem("ring_used_1")]
        consts = sem("consts")
        gmix_in = sem("gmix_in")
        params = sem("params")
        x_in = [sem("x_in_0"), sem("x_in_1")]
        win_in = [sem(f"win_in_{s}") for s in range(3)]
        rs_ready = sem("rs_ready")
        hn_ready = sem("hn_ready")
        act_step = sem("act_step")
        dve_step = sem("dve_step")
        pool_step = sem("pool_step")
        ysq_ready = sem("ysq_ready")
        rsb_ready = sem("rsb_ready")
        conv_done = sem("conv_done")
        f_ready = sem("f_ready")
        fe_ready = sem("fe_ready")
        lf_ready = sem("lf_ready")
        sq_ready = sem("sq_ready")
        ss_ready = sem("ss_ready")
        rk_ready = sem("rk_ready")
        kn_ready = sem("kn_ready")
        max_ready = sem("max_ready")
        pt_made = sem("pt_made")
        pt_out = [sem("pt_out_even"), sem("pt_out_odd")]
        pv_done = sem("pv_done")
        o_taken = sem("o_taken")
        asq_ready = sem("asq_ready")
        ass_ready = sem("ass_ready")
        ars_ready = sem("ars_ready")
        atok_ready = sem("atok_ready")
        wo_in = sem("wo_in")
        xr_in = sem("xr_in")
        u2rs_ready = sem("u2rs_ready")
        u2_ready = sem("u2_ready")
        rows_out = sem("u2_rows_out")
        h1_out = sem("h1_rows_out")
        gexp_ready = sem("gexp_ready")
        route_ready = sem("route_ready")
        gate_ask = sem("gate_ask")
        gate_exp = sem("gate_exp")
        wg_in = [sem("wg_in_0"), sem("wg_in_1")]
        wu_in = [sem("wu_in_0"), sem("wu_in_1")]
        wd_in = [sem("wd_in_0"), sem("wd_in_1")]
        g_done = sem("g_done")
        u_done = sem("u_done")
        y_done = [sem("y_done_0"), sem("y_done_1")]
        xg_in = [sem("xg_in_0"), sem("xg_in_1")]
        x_turned = sem("x_turned")
        xT_dve = sem("xT_dve")
        xT_act = sem("xT_act")
        sil_ready = sem("sil_ready")
        hid_ready = sem("hid_ready")
        hid_turned = sem("hid_turned")
        hidT_ready = sem("hidT_ready")
        yb_dve = sem("yb_dve")
        yb_act = sem("yb_act")
        ys_out = [sem("ys_out_0"), sem("ys_out_1")]
        idx_ready = sem("idx_ready")
        pool_pass = sem("pool_pass")
        yb_free = sem("yb_free")
        all_out = sem("all_expert_rows_out")
        y_in = [sem("y_in_0"), sem("y_in_1")]
        fin_ready = sem("fin_ready")
        fin_out = [sem("fin_out_0"), sem("fin_out_1")]

        def wait_made(eng, job):
            eng.wait_ge(made[side(job)], uses(job))

        def wait_used(eng, job):
            eng.wait_ge(used[side(job)], uses(job))

        toks = [NT] + list(range(NT))

        def rows(t):
            return META if t == NT else P

        def u_cols(t):
            return (0, META) if t == NT else (META + P * t, META + P * (t + 1))

        def k_cols(t):
            return P * t, P * t + rows(t)

        heads = [(i, h) for i in range(NT) for h in range(H)]
        qk = [("K", t) for t in toks] + [("Q", t) for t in range(NT)]
        NPAR = 13

        def width(i):
            return P * (i + 1) + META

        def group_no(n, g):
            return GROUPS[(*heads[n], g)]

        block = ctx.enter_context(nc.Block())

        @block.sync
        def _(sp):
            w_in_k = w_in.rearrange("(k p) c -> p k c", p=P)

            def load_x(n):
                t = toks[n]
                if n >= 2:
                    sp.wait_ge(hn_ready, n - 1)
                src = meta[:, :] if t == NT else x[P * t:P * (t + 1), :]
                sp.dma_start(xin[0:rows(t), n % 2, :], src).then_inc(x_in[n % 2], 16)

            def load_chunk(u):
                s = u % 3
                if u >= 3:
                    wait_made(sp, ("B", u - 3))
                if u < CT:
                    for n, col in enumerate((COL_B, COL_C, COL_H)):
                        sp.dma_start(win[:, s, :, P * n:P * (n + 1)],
                                     w_in_k[:, :, col + P * u:col + P * (u + 1)]).then_inc(win_in[s], 16)
                else:
                    col = (COL_V, AW, 0)[u - CT]
                    sp.dma_start(win[:, s, :, :], w_in_k[:, :, col:col + 512]).then_inc(win_in[s], 16)

            load_x(0)
            load_x(1)
            sp.dma_start(gmixT[:, :], g_mix.rearrange("(k p) -> p k", p=P),
                         allow_slow_non_contiguous=True).then_inc(gmix_in, 16)
            load_x(2)
            load_chunk(0)
            for n in range(3, NT + 1):
                load_x(n)
            load_chunk(1)
            load_chunk(2)
            for u in range(3, CT + 3):
                load_chunk(u)
            wait_made(sp, ("Q", NT - 1))
            sp.dma_start(wo[:, :, :], w_out.rearrange("(k p) c -> p k c", p=P)).then_inc(wo_in, 16)
            sp.dma_start(gffn_b[:, :], g_ffn.partition_broadcast(P)).then_inc(wo_in, 16)
            for i in range(NT):
                if i:
                    wait_used(sp, ("W", i - 1))
                sp.dma_start(xr[:, :], x[P * i:P * (i + 1), :]).then_inc(xr_in, 16)
            sp.wait_ge(pv_done, len(GROUPS))

            def load_expert(e, s):
                sp.dma_start(wg[:, s, :, :], w_gate[e].rearrange("(k p) f -> p k f", p=P)).then_inc(wg_in[s], 16)
                sp.dma_start(wu[:, s, :, :], w_up[e].rearrange("(k p) f -> p k f", p=P)).then_inc(wu_in[s], 16)
                sp.dma_start(wd[:, s, :, :], w_down[e].rearrange("(k p) f -> p k f", p=P)).then_inc(wd_in[s], 16)

            for s in range(2):
                load_expert(s, s)
            sp.wait_ge(route_ready, 1)
            nb = sp.value_load(nblocks[0:1, 0:1], min_val=NE, max_val=NE + MAX_OVER)
            with sp.Fori(2, nb, 2) as i:
                for s in range(2):
                    e = sp.value_load(bexp[0:1, bass.ds(i + s, 1)], min_val=0, max_val=NE - 1)
                    sp.wait_ge(g_done, i + s - 1)
                    sp.dma_start(wg[:, s, :, :], w_gate[bass.ds(e, 1)].rearrange("o (k p) f -> p (o k) f", p=P)
                                 ).then_inc(wg_in[s], 16)
                    sp.wait_ge(u_done, i + s - 1)
                    sp.dma_start(wu[:, s, :, :], w_up[bass.ds(e, 1)].rearrange("o (k p) f -> p (o k) f", p=P)
                                 ).then_inc(wu_in[s], 16)
                    sp.wait_ge(y_done[s], i // 2)
                    sp.dma_start(wd[:, s, :, :], w_down[bass.ds(e, 1)].rearrange("o (k p) f -> p (o k) f", p=P)
                                 ).then_inc(wd_in[s], 16)
            sp.wait_ge(all_out, 1)
            for t in range(NT):
                s = t % 2
                if t >= 2:
                    sp.wait_ge(fin_out[s], 16 * (t // 2))
                for dst, src in ((h1t, dram_h1[P * t:P * (t + 1), :]), (y0, ys[P * t:P * (t + 1), :]),
                                 (y1, ys[T + P * t:T + P * (t + 1), :])):
                    sp.dma_start(dst[:, s, :], src).then_inc(y_in[s], 16)

        @block.gpsimd
        def _(pool):
            count = [0]

            def then(ins):
                count[0] += 1
                ins.then_inc(pool_step, 1)
                pool.wait_ge(pool_step, count[0])

            for tile_, value in ((ident, 0.0), (identb, 0.0), (maskb, 0.0), (tri, 1.0), (tris, 1.0),
                                 (ones, 1.0), (eps_b, EPS), (one_b, 1.0), (blockones, 0.0), (lf, 0.0), (fz, 0.0), (kn, 1.0), (qn, 1.0)):
                then(nc.gpsimd.memset(tile_[:], value))
            for tile_, op, fill in ((ident, ALU.not_equal, 1.0), (identb, ALU.not_equal, 1.0)):
                then(nc.gpsimd.affine_select(out=tile_[:], in_=tile_[:], compare_op=op, fill=fill, base=0,
                                             pattern=[[-1, P]], channel_multiplier=1))
            then(nc.gpsimd.affine_select(out=maskb[:], in_=maskb[:], compare_op=ALU.is_ge, fill=NEG, base=0,
                                         pattern=[[-1, P]], channel_multiplier=1))
            then(nc.gpsimd.affine_select(out=tri[:], in_=tri[:], compare_op=ALU.is_ge, fill=0.0, base=0,
                                         pattern=[[1, P]], channel_multiplier=-1))
            then(nc.gpsimd.affine_select(out=tris[:], in_=tris[:], compare_op=ALU.is_gt, fill=0.0, base=0,
                                         pattern=[[1, P]], channel_multiplier=-1))
            for n in range(2):
                then(nc.gpsimd.memset(blockones[HD * n:HD * (n + 1), HD * n:HD * (n + 1)], 1.0 / HD))
            then(nc.gpsimd.iota(iota128[:], pattern=[[1, P]], base=0, channel_multiplier=0,
                                allow_small_or_imprecise_dtypes=True))
            nc.gpsimd.iota(tokcode[:], pattern=[[P, NT]], base=1, channel_multiplier=1,
                           allow_small_or_imprecise_dtypes=True).then_inc(consts, 1)
            slow = dict(allow_slow_non_contiguous=True)
            pool.dma_start(wf[:, :, :], w_in.rearrange("(k p) c -> p k c", p=P)[:, :, COL_F:COL_F + H],
                           **slow).then_inc(params, 16)
            pool.dma_start(wr[:, :, 0:NG], w_rg.rearrange("(k p) c -> p k c", p=P), **slow).then_inc(params, 16)
            pool.dma_start(wr[:, :, NG:], w_re.rearrange("(k p) c -> p k c", p=P), **slow).then_inc(params, 16)
            pool.dma_start(gattnT[:, :], g_attn.rearrange("(k p) -> p k", p=P), **slow).then_inc(params, 16)
            pool.dma_start(gconvT[:, :], g_conv.rearrange("(k p) -> p k", p=P), **slow).then_inc(params, 16)
            for n in range(3):
                pool.dma_start(convwT[:, n, :], conv_w[n].rearrange("(k p) -> p k", p=P),
                               **slow).then_inc(params, 16)
            pool.dma_start(bf_b[:, :], b_forget.partition_broadcast(P)).then_inc(params, 16)
            pool.dma_start(gqk_b[:, 0, :], gq.partition_broadcast(P)).then_inc(params, 16)
            pool.dma_start(gqk_b[:, 1, :], gk.partition_broadcast(P)).then_inc(params, 16)
            pool.dma_start(br_b[:, 0:NG], b_rg.partition_broadcast(P)).then_inc(params, 16)
            pool.dma_start(br_b[:, NG:], b_re.partition_broadcast(P)).then_inc(params, 16)
            wait_made(pool, ("Q", NT - 1))
            nc.gpsimd.memset(probs[:], 0.0).then_inc(consts, 1)
            for i in range(NT):
                wait_used(pool, ("W", i))
                pool.dma_start(dram_h1[P * i:P * (i + 1), :], h1b[:, :]).then_inc(h1_out, 16)
                pool.wait_ge(u2_ready, i + 1)
                pool.dma_start(dram_u2[P * i:P * (i + 1), :], u2[:, :]).then_inc(rows_out, 16)
            pool.wait_ge(rows_out, 16 * NT)
            pool.wait_ge(route_ready, 1)
            nc.gpsimd.memset(xg[:], 0.0).then_inc(pool_step, 1)
            count[0] += 1
            pool.wait_ge(pool_step, count[0])
            last_token, last_row = pool.to_reg(T - 1), pool.to_reg(2 * T - 1)
            for s in range(2):
                nc.gpsimd.tensor_copy(idxg[:, s:s + 1], gtab[:, s:s + 1]).then_inc(idx_ready, 1)
                pool.wait_ge(idx_ready, s + 1)
                nc.gpsimd.indirect_dma_start(
                    out=xg[:, s, :], out_offset=None, in_=dram_u2[:, :],
                    in_offset=bass.IndirectOffsetOnAxis(ap=idxg[:, s:s + 1].bitcast(U32), axis=0),
                    bounds_check=last_token, oob_is_err=False).then_inc(xg_in[s], 16)
                pool.sem_inc(yb_free, 1)
            nb = pool.value_load(nblocks[0:1, 0:1], min_val=NE, max_val=NE + MAX_OVER)
            with pool.Fori(0, nb, 2) as i:
                for s in range(2):
                    nc.gpsimd.tensor_copy(idxs[:, s:s + 1], stab[:, bass.ds(i + s, 1)]).then_inc(idx_ready, 1)
                    pool.wait_ge(idx_ready, 2 * (i + s) + 3)
                    pool.wait_ge(yb_dve, i + s + 2)
                    pool.wait_ge(yb_act, i + s + 2)
                    pool.sem_inc(pool_pass, 1)
                    nc.gpsimd.indirect_dma_start(
                        out=ys[:, :], in_=yb[:, s, :], in_offset=None,
                        out_offset=bass.IndirectOffsetOnAxis(ap=idxs[:, s:s + 1].bitcast(U32), axis=0),
                        bounds_check=last_row, oob_is_err=False).then_inc(ys_out[s], 16)
                    pool.wait_ge(x_turned, i + s + 1)
                    nc.gpsimd.tensor_copy(idxg[:, s:s + 1], gtab[:, bass.ds(i + s + 2, 1)]).then_inc(idx_ready, 1)
                    pool.wait_ge(idx_ready, 2 * (i + s) + 4)
                    pool.sem_inc(pool_pass, 1)
                    nc.gpsimd.indirect_dma_start(
                        out=xg[:, s, :], out_offset=None, in_=dram_u2[:, :],
                        in_offset=bass.IndirectOffsetOnAxis(ap=idxg[:, s:s + 1].bitcast(U32), axis=0),
                        bounds_check=last_token, oob_is_err=False).then_inc(xg_in[s], 16)
                    pool.wait_ge(ys_out[s], 16 * (i // 2 + 1))
                    pool.sem_inc(yb_free, 1)
            pairs = (nb + 1) // 2
            for s in range(2):
                pool.wait_ge(ys_out[s], 16 * pairs)
                pool.wait_ge(xg_in[s], 16 * pairs + 16)
            pool.wait_ge(h1_out, 16 * NT)
            pool.sem_inc(all_out, 1)

        @block.tensor
        def _(pe):
            mm = nc.tensor.matmul

            def start(job):
                if uses(job) > 1:
                    pe.wait_ge(used[side(job)], uses(job) - 1)

            def done(job, last):
                last.then_inc(made[side(job)], 1)

            def turn_x(t, n):
                job = ("T", t)
                start(job)
                pe.wait_ge(hn_ready, n + 1)
                r = rows(t)
                for k in range(KT):
                    last = nc.tensor.transpose(buf(job, KT * P)[:, P * k:P * k + r],
                                               hn[0:r, n % 2, P * k:P * (k + 1)], ident[0:r, 0:r])
                done(job, last)

            def wait_chunk(u):
                per = [3 if n < CT else 1 for n in range(CT + 3)]
                pe.wait_ge(win_in[u % 3], 16 * sum(per[n] for n in range(u + 1) if n % 3 == u % 3))

            def channels(kind, c):
                job = (kind, c)
                start(job)
                sect = {"B": 0, "C": 1, "H": 2}[kind]
                n_chunk, size, at = (2, 512, META) if kind == "B" else (3, (T + 2) // 3, META - 2)
                for j in range(n_chunk):
                    for k in range(KT):
                        last = mm(ps[:, 3 * side(job) + j, 0:size], win[:, c % 3, k, P * sect:P * (sect + 1)],
                                  uT[:, k, at + size * j:at + size * (j + 1)], start=(k == 0), stop=(k == KT - 1))
                done(job, last)

            def conv_mean(c):
                job = ("R", c)
                start(job)
                pe.wait_ge(ysq_ready, c + 1)
                for j in range(2):
                    last = mm(ps[:, 3 * side(job) + j, :], blockones[:, :], ysq[:, 512 * j:512 * (j + 1)],
                              start=True, stop=True)
                done(job, last)

            def tokens(job, slot, forget=False):
                t = job[1]
                a, b = u_cols(t)
                start(job)
                for k in range(KT):
                    last = mm(ps[0:rows(t), 3 * side(job), :], uT[:, k, a:b], win[:, slot, k, :],
                              start=(k == 0), stop=(k == KT - 1))
                if forget:
                    for k in range(KT):
                        last = mm(ps[0:rows(t), 3 * side(job) + 1, 0:H], uT[:, k, a:b], wf[:, k, :],
                                  start=(k == 0), stop=(k == KT - 1))
                done(job, last)

            def turn_heads(job, n):
                kind, t = job
                start(job)
                pe.wait_ge(kn_ready, n + 1)
                src, at = (kn, toks.index(t)) if kind == "KT" else (qn, t)
                r = rows(t)
                for h in range(H):
                    last = nc.tensor.transpose(buf(job, H * P)[0:AUG, P * h:P * h + r], src[0:r, at % 2, h, :],
                                               ident[0:r, 0:r])
                done(job, last)

            def scores(n):
                i, h = heads[n]
                job = ("S", i, h)
                start(job)
                q = qT[0:AUG, h, P * i:P * (i + 1)]
                b0 = 3 * side(job)
                real = P * (i + 1)
                for c0 in range(0, real, 512):
                    c1 = min(real, c0 + 512)
                    diag = c1 == real
                    mm(ps[:, b0 + c0 // 512, 0:c1 - c0], q, kT[0:AUG, h, c0:c1], start=True, stop=not diag)
                    if diag:
                        mm(ps[:, b0 + c0 // 512, P * i - c0:P * (i + 1) - c0], identb[:, :], maskb[:, :],
                           start=False, stop=True)
                last = mm(big[:, 512 * b0 + real:512 * b0 + real + META], q, kT[0:AUG, h, T:KEYS],
                          start=True, stop=True)
                done(job, last)

            def attend(n):
                i, h = heads[n]
                gs = groups(i)
                wait_used(pe, ("S", i, h))

                def turn(g):
                    no = group_no(n, g)
                    if no >= 2:
                        pe.wait_ge(pt_out[no % 2], no // 2)
                    if n >= H * (NT - 1) - 1:
                        pe.wait_ge(pt_out[(no - 1) % 2], (no - 1) // 2 + 1)
                    for m, j in enumerate(gs[g]):
                        last = nc.tensor.transpose(ps[:, pt_bank(n, no), P * m:P * (m + 1)],
                                                   probs[:, n % 2, P * j:P * (j + 1)], ident[:, :])
                    last.then_inc(pt_made, 1)

                def times_v(g):
                    no = group_no(n, g)
                    pe.wait_ge(pt_out[no % 2], no // 2 + 1)
                    if g == 0 and h == 0 and i:
                        pe.wait_ge(o_taken, i)
                    for m, j in enumerate(gs[g]):
                        r = META if j == i + 1 else P
                        t = NT if j == i + 1 else j
                        last = mm(ps[:, OB, HD * h:HD * (h + 1)], pT[0:r, no % 2, P * m:P * (m + 1)],
                                  v[0:r, t, HD * h:HD * (h + 1)], start=(j == 0), stop=(j == i + 1))
                    last.then_inc(pv_done, 1)

                turn(0)
                for g in range(1, len(gs)):
                    turn(g)
                    times_v(g - 1)
                times_v(len(gs) - 1)

            def extra(kind, i):
                job = (kind, i)
                start(job)
                b0 = 3 * side(job)
                if kind == "M":
                    pe.wait_ge(atok_ready, i + 1)
                    for k in range(CT):
                        last = nc.tensor.transpose(ps[:, b0, P * k:P * (k + 1)],
                                                   atok[:, i % 2, P * k:P * (k + 1)], ident[:, :])
                elif kind == "W":
                    wait_used(pe, ("M", i))
                    if i == 0:
                        pe.wait_ge(wo_in, 32)
                        pe.wait_ge(conv_done, CT)
                    for j in range(2):
                        for k in range(KT):
                            lhs = aT[:, k, :] if k < CT else conv[:, k - CT, P * i:P * (i + 1)]
                            last = mm(ps[:, b0 + j, :], lhs, wo[:, k, 512 * j:512 * (j + 1)],
                                      start=(k == 0), stop=(k == KT - 1))
                elif kind == "U":
                    pe.wait_ge(u2_ready, i + 1)
                    for k in range(KT):
                        last = nc.tensor.transpose(buf(job, D)[:, P * k:P * (k + 1)], u2[:, P * k:P * (k + 1)],
                                                   ident[:, :])
                else:
                    wait_used(pe, ("U", i))
                    for k in range(KT):
                        last = mm(ps[:, b0, 0:NG + NE], u2T[:, k, :], wr[:, k, :], start=(k == 0), stop=(k == KT - 1))
                done(job, last)

            pe.wait_ge(consts, 1)
            pe.wait_ge(params, 16 * NPAR)
            for n, t in enumerate(toks):
                turn_x(t, n)
            for t in toks[-2:]:
                wait_used(pe, ("T", t))
            for c in range(CT):
                wait_chunk(c)
                channels("C", c)
                channels("H", c)
                channels("B", c)
                if c:
                    conv_mean(c - 1)
            wait_chunk(CT)
            for n, t in enumerate(toks):
                tokens(("V", t), CT % 3, forget=True)
                if n == 1:
                    conv_mean(CT - 1)
            job = ("CUM", 0)
            start(job)
            pe.wait_ge(lf_ready, 1)
            mm(ps[:, 3 * side(job), 0:(NT + 1) * H], tri[:, :], lf[:, :, :].rearrange("p t h -> p (t h)"),
               start=True, stop=False)
            done(job, mm(ps[:, 3 * side(job), 0:(NT + 1) * H], ones[:, :],
                         facc[:, :, :].rearrange("p t h -> p (t h)"), start=False, stop=True))
            n_turned = 0
            for job in JOBS:
                if job[0] in ("K", "Q"):
                    if job == ("K", NT):
                        wait_chunk(CT + 1)
                    if job == ("Q", 0):
                        wait_chunk(CT + 2)
                    tokens(job, (CT + 1 if job[0] == "K" else CT + 2) % 3)
                elif job[0] in ("KT", "QT"):
                    turn_heads(job, n_turned)
                    n_turned += 1
            wait_used(pe, ("KT", NT - 1))
            wait_used(pe, ("QT", NT - 1))
            wait_used(pe, ("QT", NT - 2))
            pe.wait_ge(consts, 2)
            for n, (i, h) in enumerate(heads):
                scores(n)
                if n:
                    attend(n - 1)
                if i and h in EXTRA:
                    extra(EXTRA[h], i - 1)
            attend(len(heads) - 1)
            for kind in ("M", "W", "U", "L"):
                extra(kind, NT - 1)
            job = ("RANK", 0)
            start(job)
            pe.wait_ge(gate_ask, 2)
            b0 = 3 * side(job)
            mm(ps[:, b0, 0:NT * NE], tris[:, :], both[:, :, :].rearrange("p t e -> p (t e)"), start=True, stop=False)
            mm(ps[:, b0, 0:NT * NE], ones[:, :], prev[:, 0:NT, :].rearrange("p t e -> p (t e)"),
               start=False, stop=True)
            done(job, mm(ps[:, b0, NT * NE:(NT + 1) * NE], ones[:, :], prev[:, NT, :], start=True, stop=True))
            job = ("TABLE", 0)
            start(job)
            pe.wait_ge(gate_ask, 3)
            for m in range(2 * NT):
                last = mm(ps[:, 3 * side(job), 0:COLS], rowhot[:, m, :], colhot[:, m, :],
                          start=(m == 0), stop=(m == 2 * NT - 1))
            done(job, last)
            pe.wait_ge(route_ready, 1)
            nb = pe.value_load(nblocks[0:1, 0:1], min_val=NE, max_val=NE + MAX_OVER)
            with pe.Fori(0, nb, 2) as i:
                for s in range(2):
                    pair = i // 2 + 1
                    pe.wait_ge(xg_in[s], 16 * pair)
                    for k in range(KT):
                        last = nc.tensor.transpose(big[:, P * k:P * (k + 1)], xg[:, s, P * k:P * (k + 1)], ident[:, :])
                    last.then_inc(x_turned, 1)
                    pe.wait_ge(wg_in[s], 16 * pair)
                    pe.wait_ge(xT_dve, i + s + 1)
                    pe.wait_ge(xT_act, i + s + 1)
                    for k in range(KT):
                        last = mm(ps[:, 2, :], xT[:, k, :], wg[:, s, k, :], start=(k == 0), stop=(k == KT - 1))
                    last.then_inc(g_done, 1)
                    pe.wait_ge(wu_in[s], 16 * pair)
                    for k in range(KT):
                        last = mm(ps[:, 3, :], xT[:, k, :], wu[:, s, k, :], start=(k == 0), stop=(k == KT - 1))
                    last.then_inc(u_done, 1)
                    pe.wait_ge(hid_ready, i + s + 1)
                    for k in range(FT):
                        last = nc.tensor.transpose(ps[:, 4, P * k:P * (k + 1)], hid[:, P * k:P * (k + 1)], ident[:, :])
                    last.then_inc(hid_turned, 1)
                    pe.wait_ge(wd_in[s], 16 * pair)
                    pe.wait_ge(hidT_ready, i + s + 1)
                    pe.wait_ge(yb_dve, i + s + 1)
                    pe.wait_ge(yb_act, i + s + 1)
                    for j in range(2):
                        for k in range(FT):
                            last = mm(ps[:, 5 + j, :], hidT[:, k, :], wd[:, s, k, 512 * j:512 * (j + 1)],
                                      start=(k == 0), stop=(k == FT - 1))
                    last.then_inc(y_done[s], 1)

        @block.scalar
        def _(act):
            count = [0]
            A = nc.scalar.activation

            def then(ins):
                count[0] += 1
                ins.then_inc(act_step, 1)
                act.wait_ge(act_step, count[0])

            def inv_root(dst, src, scale):
                then(A(dst, src, ACT.Ln, bias=eps_b[0:dst.shape[0], :], scale=scale))
                return A(dst, dst, ACT.Exp, scale=-0.5)

            act.wait_ge(consts, 1)
            for n, t in enumerate(toks):
                r = rows(t)
                act.wait_ge(x_in[n % 2], 16 * (n // 2 + 1))
                if n >= 2:
                    act.wait_ge(hn_ready, n - 1)
                then(A(sqj[0:r, :], xin[0:r, n % 2, :], ACT.Square, accum_out=ms[0:r, n % 2:n % 2 + 1]))
                inv_root(ms[0:r, n % 2:n % 2 + 1], ms[0:r, n % 2:n % 2 + 1], 1.0 / D).then_inc(rs_ready, 1)

            def conv_root(c):
                wait_made(act, ("R", c))
                if c:
                    act.wait_ge(conv_done, c)
                count[0] += 1
                A(rsb[:, :], buf(("R", c), T), ACT.Ln, bias=eps_b[:, :]).then_inc(used[side(("R", c))], 1)
                wait_used(act, ("R", c))
                count[0] -= 1
                A(rsb[:, :], rsb[:, :], ACT.Exp, scale=-0.5).then_inc(rsb_ready, 1)

            for c in range(CT):
                job = ("C", c)
                wait_made(act, job)
                if c:
                    wait_used(act, ("H", c - 1))
                b0 = 3 * side(job)
                A(csb[:, :].rearrange("p (j n) -> p j n", j=3), ps[:, b0:b0 + 3, 0:(T + 2) // 3],
                  ACT.Copy).then_inc(used[side(job)], 1)
                wait_used(act, ("B", c))
                if c:
                    wait_made(act, ("R", c - 1))
                    conv_root(c - 1)
                A(ysq[:, :], conv[:, c, :], ACT.Square).then_inc(ysq_ready, 1)
            for n, t in enumerate(toks):
                job, r = ("V", t), rows(t)
                wait_made(act, job)
                b0 = 3 * side(job)
                A(v[0:r, t, :], ps[0:r, b0, :], ACT.Copy)
                A(fz[0:r, t, :], ps[0:r, b0 + 1, 0:H], ACT.Copy).then_inc(used[side(job)], 1)
                if n == 1:
                    conv_root(CT - 1)
            act.wait_ge(f_ready, 1)
            then(A(fe[:, :, :], fe[:, :, :], ACT.Exp, scale=-1.0))
            A(fe[:, :, :], fe[:, :, :], ACT.Ln, bias=one_b[:, :]).then_inc(fe_ready, 1)

            n = 0
            for job in JOBS:
                kind, t = job[0], job[1]
                if kind in ("K", "Q"):
                    r = rows(t)
                    wait_made(act, job)
                    if n:
                        act.wait_ge(ss_ready, n)
                    A(sq[0:r, :], ps[0:r, 3 * side(job), :], ACT.Square).then_inc(sq_ready, 1)
                    act.wait_ge(ss_ready, n + 1)
                    inv_root(stat[0:r, n % 2, :], stat[0:r, n % 2, :], 1.0 / HD).then_inc(rk_ready, 1)
                    n += 1
                elif kind in ("KT", "QT"):
                    r = rows(t)
                    wait_made(act, job)
                    if job == ("KT", NT):
                        act.wait_ge(conv_done, CT)
                    dst = kT[0:AUG, :, slice(*k_cols(t))] if kind == "KT" else qT[0:AUG, :, P * t:P * (t + 1)]
                    A(dst, buf(job, H * P)[0:AUG, :].rearrange("p (h n) -> p h n", h=H)[:, :, 0:r],
                      ACT.Copy).then_inc(used[side(job)], 1)

            act.wait_ge(consts, 2)

            def evict(n, which):
                odd = [g for g in range(len(groups(heads[n][0]))) if group_no(n, g) % 2]
                for g in odd[which]:
                    no = group_no(n, g)
                    act.wait_ge(pt_made, no + 1)
                    act.wait_ge(pv_done, no - 1) if no >= 2 else None
                    w = P * len(groups(heads[n][0])[g])
                    A(pT[:, 1, 0:w], ps[:, pt_bank(n, no), 0:w], ACT.Copy).then_inc(pt_out[1], 1)

            def extra(kind, i):
                if kind == "ASQ":
                    act.wait_ge(o_taken, i + 1)
                    A(asq[:, :], atok[:, i % 2, :], ACT.Square).then_inc(asq_ready, 1)
                elif kind == "ARS":
                    act.wait_ge(ass_ready, i + 1)
                    inv_root(stat[:, 0, :], stat[:, 0, :], 1.0 / HD).then_inc(ars_ready, 1)
                elif kind == "URS":
                    wait_used(act, ("W", i))
                    then(A(u2sq[:, :], h1b[:, :], ACT.Square, accum_out=ms[:, 2:3]))
                    inv_root(ms[:, 2:3], ms[:, 2:3], 1.0 / D).then_inc(u2rs_ready, 1)
                else:
                    job = ("U", i)
                    wait_made(act, job)
                    if i:
                        wait_made(act, ("L", i - 1))
                    A(u2T[:, :, :].rearrange("p k n -> p (k n)"), buf(job, D), ACT.Copy).then_inc(used[side(job)], 1)

            extras = {1: "ASQ", 2: "ARS", 5: "URS", 6: "U"}
            for n, (i, h) in enumerate(heads):
                if n:
                    evict(n - 1, slice(0, 1))
                act.wait_ge(max_ready, n + 1)
                if n >= 2:
                    last = len(groups(heads[n - 2][0])) - 1
                    act.wait_ge(pt_made, group_no(n - 2, last) + 1)
                job = ("S", i, h)
                A(probs[:, n % 2, 0:width(i)], buf(job, width(i)), ACT.Exp, bias=negmax[:, n % 2:n % 2 + 1],
                  accum_out=rowsum[:, i % 2, h:h + 1]).then_inc(used[side(job)], 1)
                if n:
                    evict(n - 1, slice(1, None))
                if i and h in extras:
                    extra(extras[h], i - 1)
            evict(len(heads) - 1, slice(0, None))
            for kind in ("ASQ", "ARS", "URS", "U"):
                extra(kind, NT - 1)
            act.wait_ge(gate_ask, 1)
            A(r4[0][:, :, :], r4[0][:, :, :], ACT.Exp)
            A(r8[0][:, 0, :], r8[0][:, 0, :], ACT.Exp).then_inc(gate_exp, 1)
            act.wait_ge(route_ready, 1)
            nc.scalar.sem_inc(yb_act, 1)
            nb = act.value_load(nblocks[0:1, 0:1], min_val=NE, max_val=NE + MAX_OVER)
            with act.Fori(0, nb, 2) as i:
                for s in range(2):
                    act.wait_ge(x_turned, i + s + 1)
                    A(xT[:, KT // 2:, :].rearrange("p k n -> p (k n)"), ps[:, 1, :], ACT.Copy).then_inc(xT_act, 1)
                    act.wait_ge(g_done, i + s + 1)
                    A(sil[:, :], ps[:, 2, :], ACT.Silu).then_inc(sil_ready, 1)
                    act.wait_ge(hid_turned, i + s + 1)
                    A(hidT[:, :, :].rearrange("p k n -> p (k n)"), ps[:, 4, :], ACT.Copy).then_inc(hidT_ready, 1)
                    act.wait_ge(y_done[s], i // 2 + 1)
                    act.wait_ge(yb_free, i + s + 1)
                    A(yb[:, s, 512:], ps[:, 6, :], ACT.Copy).then_inc(yb_act, 1)
            for t in range(NT):
                act.wait_ge(fin_ready, t + 1)
                act.dma_start(out[P * t:P * (t + 1), :], h1t[:, t % 2, :]).then_inc(fin_out[t % 2], 16)
            for s in range(2):
                act.wait_ge(fin_out[s], 16 * (NT // 2))

        @block.vector
        def _(dve):
            count = [0]
            V = nc.vector

            def then(ins):
                count[0] += 1
                ins.then_inc(dve_step, 1)
                dve.wait_ge(dve_step, count[0])

            def bc(ap, shape):
                return ap.unsqueeze(2).broadcast_to(shape)

            dve.wait_ge(consts, 1)
            dve.wait_ge(params, 16 * NPAR)

            dve.wait_ge(gmix_in, 16)

            def take_turned(t):
                job, r = ("T", t), rows(t)
                wait_made(dve, job)
                a, b = u_cols(t)
                V.tensor_tensor(uT[:, :, a:b], buf(job, KT * P).rearrange("p (k n) -> p k n", k=KT)[:, :, 0:r],
                                bc(gmixT[:, :], [P, KT, r]), ALU.mult).then_inc(used[side(job)], 1)

            for n, t in enumerate(toks):
                r = rows(t)
                dve.wait_ge(rs_ready, n + 1)
                if n >= 2:
                    wait_made(dve, ("T", toks[n - 2]))
                V.tensor_scalar(hn[0:r, n % 2, :], xin[0:r, n % 2, :], ms[0:r, n % 2:n % 2 + 1], None,
                                ALU.mult).then_inc(hn_ready, 1)
                if n:
                    take_turned(toks[n - 1])
            take_turned(toks[-1])
            then(V.tensor_scalar(gqk_b[:, 0, :], gqk_b[:, 0, :], HD ** -0.5, None, ALU.mult))
            then(V.tensor_tensor(gqk_b[:, 0, :], gqk_b[:, 0, :], gqk_b[:, 1, :], ALU.mult))

            def conv_norm(c):
                dve.wait_ge(rsb_ready, c + 1)
                V.scalar_tensor_tensor(conv[:, c, :], conv[:, c, :], gconvT[:, c:c + 1], rsb[:, :],
                                       ALU.mult, ALU.mult).then_inc(conv_done, 1)

            for c in range(CT):
                job = ("H", c)
                wait_made(dve, job)
                wait_used(dve, ("C", c))
                b0 = 3 * side(job)
                V.tensor_tensor(uc[:, :].rearrange("p (j n) -> p j n", j=3), ps[:, b0:b0 + 3, 0:(T + 2) // 3],
                                csb[:, :].rearrange("p (j n) -> p j n", j=3), ALU.mult).then_inc(used[side(job)], 1)
                wait_used(dve, job)
                y = conv[:, c, :]
                then(V.tensor_scalar(y, uc[:, 0:T], convwT[:, 0, c:c + 1], None, ALU.mult))
                for n in (1, 2):
                    then(V.scalar_tensor_tensor(y, uc[:, n:n + T], convwT[:, n, c:c + 1], y, ALU.mult, ALU.add))
                job = ("B", c)
                wait_made(dve, job)
                V.tensor_tensor(y, y, buf(job, T), ALU.mult).then_inc(used[side(job)], 1)
                if c:
                    conv_norm(c - 1)
            conv_norm(CT - 1)
            for t in toks[-2:]:
                wait_used(dve, ("V", t))
            then(V.tensor_tensor(fz[:, :, :], fz[:, :, :], bf_b[:, :].unsqueeze(1).broadcast_to([P, NT + 1, H]),
                                 ALU.add))
            V.scalar_tensor_tensor(fe[:, :, :], fz[:, :, :], -1.0, fz[:, :, :], ALU.mult, ALU.max).then_inc(f_ready, 1)
            dve.wait_ge(fe_ready, 1)
            for r, a, b in ((P, 0, NT), (META, NT, NT + 1)):
                ins = V.scalar_tensor_tensor(lf[0:r, a:b, :], fz[0:r, a:b, :], 0.0, fe[0:r, a:b, :],
                                             ALU.min, ALU.subtract)
            then(ins)
            V.memset(facc[:, NT, :], 0.0)
            then(V.tensor_copy(facc[:, 0, :], lf[:, NT, :]))
            for t in range(1, NT):
                ins = V.tensor_tensor(facc[:, t, :], facc[:, t - 1, :], lf[:, t - 1, :], ALU.add)
                if t < NT - 1:
                    then(ins)
            ins.then_inc(lf_ready, 1)
            job = ("CUM", 0)
            wait_made(dve, job)
            V.tensor_copy(cum[:, :, :].rearrange("p t h -> p (t h)"),
                          buf(job, (NT + 1) * H)).then_inc(used[side(job)], 1)
            wait_used(dve, job)

            n = 0
            turns = ["KT"] * (NT + 1) + ["QT"] * NT
            for kind, t in [j for j in JOBS if j[0] in ("K", "Q")]:
                job, r = (kind, t), rows(t)
                dve.wait_ge(sq_ready, n + 1)
                if n >= 2:
                    dve.wait_ge(rk_ready, n - 1)
                V.tensor_reduce(stat[0:r, n % 2, :], sq[0:r, :].rearrange("p (h d) -> p h d", h=H), AX.X,
                                ALU.add).then_inc(ss_ready, 1)
                at = toks.index(t) if kind == "K" else t
                dst = (kn if kind == "K" else qn)[0:r, at % 2, :, :]
                if at >= 2:
                    wait_made(dve, ("KT", toks[at - 2]) if kind == "K" else ("QT", at - 2))
                if kind == "K":
                    V.tensor_scalar(dst[:, :, HD], cum[0:r, t, :], -1.0, None, ALU.mult)
                else:
                    V.tensor_copy(dst[:, :, HD + 1], cum[0:r, t, :])
                dve.wait_ge(rk_ready, n + 1)
                src = ps[0:r, 3 * side(job), :].rearrange("p (h d) -> p h d", h=H)
                V.tensor_tensor(dst[:, :, 0:HD], src, bc(stat[0:r, n % 2, :], [r, H, HD]),
                                ALU.mult).then_inc(used[side(job)], 1)
                wait_used(dve, job)
                if kind == "Q":
                    V.tensor_tensor(dst[:, :, 0:HD], dst[:, :, 0:HD],
                                    gqk_b[:, 0, :].unsqueeze(1).broadcast_to([P, H, HD]),
                                    ALU.mult).then_inc(kn_ready, 1)
                else:
                    dve.sem_inc(kn_ready, 1)
                n += 1

            def extra(kind, i):
                a = atok[:, i % 2, :].rearrange("p (h d) -> p h d", h=H)
                if kind == "O":
                    dve.wait_ge(pv_done, GROUPS[(i, H - 1, len(groups(i)) - 1)] + 1)
                    then(V.reciprocal(stat[:, 1, :], rowsum[:, i % 2, :]))
                    if i >= 2:
                        wait_made(dve, ("M", i - 2))
                    V.tensor_tensor(a, ps[:, OB, :].rearrange("p (h d) -> p h d", h=H),
                                    bc(stat[:, 1, :], [P, H, HD]), ALU.mult).then_inc(o_taken, 1)
                elif kind == "ASS":
                    dve.wait_ge(asq_ready, i + 1)
                    V.tensor_reduce(stat[:, 0, :], asq[:, :].rearrange("p (h d) -> p h d", h=H), AX.X,
                                    ALU.add).then_inc(ass_ready, 1)
                elif kind == "ANORM":
                    dve.wait_ge(ars_ready, i + 1)
                    V.tensor_tensor(a, a, bc(stat[:, 0, :], [P, H, HD]), ALU.mult).then_inc(atok_ready, 1)
                elif kind == "M":
                    job = ("M", i)
                    wait_made(dve, job)
                    if i:
                        wait_made(dve, ("W", i - 1))
                    V.tensor_tensor(aT[:, :, :], ps[:, 3 * side(job), :].rearrange("p (k n) -> p k n", k=CT),
                                    bc(gattnT[:, :], [P, CT, P]), ALU.mult).then_inc(used[side(job)], 1)
                elif kind == "W":
                    job = ("W", i)
                    wait_made(dve, job)
                    dve.wait_ge(xr_in, 16 * (i + 1))
                    if i:
                        dve.wait_ge(h1_out, 16 * i)
                    V.tensor_tensor(h1b[:, :], buf(job, D), xr[:, :], ALU.add).then_inc(used[side(job)], 1)
                elif kind == "U2":
                    dve.wait_ge(u2rs_ready, i + 1)
                    if i:
                        dve.wait_ge(rows_out, 16 * i)
                        wait_made(dve, ("U", i - 1))
                    V.scalar_tensor_tensor(u2[:, :], h1b[:, :], ms[:, 2:3], gffn_b[:, :], ALU.mult,
                                           ALU.mult).then_inc(u2_ready, 1)
                else:
                    job = ("L", i)
                    wait_made(dve, job)
                    V.tensor_tensor(logits[:, i, :], ps[:, 3 * side(job), 0:NG + NE], br_b[:, :],
                                    ALU.add).then_inc(used[side(job)], 1)

            def evict(n):
                for g in range(len(groups(heads[n][0]))):
                    no = group_no(n, g)
                    if no % 2:
                        continue
                    dve.wait_ge(pt_made, no + 1)
                    if no >= 2:
                        dve.wait_ge(pv_done, no - 1)
                    w = P * len(groups(heads[n][0])[g])
                    V.tensor_copy(pT[:, 0, 0:w], ps[:, pt_bank(n, no), 0:w]).then_inc(pt_out[0], 1)

            extras = {0: "O", 1: "ASS", 2: "ANORM", 3: "M", 4: "W", 5: "U2", 7: "L"}
            dve.wait_ge(consts, 2)
            for n, (i, h) in enumerate(heads):
                job = ("S", i, h)
                wait_made(dve, job)
                if n >= 2:
                    wait_used(dve, ("S", *heads[n - 2]))
                V.tensor_reduce(negmax[:, n % 2:n % 2 + 1], buf(job, width(i)), AX.X, ALU.max,
                                negate=True).then_inc(max_ready, 1)
                if n:
                    evict(n - 1)
                if i and h in extras:
                    extra(extras[h], i - 1)
            evict(len(heads) - 1)
            for kind in ("O", "ASS", "ANORM", "M", "W", "U2", "L"):
                extra(kind, NT - 1)

            for i in (NT - 1, NT - 2):
                wait_used(dve, ("L", i))
            gl, e_l = logits[:, :, 0:NG], logits[:, :, NG:]
            gmax, gidx = r8[1][:, 0, :], r8[1][:, 1, :]
            iota_g = iota128[:, 0:NG].unsqueeze(1).broadcast_to([P, NT, NG])
            iota_e = iota128[:, 0:NE].unsqueeze(1).broadcast_to([P, NT, NE])

            def first_max(dst_max, dst_idx, src, scratch, iota, n):
                then(V.tensor_reduce(dst_max, src, AX.X, ALU.max))
                then(V.tensor_tensor(scratch, src, bc(dst_max, [P, NT, n]), ALU.is_equal))
                then(V.scalar_tensor_tensor(scratch, scratch, -100.0, iota, ALU.mult, ALU.add))
                then(V.tensor_reduce(dst_idx, scratch, AX.X, ALU.min))
                then(V.tensor_scalar(dst_idx, dst_idx, 100.0, None, ALU.add))

            first_max(gmax, gidx, gl, r4[0][:, :, :], iota_g, NG)
            then(V.tensor_tensor(r4[1][:, :, :], iota_g, bc(gidx, [P, NT, NG]), ALU.is_equal))
            oh = r4[1][:, :, :].rearrange("p t g -> p (t g)").unsqueeze(2).broadcast_to([P, NT * NG, EG])
            e4 = et[:, :, :].rearrange("p t (g e) -> p (t g) e", g=NG)
            then(V.tensor_copy(e4, oh))
            then(V.tensor_tensor(el[:, :, :], e_l, et[:, :, :], ALU.mult))
            then(V.tensor_scalar(et[:, :, :], et[:, :, :], 1.0, -NEG, ALU.subtract, ALU.mult))
            then(V.tensor_tensor(el[:, :, :], el[:, :, :], et[:, :, :], ALU.add))
            m0, x0 = r8[2][:, 0, :], r8[3][:, 0, :]
            m1, x1 = r8[2][:, 1, :], r8[3][:, 1, :]
            first_max(m0, x0, el[:, :, :], et[:, :, :], iota_e, NE)
            then(V.tensor_tensor(one0[:, :, :], iota_e, bc(x0, [P, NT, NE]), ALU.is_equal))
            then(V.scalar_tensor_tensor(el[:, :, :], one0[:, :, :], 2 * NEG, el[:, :, :], ALU.mult, ALU.add))
            first_max(m1, x1, el[:, :, :], et[:, :, :], iota_e, NE)
            then(V.tensor_tensor(one1[:, :, :], iota_e, bc(x1, [P, NT, NE]), ALU.is_equal))
            then(V.tensor_tensor(r8[0][:, 0, :], m1, m0, ALU.subtract))
            V.tensor_tensor(r4[0][:, :, :], gl, bc(gmax, [P, NT, NG]), ALU.subtract).then_inc(gate_ask, 1)
            then(V.tensor_tensor(both[:, :, :], one0[:, :, :], one1[:, :, :], ALU.add))
            then(V.memset(prev[:, 0, :], 0.0))
            for t in range(1, NT + 1):
                ins = V.tensor_tensor(prev[:, t, :], prev[:, t - 1, :], both[:, t - 1, :], ALU.add)
                if t < NT:
                    then(ins)
            ins.then_inc(gate_ask, 1)
            dve.wait_ge(gate_exp, 1)
            then(V.tensor_reduce(r8[4][:, 0, :], r4[0][:, :, :], AX.X, ALU.add))
            then(V.tensor_scalar(r8[4][:, 1, :], r8[0][:, 0, :], 1.0, None, ALU.add))
            then(V.tensor_tensor(r8[4][:, 0, :], r8[4][:, 0, :], r8[4][:, 1, :], ALU.mult))
            then(V.reciprocal(gates[:, 0, :], r8[4][:, 0, :]))
            then(V.tensor_tensor(gates[:, 1, :], gates[:, 0, :], r8[0][:, 0, :], ALU.mult))
            job = ("RANK", 0)
            wait_made(dve, job)
            b0 = 3 * side(job)
            V.tensor_copy(cnt[:, :], ps[:, b0, NT * NE:(NT + 1) * NE])
            V.tensor_copy(ranks[:, :, :].rearrange("p t e -> p (t e)"), ps[:, b0, 0:NT * NE]).then_inc(used[side(job)], 1)
            wait_used(dve, job)
            rank, jblk, row, col, ovs, gt0 = (r8[n][:, :, :] for n in (4, 5, 6, 7, 8, 9))
            for k, one in ((0, one0), (1, one1)):
                then(V.tensor_tensor(et[:, :, :], one[:, :, :], ranks[:, :, :], ALU.mult))
                then(V.tensor_reduce(rank[:, k, :], et[:, :, :], AX.X, ALU.add))
            lim = t256[:, 0, 0:7]
            then(V.tensor_scalar(lim, iota128[:, 1:8], float(P), None, ALU.mult))
            c7 = cmp7[:, :, 0:7]
            then(V.tensor_tensor(c7, bc(cnt[:, :], [P, NE, 7]), lim.unsqueeze(1).broadcast_to([P, NE, 7]), ALU.is_gt))
            then(V.tensor_reduce(nover[:, :], c7, AX.X, ALU.add))
            then(V.tensor_copy(over[:, 0, :], nover[:, :]))
            cur = 0
            for d in (1, 2, 4, 8, 16):
                then(V.tensor_copy(over[:, 1 - cur, 0:d], over[:, cur, 0:d]))
                then(V.tensor_tensor(over[:, 1 - cur, d:], over[:, cur, d:], over[:, cur, 0:NE - d], ALU.add))
                cur = 1 - cur
            end = over[:, cur, :]
            begin = over[:, 1 - cur, :]
            NX = COLS - NE
            then(V.tensor_tensor(bcmp[:, 0:NX, :], end.unsqueeze(1).broadcast_to([P, NX, NE]),
                                 bc(iota128[:, 0:NX], [P, NX, NE]), ALU.is_le))
            then(V.tensor_reduce(tabf[0][:, 0:NX], bcmp[:, 0:NX, :], AX.X, ALU.add))
            V.tensor_scalar(bexp[:, NE:], tabf[0][:, 0:NX], float(NE - 1), None, ALU.min)
            V.tensor_copy(bexp[:, 0:NE], iota128[:, 0:NE])
            V.tensor_scalar(nblocks[:, :], end[:, NE - 1:NE], float(NE), None, ALU.add)
            then(V.tensor_tensor(begin, end, nover[:, :], ALU.subtract))
            for k, one in ((0, one0), (1, one1)):
                then(V.tensor_tensor(et[:, :, :], one[:, :, :], begin.unsqueeze(1).broadcast_to([P, NT, NE]), ALU.mult))
                then(V.tensor_reduce(ovs[:, k, :], et[:, :, :], AX.X, ALU.add))
            lim1 = lim.unsqueeze(1).broadcast_to([P, 16, 7])
            c16 = t256[:, :, 8:15]
            flat = r8[4][:, :, :].rearrange("p k t -> p (k t)")
            then(V.tensor_tensor(c16, bc(flat, [P, 16, 7]), lim1, ALU.is_ge))
            then(V.tensor_reduce(r8[5][:, :, :].rearrange("p k t -> p (k t)"), c16, AX.X, ALU.add))
            then(V.scalar_tensor_tensor(row, jblk, -float(P), rank, ALU.mult, ALU.add))
            then(V.tensor_scalar(gt0, jblk, 0.0, None, ALU.is_gt))
            then(V.scalar_tensor_tensor(col, jblk, float(NE - 1), ovs, ALU.add, ALU.add))
            then(V.tensor_tensor(col, col, r8[3][:, :, :], ALU.subtract))
            then(V.tensor_tensor(col, col, gt0, ALU.mult))
            then(V.tensor_tensor(col, col, r8[3][:, :, :], ALU.add))
            code = r8[0][:, :, :]
            V.tensor_copy(code[:, 0, :], tokcode[:, :])
            then(V.tensor_scalar(code[:, 1, :], tokcode[:, :], float(T), None, ALU.add))
            for k in range(2):
                for t in range(NT):
                    m = NT * k + t
                    V.tensor_scalar(rowhot[:, m, :], iota128[:, :], row[:, k, t:t + 1], None, ALU.is_equal)
                    ins = V.tensor_scalar(colhot[:, m, :], iota128[:, 0:COLS], col[:, k, t:t + 1],
                                          code[:, k, t:t + 1], ALU.is_equal, ALU.mult)
            ins.then_inc(gate_ask, 1)
            job = ("TABLE", 0)
            wait_made(dve, job)
            c, pad, hi = (tabf[n][:, :] for n in range(3))
            V.tensor_copy(c, buf(job, COLS)).then_inc(used[side(job)], 1)
            wait_used(dve, job)
            then(V.tensor_scalar(pad, c, 0.5, float(NOWHERE), ALU.is_lt, ALU.mult))
            then(V.scalar_tensor_tensor(pad, c, -1.0, pad, ALU.add, ALU.add))
            V.tensor_copy(stab[:, :], pad)
            then(V.tensor_scalar(hi, c, T + 0.5, -float(T), ALU.is_gt, ALU.mult))
            V.tensor_tensor(gtab[:, :], pad, hi, ALU.add).then_inc(route_ready, 1)

            dve.wait_ge(route_ready, 1)
            dve.sem_inc(yb_dve, 1)
            nb = dve.value_load(nblocks[0:1, 0:1], min_val=NE, max_val=NE + MAX_OVER)
            with dve.Fori(0, nb, 2) as i:
                for s in range(2):
                    dve.wait_ge(x_turned, i + s + 1)
                    V.tensor_copy(xT[:, 0:KT // 2, :].rearrange("p k n -> p (k n)"), ps[:, 0, :]).then_inc(xT_dve, 1)
                    dve.wait_ge(sil_ready, i + s + 1)
                    dve.wait_ge(u_done, i + s + 1)
                    V.tensor_tensor(hid[:, :], sil[:, :], ps[:, 3, :], ALU.mult).then_inc(hid_ready, 1)
                    dve.wait_ge(y_done[s], i // 2 + 1)
                    dve.wait_ge(yb_free, i + s + 1)
                    V.tensor_copy(yb[:, s, 0:512], ps[:, 5, :]).then_inc(yb_dve, 1)

            for t in range(NT):
                s = t % 2
                dve.wait_ge(y_in[s], 48 * (t // 2 + 1))
                then(V.scalar_tensor_tensor(h1t[:, s, :], y0[:, s, :], gates[:, 0, t:t + 1], h1t[:, s, :],
                                            ALU.mult, ALU.add))
                V.scalar_tensor_tensor(h1t[:, s, :], y1[:, s, :], gates[:, 1, t:t + 1], h1t[:, s, :],
                                       ALU.mult, ALU.add).then_inc(fin_ready, 1)


_ORDER = ["x", "meta_tokens", "norm_mix_g", "w_in", "b_forget", "q_norm_g", "k_norm_g", "conv_w", "attn_out_g",
          "conv_out_g", "w_out", "norm_ffn_g", "w_router_group", "b_router_group", "w_router_expert",
          "b_router_expert", "w_gate", "w_up", "w_down"]


def kernel(**inputs):
    import numpy as _np
    import concourse.bacc as _bacc
    from concourse import mybir as _mybir
    from concourse.bass_utils import run_bass_kernel_spmd as _run

    nc = _bacc.Bacc("TRN2", target_bir_lowering=False, num_devices=1)
    arrays, args = {}, []
    for name in _ORDER:
        a = _np.ascontiguousarray(inputs[name])
        if name != "meta_tokens":
            a = a[0]
        arrays[f"in_{name}"] = a
        args.append(nc.dram_tensor(f"in_{name}", a.shape, _mybir.dt.from_np(a.dtype), kind="ExternalInput").ap())
    args.append(nc.dram_tensor("out_0", (T, D), F32, kind="ExternalOutput").ap())
    build(nc, *args)
    r = _run(nc, [arrays], core_ids=[0])
    return r.results[0]["out_0"].reshape(1, T, D)
```

```python
import concourse.bass as bass
from concourse import mybir
from contextlib import ExitStack

F32 = mybir.dt.float32
BF16 = mybir.dt.bfloat16
I32 = mybir.dt.int32
U32 = mybir.dt.uint32
ALU = mybir.AluOpType
ACT = mybir.ActivationFunctionType
AX = mybir.AxisListType

P = 128
D = 1024
KT = D // P
T = 1024
NT = T // P
META = 16
KEYS = T + META
KPAD = KEYS + META
H = 8
HD = 64
AW = H * HD
CW = D - AW
CT = CW // P
AUG = HD + 2
NG = 4
NE = 32
EG = NE // NG
F = 512
FT = F // P
EPS = 1e-6
NEG = -1e30
MAX_OVER = 2 * T // P - 1
COLS = NE + MAX_OVER + 3
NOWHERE = 1 << 20

VC = (AW + H) // 2

COL_V, COL_F = 2 * AW, 3 * AW
COL_B = 3 * AW + H
COL_C, COL_H = COL_B + CW, COL_B + 2 * CW

BASE = 16512


class Plan:

    def __init__(self, nc, at, end):
        self.nc, self.at, self.end = nc, at, end

    def __call__(self, name, shape, dt=F32):
        n = 1
        for s in shape[1:]:
            n *= s
        size = n * (2 if dt == BF16 else 4)
        t = self.nc.alloc_sbuf_tensor_at(name, list(shape), dt, offset=self.at)
        self.at += -(-size // 32) * 32
        assert self.at <= self.end, (name, self.at, self.end)
        return t


EXTRA = {2: "N", 3: "M", 4: "W", 6: "U", 7: "L"}


def ring_jobs():
    jobs = [("T", NT)] + [("T", t) for t in range(NT)]
    for c in range(CT):
        jobs += [("C", c), ("H", c), ("B", c)]
        if c:
            jobs.append(("R", c - 1))
    jobs += [("V", NT), ("V", 0), ("R", CT - 1)] + [("V", t) for t in range(1, NT)]
    jobs.append(("CUM", 0))
    toks = [NT] + list(range(NT))
    jobs += [("K", NT), ("K", 0)]
    for n in range(1, len(toks)):
        jobs.append(("KT", toks[n - 1]))
        jobs.append(("K", toks[n + 1]) if n + 1 < len(toks) else ("Q", 0))
    jobs += [("KT", NT - 1), ("Q", 1)]
    for t in range(NT):
        jobs.append(("QT", t))
        if t + 2 < NT:
            jobs.append(("Q", t + 2))
    for i in range(NT):
        for h in range(H):
            jobs.append(("S", i, h))
            if i and h in EXTRA:
                jobs.append((EXTRA[h], i - 1))
    jobs += [(k, NT - 1) for k in ("N", "M", "W", "U", "L")]
    jobs += [("LT", 0), ("RANK", 0), ("TABLE", 0)]
    return jobs


JOBS = ring_jobs()
TURN = {job: n for n, job in enumerate(JOBS)}


def side(job):
    return TURN[job] % 2


def uses(job):
    return TURN[job] // 2 + 1


def groups(i):
    blocks = list(range(i + 2))
    n = -(-len(blocks) // 4)
    if n == 1 and len(blocks) > 2:
        n = 2
    cuts = [len(blocks) * g // n for g in range(n + 1)]
    return [blocks[a:b] for a, b in zip(cuts, cuts[1:])]


GROUPS = {}
for _i in range(NT):
    for _h in range(H):
        for _g in range(len(groups(_i))):
            GROUPS[(_i, _h, _g)] = len(GROUPS)


def build(nc, x, meta, g_mix, w_in, b_forget, gq, gk, conv_w, g_attn, g_conv, w_out, g_ffn,
          w_rg, b_rg, w_re, b_re, w_gate, w_up, w_down, out):
    ctx = ExitStack()
    with ctx:
        def sem(name):
            return ctx.enter_context(nc.semaphore(name))

        top = BASE + 212800
        small = Plan(nc, BASE, BASE + 20000)
        ident = small("ident", [P, P])
        identb = small("identb", [P, P], BF16)
        maskb = small("maskb", [P, P + META], BF16)
        tri = small("tri", [P, P])
        tris = small("tris", [P, P])
        ones = small("ones", [P, P])
        blockones = small("blockones", [P, P])
        iota128 = small("iota128", [P, P])
        sel = small("sel", [H, CT, P])
        l2 = small("l2", [P, H])
        l2T = small("l2T", [H, P])
        wr = small("wr", [P, KT, NG + NE])
        gmixT = small("gmixT", [P, KT])
        gattnT = small("gattnT", [P, CT])
        gconvT = small("gconvT", [P, CT])
        convwT = small("convwT", [P, 3, CT])
        bf_b = small("bf_b", [P, H])
        gqk_b = small("gqk_b", [P, 2, HD])
        br_c = small("br_c", [NG + NE, 1])
        stat = small("stat", [P, 2, H])
        ms = small("ms", [P, 4])
        negmax = small("negmax", [P, 2])
        rowsum = small("rowsum", [P, 2, H])
        lT = small("lT", [P, T])
        logits = small("logits", [P, NT, NG + NE])
        tokcode = small("tokcode", [P, NT])
        gates = small("gates", [P, 2, NT])
        eps_b = small("eps_b", [P, 1])
        one_b = small("one_b", [P, 1])
        gtab = small("gtab", [P, COLS], I32)
        stab = small("stab", [P, COLS], I32)
        bexp = small("bexp", [P, COLS], I32)
        nblocks = small("nblocks", [P, 1], I32)
        idxg = small("idxg", [P, 2], I32)
        idxs = small("idxs", [P, 2], I32)

        A0 = small.at

        p = Plan(nc, A0, top)
        uT = p("uT", [P, KT, KEYS])
        ring_at = p.at
        win = p("win", [P, 3, KT, AW + H])
        conv = p("conv", [P, CT, T])
        v_at = p.at
        v = p("v", [P, NT + 1, AW])
        qT_at = p.at
        qT = p("qT", [P, H, T])
        kT = p("kT", [P, H, KPAD])
        kn_at = p.at
        c_ = Plan(nc, qT_at, kn_at)
        xin = c_("xin", [P, 2, D])
        hn = c_("hn", [P, 2, D])
        sqj = c_("sqj", [P, D])
        csb = c_("csb", [P, T + 2])
        uc = c_("uc", [P, T + 2])
        ysq = c_("ysq", [P, T])
        rsb = c_("rsb", [P, T])
        m_ = Plan(nc, kn_at, top)
        kn = m_("kn", [P, 2, H, AUG])
        qn = m_("qn", [P, 2, H, AUG])
        fz = m_("fz", [P, NT + 1, H])
        fe = m_("fe", [P, NT + 1, H])
        lf = m_("lf", [P, NT + 1, H])
        facc = m_("facc", [P, NT + 1, H])
        cum = m_("cum", [P, NT + 1, H])
        sq = m_("sq", [P, AW])
        xr = Plan(nc, kn_at, top)("xr", [P, D])
        a_ = Plan(nc, A0, ring_at)
        probs = a_("probs", [P, 2, KPAD])
        pT = a_("pT", [P, 2, (NT + 1) * P])
        ot = a_("ot", [P, AW])
        rsa = a_("rsa", [P, AW])
        asq = a_("asq", [P, AW])
        aT = a_("aT", [P, CT, P])
        u2T = a_("u2T", [P, KT, P])
        r_ = Plan(nc, ring_at, v_at - 4 * CT * T)
        wo = r_("wo", [P, KT, D])
        h1b = r_("h1b", [P, D])
        u2 = r_("u2", [P, D])
        gffn_b = r_("gffn_b", [P, D])
        u2sq = r_("u2sq", [P, D])
        q_ = Plan(nc, A0, ring_at)
        one0 = q_("one0", [P, NT, NE])
        one1 = q_("one1", [P, NT, NE])
        both = q_("both", [P, NT, NE])
        prev = q_("prev", [P, NT + 1, NE])
        ranks = q_("ranks", [P, NT, NE])
        el = q_("el", [P, NT, NE])
        et = q_("et", [P, NT, NE])
        cmp7 = q_("cmp7", [P, NE, 8])
        t256 = q_("t256", [P, 16, 16])
        oc = Plan(nc, ring_at, v_at)
        rowhot = oc("rowhot", [P, 2 * NT, P])
        colhot = oc("colhot", [P, 2 * NT, COLS])
        over = oc("over", [P, 2, NE])
        nover = oc("nover", [P, NE])
        cnt = oc("cnt", [P, NE])
        bcmp = oc("bcmp", [P, MAX_OVER + 3, NE])
        r8 = [oc(f"r8_{n}", [P, 2, NT]) for n in range(10)]
        r4 = [oc(f"r4_{n}", [P, NT, NG]) for n in range(2)]
        tabf = [oc(f"tabf_{n}", [P, COLS]) for n in range(3)]
        iotag = oc("iotag", [P, NG])
        w_ = Plan(nc, v_at, top)
        wg = w_("wg", [P, 2, KT, F])
        wu = w_("wu", [P, 2, KT, F])
        wd = w_("wd", [P, 2, FT, D])
        e_ = Plan(nc, oc.at, v_at)
        xg = e_("xg", [P, 2, D])
        yb = e_("yb", [P, 2, D])
        f_ = Plan(nc, A0, ring_at)
        xT = f_("xT", [P, KT, P])
        sil = f_("sil", [P, F])
        hid = f_("hid", [P, F])
        hidT = f_("hidT", [P, FT, P])
        g_ = Plan(nc, f_.at, ring_at)
        h1t = g_("h1t", [P, 2, D])
        l_ = Plan(nc, v_at, top)
        y0 = l_("y0", [P, 2, D])
        y1 = l_("y1", [P, 2, D])

        ps = ctx.enter_context(nc.psum_tensor("ps", [P, 8, 512], F32))
        OB = 7

        NH = H * NT
        ONE_BANK = NH - H - 1

        def pt_bank(n, no):
            return 6 if no % 2 == 0 or n >= ONE_BANK else 2
        big = ps[:, :, :].rearrange("p b n -> p (b n)")

        def buf(job, width, rows=P):
            at = 3 * 512 * side(job)
            return big[0:rows, at:at + width]

        dram_u2 = nc.dram_tensor("u2_rows", [T, D], F32).ap()
        dram_h1 = nc.dram_tensor("h1_rows", [T, D], F32).ap()
        ys = nc.dram_tensor("expert_rows", [2 * T, D], F32).ap()

        made = [sem("ring_made_0"), sem("ring_made_1")]
        used = [sem("ring_used_0"), sem("ring_used_1")]
        consts = sem("consts")
        gmix_in = sem("gmix_in")
        params = sem("params")
        x_in = [sem("x_in_0"), sem("x_in_1")]
        win_in = [sem(f"win_in_{s}") for s in range(3)]
        rs_ready = sem("rs_ready")
        hn_ready = sem("hn_ready")
        act_step = sem("act_step")
        dve_step = sem("dve_step")
        pool_step = sem("pool_step")
        ysq_ready = sem("ysq_ready")
        rsb_ready = sem("rsb_ready")
        conv_done = sem("conv_done")
        f_ready = sem("f_ready")
        fe_ready = sem("fe_ready")
        lf_ready = sem("lf_ready")
        sq_ready = sem("sq_ready")
        ss_ready = sem("ss_ready")
        rk_ready = sem("rk_ready")
        kn_ready = sem("kn_ready")
        max_ready = sem("max_ready")
        pt_made = sem("pt_made")
        pt_out = [sem("pt_out_even"), sem("pt_out_odd")]
        pv_done = sem("pv_done")
        o_taken = sem("o_taken")
        asq_ready = sem("asq_ready")
        l2_ready = sem("l2_ready")
        rsa_ready = sem("rsa_ready")
        aT_ready = sem("aT_ready")
        wo_ready = sem("wo_ready")
        wo_in = sem("wo_in")
        xr_in = sem("xr_in")
        u2rs_ready = sem("u2rs_ready")
        u2_ready = sem("u2_ready")
        rows_out = sem("u2_rows_out")
        h1_out = sem("h1_rows_out")
        gexp_ready = sem("gexp_ready")
        route_ready = sem("route_ready")
        gate_ask = sem("gate_ask")
        gate_exp = sem("gate_exp")
        wg_in = [sem("wg_in_0"), sem("wg_in_1")]
        wu_in = [sem("wu_in_0"), sem("wu_in_1")]
        wd_in = [sem("wd_in_0"), sem("wd_in_1")]
        g_done = sem("g_done")
        u_done = sem("u_done")
        y_done = [sem("y_done_0"), sem("y_done_1")]
        xg_in = [sem("xg_in_0"), sem("xg_in_1")]
        x_turned = sem("x_turned")
        xT_dve = sem("xT_dve")
        xT_act = sem("xT_act")
        sil_ready = sem("sil_ready")
        hid_ready = sem("hid_ready")
        hid_turned = sem("hid_turned")
        hidT_ready = sem("hidT_ready")
        yb_dve = sem("yb_dve")
        yb_act = sem("yb_act")
        ys_out = [sem("ys_out_0"), sem("ys_out_1")]
        idx_ready = sem("idx_ready")
        pool_pass = sem("pool_pass")
        yb_free = sem("yb_free")
        all_out = sem("all_expert_rows_out")
        y_in = [sem("y_in_0"), sem("y_in_1")]
        fin_ready = sem("fin_ready")
        fin_out = [sem("fin_out_0"), sem("fin_out_1")]

        def wait_made(eng, job):
            eng.wait_ge(made[side(job)], uses(job))

        def wait_used(eng, job):
            eng.wait_ge(used[side(job)], uses(job))

        toks = [NT] + list(range(NT))

        def rows(t):
            return META if t == NT else P

        def u_cols(t):
            return (0, META) if t == NT else (META + P * t, META + P * (t + 1))

        heads = [(i, h) for i in range(NT) for h in range(H)]
        qk = [("K", t) for t in toks] + [("Q", t) for t in range(NT)]
        NPAR = 12

        def width(i):
            return KPAD if i == NT - 1 else META + P * (i + 1)

        def banks(i):
            return -(-width(i) // 512)

        def score_buf(i, h):
            b0, n = 3 * side(("S", i, h)), banks(i)
            return ps[:, b0:b0 + n, 0:width(i) // n]

        def group_no(n, g):
            return GROUPS[(*heads[n], g)]

        block = ctx.enter_context(nc.Block())

        @block.sync
        def _(sp):
            w_in_k = w_in.rearrange("(k p) c -> p k c", p=P)

            def load_x(n):
                t = toks[n]
                if n >= 2:
                    sp.wait_ge(hn_ready, n - 1)
                src = meta[:, :] if t == NT else x[P * t:P * (t + 1), :]
                sp.dma_start(xin[0:rows(t), n % 2, :], src).then_inc(x_in[n % 2], 16)

            def load_chunk(u):
                s = u % 3
                if u >= 3:
                    wait_made(sp, ("B", u - 3))
                if u < CT:
                    for n, col in enumerate((COL_B, COL_C, COL_H)):
                        sp.dma_start(win[:, s, :, P * n:P * (n + 1)],
                                     w_in_k[:, :, col + P * u:col + P * (u + 1)]).then_inc(win_in[s], 16)
                else:
                    col = (COL_V, AW, 0)[u - CT]
                    n = AW + H if col == COL_V else AW
                    sp.dma_start(win[:, s, :, 0:n], w_in_k[:, :, col:col + n]).then_inc(win_in[s], 16)

            load_x(0)
            load_x(1)
            sp.dma_start(gmixT[:, :], g_mix.rearrange("(k p) -> p k", p=P),
                         allow_slow_non_contiguous=True).then_inc(gmix_in, 16)
            load_x(2)
            load_chunk(0)
            for n in range(3, NT + 1):
                load_x(n)
            load_chunk(1)
            load_chunk(2)
            for u in range(3, CT + 3):
                load_chunk(u)
            wait_made(sp, ("Q", NT - 1))
            sp.dma_start(wo[:, :, :], w_out.rearrange("(k p) c -> p k c", p=P)).then_inc(wo_in, 16)
            sp.dma_start(gffn_b[:, :], g_ffn.partition_broadcast(P)).then_inc(wo_in, 16)
            for i in range(NT):
                if i:
                    wait_used(sp, ("W", i - 1))
                sp.dma_start(xr[:, :], x[P * i:P * (i + 1), :]).then_inc(xr_in, 16)
            sp.wait_ge(pv_done, NH)

            def load_expert(e, s):
                sp.dma_start(wg[:, s, :, :], w_gate[e].rearrange("(k p) f -> p k f", p=P)).then_inc(wg_in[s], 16)
                sp.dma_start(wu[:, s, :, :], w_up[e].rearrange("(k p) f -> p k f", p=P)).then_inc(wu_in[s], 16)
                sp.dma_start(wd[:, s, :, :], w_down[e].rearrange("(k p) f -> p k f", p=P)).then_inc(wd_in[s], 16)

            load_expert(0, 0)
            wait_used(sp, ("W", NT - 1))
            load_expert(1, 1)
            sp.wait_ge(route_ready, 1)
            nb = sp.value_load(nblocks[0:1, 0:1], min_val=NE, max_val=NE + MAX_OVER)
            with sp.Fori(2, nb, 2) as i:
                for s in range(2):
                    e = sp.value_load(bexp[0:1, bass.ds(i + s, 1)], min_val=0, max_val=NE - 1)
                    sp.wait_ge(g_done, i + s - 1)
                    sp.dma_start(wg[:, s, :, :], w_gate[bass.ds(e, 1)].rearrange("o (k p) f -> p (o k) f", p=P)
                                 ).then_inc(wg_in[s], 16)
                    sp.wait_ge(u_done, i + s - 1)
                    sp.dma_start(wu[:, s, :, :], w_up[bass.ds(e, 1)].rearrange("o (k p) f -> p (o k) f", p=P)
                                 ).then_inc(wu_in[s], 16)
                    sp.wait_ge(y_done[s], i // 2)
                    sp.dma_start(wd[:, s, :, :], w_down[bass.ds(e, 1)].rearrange("o (k p) f -> p (o k) f", p=P)
                                 ).then_inc(wd_in[s], 16)
            sp.wait_ge(all_out, 1)
            for t in range(NT):
                s = t % 2
                if t >= 2:
                    sp.wait_ge(fin_out[s], 16 * (t // 2))
                for dst, src in ((h1t, dram_h1[P * t:P * (t + 1), :]), (y0, ys[P * t:P * (t + 1), :]),
                                 (y1, ys[T + P * t:T + P * (t + 1), :])):
                    sp.dma_start(dst[:, s, :], src).then_inc(y_in[s], 16)

        @block.gpsimd
        def _(pool):
            count = [0]

            def then(ins):
                count[0] += 1
                ins.then_inc(pool_step, 1)
                pool.wait_ge(pool_step, count[0])

            for tile_, value in ((ident, 0.0), (identb, 0.0), (maskb, 0.0), (tri, 1.0), (tris, 1.0),
                                 (ones, 1.0), (sel, 0.0), (eps_b, EPS), (one_b, 1.0), (blockones, 0.0), (lf, 0.0), (fz, 0.0), (kn, 1.0), (qn, 1.0)):
                then(nc.gpsimd.memset(tile_[:], value))
            for tile_, op, fill in ((ident, ALU.not_equal, 1.0), (identb, ALU.not_equal, 1.0)):
                then(nc.gpsimd.affine_select(out=tile_[:], in_=tile_[:], compare_op=op, fill=fill, base=0,
                                             pattern=[[-1, P]], channel_multiplier=1))
            then(nc.gpsimd.affine_select(out=maskb[:], in_=maskb[:], compare_op=ALU.is_ge, fill=NEG, base=0,
                                         pattern=[[-1, P + META]], channel_multiplier=1))
            then(nc.gpsimd.affine_select(out=sel[:].rearrange("h c (r d) -> h c r d", r=2),
                                         in_=sel[:].rearrange("h c (r d) -> h c r d", r=2),
                                         compare_op=ALU.not_equal, fill=EPS, base=0,
                                         pattern=[[-2, CT], [-1, 2], [0, HD]], channel_multiplier=1))
            then(nc.gpsimd.affine_select(out=tri[:], in_=tri[:], compare_op=ALU.is_ge, fill=0.0, base=0,
                                         pattern=[[1, P]], channel_multiplier=-1))
            then(nc.gpsimd.affine_select(out=tris[:], in_=tris[:], compare_op=ALU.is_gt, fill=0.0, base=0,
                                         pattern=[[1, P]], channel_multiplier=-1))
            for n in range(2):
                then(nc.gpsimd.memset(blockones[HD * n:HD * (n + 1), HD * n:HD * (n + 1)], 1.0 / HD))
            then(nc.gpsimd.iota(iota128[:], pattern=[[1, P]], base=0, channel_multiplier=0,
                                allow_small_or_imprecise_dtypes=True))
            nc.gpsimd.iota(tokcode[:], pattern=[[P, NT]], base=1, channel_multiplier=1,
                           allow_small_or_imprecise_dtypes=True).then_inc(consts, 1)
            slow = dict(allow_slow_non_contiguous=True)
            pool.dma_start(wr[:, :, 0:NG], w_rg.rearrange("(k p) c -> p k c", p=P), **slow).then_inc(params, 16)
            pool.dma_start(wr[:, :, NG:], w_re.rearrange("(k p) c -> p k c", p=P), **slow).then_inc(params, 16)
            pool.dma_start(gattnT[:, :], g_attn.rearrange("(k p) -> p k", p=P), **slow).then_inc(params, 16)
            pool.dma_start(gconvT[:, :], g_conv.rearrange("(k p) -> p k", p=P), **slow).then_inc(params, 16)
            for n in range(3):
                pool.dma_start(convwT[:, n, :], conv_w[n].rearrange("(k p) -> p k", p=P),
                               **slow).then_inc(params, 16)
            pool.dma_start(bf_b[:, :], b_forget.partition_broadcast(P)).then_inc(params, 16)
            pool.dma_start(gqk_b[:, 0, :], gq.partition_broadcast(P)).then_inc(params, 16)
            pool.dma_start(gqk_b[:, 1, :], gk.partition_broadcast(P)).then_inc(params, 16)
            pool.dma_start(br_c[0:NG, :], b_rg.unsqueeze(1), **slow).then_inc(params, 16)
            pool.dma_start(br_c[NG:, :], b_re.unsqueeze(1), **slow).then_inc(params, 16)
            pool.wait_ge(conv_done, CT)
            nc.gpsimd.memset(kT[:, :, KEYS:], 0.0).then_inc(consts, 1)
            for i in range(NT):
                wait_used(pool, ("W", i))
                pool.dma_start(dram_h1[P * i:P * (i + 1), :], h1b[:, :]).then_inc(h1_out, 16)
                pool.wait_ge(u2_ready, i + 1)
                pool.dma_start(dram_u2[P * i:P * (i + 1), :], u2[:, :]).then_inc(rows_out, 16)
            pool.wait_ge(rows_out, 16 * NT)
            pool.wait_ge(route_ready, 1)
            nc.gpsimd.memset(xg[:], 0.0).then_inc(pool_step, 1)
            count[0] += 1
            pool.wait_ge(pool_step, count[0])
            last_token, last_row = pool.to_reg(T - 1), pool.to_reg(2 * T - 1)
            for s in range(2):
                nc.gpsimd.tensor_copy(idxg[:, s:s + 1], gtab[:, s:s + 1]).then_inc(idx_ready, 1)
                pool.wait_ge(idx_ready, s + 1)
                nc.gpsimd.indirect_dma_start(
                    out=xg[:, s, :], out_offset=None, in_=dram_u2[:, :],
                    in_offset=bass.IndirectOffsetOnAxis(ap=idxg[:, s:s + 1].bitcast(U32), axis=0),
                    bounds_check=last_token, oob_is_err=False).then_inc(xg_in[s], 16)
                pool.sem_inc(yb_free, 1)
            nb = pool.value_load(nblocks[0:1, 0:1], min_val=NE, max_val=NE + MAX_OVER)
            with pool.Fori(0, nb, 2) as i:
                for s in range(2):
                    nc.gpsimd.tensor_copy(idxs[:, s:s + 1], stab[:, bass.ds(i + s, 1)]).then_inc(idx_ready, 1)
                    pool.wait_ge(idx_ready, 2 * (i + s) + 3)
                    pool.wait_ge(yb_dve, i + s + 2)
                    pool.wait_ge(yb_act, i + s + 2)
                    pool.sem_inc(pool_pass, 1)
                    nc.gpsimd.indirect_dma_start(
                        out=ys[:, :], in_=yb[:, s, :], in_offset=None,
                        out_offset=bass.IndirectOffsetOnAxis(ap=idxs[:, s:s + 1].bitcast(U32), axis=0),
                        bounds_check=last_row, oob_is_err=False).then_inc(ys_out[s], 16)
                    pool.wait_ge(x_turned, i + s + 1)
                    nc.gpsimd.tensor_copy(idxg[:, s:s + 1], gtab[:, bass.ds(i + s + 2, 1)]).then_inc(idx_ready, 1)
                    pool.wait_ge(idx_ready, 2 * (i + s) + 4)
                    pool.sem_inc(pool_pass, 1)
                    nc.gpsimd.indirect_dma_start(
                        out=xg[:, s, :], out_offset=None, in_=dram_u2[:, :],
                        in_offset=bass.IndirectOffsetOnAxis(ap=idxg[:, s:s + 1].bitcast(U32), axis=0),
                        bounds_check=last_token, oob_is_err=False).then_inc(xg_in[s], 16)
                    pool.wait_ge(ys_out[s], 16 * (i // 2 + 1))
                    pool.sem_inc(yb_free, 1)
            pairs = (nb + 1) // 2
            for s in range(2):
                pool.wait_ge(ys_out[s], 16 * pairs)
                pool.wait_ge(xg_in[s], 16 * pairs + 16)
            pool.wait_ge(h1_out, 16 * NT)
            pool.sem_inc(all_out, 1)

        @block.tensor
        def _(pe):
            mm = nc.tensor.matmul

            def start(job):
                if uses(job) > 1:
                    pe.wait_ge(used[side(job)], uses(job) - 1)

            def done(job, last):
                last.then_inc(made[side(job)], 1)

            def turn_x(t, n):
                job = ("T", t)
                start(job)
                pe.wait_ge(hn_ready, n + 1)
                r = rows(t)
                for k in range(KT):
                    last = nc.tensor.transpose(buf(job, KT * P)[:, P * k:P * k + r],
                                               hn[0:r, n % 2, P * k:P * (k + 1)], ident[0:r, 0:r])
                done(job, last)

            def wait_chunk(u):
                per = [3 if n < CT else 1 for n in range(CT + 3)]
                pe.wait_ge(win_in[u % 3], 16 * sum(per[n] for n in range(u + 1) if n % 3 == u % 3))

            def channels(kind, c):
                job = (kind, c)
                start(job)
                sect = {"B": 0, "C": 1, "H": 2}[kind]
                n_chunk, size, at = (2, 512, META) if kind == "B" else (3, (T + 2) // 3, META - 2)
                for j in range(n_chunk):
                    for k in range(KT):
                        last = mm(ps[:, 3 * side(job) + j, 0:size], win[:, c % 3, k, P * sect:P * (sect + 1)],
                                  uT[:, k, at + size * j:at + size * (j + 1)], start=(k == 0), stop=(k == KT - 1))
                done(job, last)

            def conv_mean(c):
                job = ("R", c)
                start(job)
                pe.wait_ge(ysq_ready, c + 1)
                for j in range(2):
                    last = mm(ps[:, 3 * side(job) + j, :], blockones[:, :], ysq[:, 512 * j:512 * (j + 1)],
                              start=True, stop=True)
                done(job, last)

            def tokens(job, slot, n_chunk, size):
                t = job[1]
                a, b = u_cols(t)
                start(job)
                for j in range(n_chunk):
                    for k in range(KT):
                        last = mm(ps[0:rows(t), 3 * side(job) + j, 0:size], uT[:, k, a:b],
                                  win[:, slot, k, size * j:size * (j + 1)], start=(k == 0), stop=(k == KT - 1))
                done(job, last)

            def turn_heads(job, n):
                kind, t = job
                start(job)
                pe.wait_ge(kn_ready, n + 1)
                src, at = (kn, toks.index(t)) if kind == "KT" else (qn, t)
                r = rows(t)
                for h in range(H):
                    last = nc.tensor.transpose(buf(job, H * P)[0:AUG, P * h:P * h + r], src[0:r, at % 2, h, :],
                                               ident[0:r, 0:r])
                done(job, last)

            def scores(n):
                i, h = heads[n]
                job = ("S", i, h)
                start(job)
                q = qT[0:AUG, h, P * i:P * (i + 1)]
                b0 = 3 * side(job)
                size = width(i) // banks(i)
                for b in range(banks(i)):
                    diag = b == banks(i) - 1
                    mm(ps[:, b0 + b, 0:size], q, kT[0:AUG, h, size * b:size * (b + 1)], start=True, stop=not diag)
                at = META + P * i - size * b
                done(job, mm(ps[:, b0 + b, at:size], identb[:, :], maskb[:, 0:size - at], start=False, stop=True))

            def turn(n, g):
                no = group_no(n, g)
                if g == 0:
                    wait_used(pe, ("S", *heads[n]))
                if no >= 2:
                    pe.wait_ge(pt_out[no % 2], no // 2)
                if n >= ONE_BANK:
                    pe.wait_ge(pt_out[(no - 1) % 2], (no - 1) // 2 + 1)
                for m, j in enumerate(groups(heads[n][0])[g]):
                    at = max(0, META + P * (j - 1))
                    last = nc.tensor.transpose(ps[:, pt_bank(n, no), P * m:P * (m + 1)],
                                               probs[:, n % 2, at:at + P], ident[:, :])
                last.then_inc(pt_made, 1)

            def times_v(n, part, parts):
                i, h = heads[n]
                gs = groups(i)
                if part == 0 and h == 0 and i:
                    pe.wait_ge(o_taken, i)
                blocks = [(g, j) for g, js in enumerate(gs) for j in js]
                for g, j in blocks[len(blocks) * part // parts:len(blocks) * (part + 1) // parts]:
                    no = group_no(n, g)
                    if j == gs[g][0]:
                        pe.wait_ge(pt_out[no % 2], no // 2 + 1)
                    r, t = (META, NT) if j == 0 else (P, j - 1)
                    a = HD * (h % 2)
                    last = mm(ps[a:a + HD, OB, P * (h // 2):P * (h // 2 + 1)], v[0:r, t, HD * h:HD * (h + 1)],
                              pT[0:r, n % 2, P * j:P * (j + 1)], start=(j == 0), stop=(j == i + 1))
                    if j == i + 1:
                        last.then_inc(pv_done, 1)

            def extra(kind, i):
                job = (kind, i)
                start(job)
                b0 = 3 * side(job)
                if kind == "N":
                    pe.wait_ge(l2_ready, i + 1)
                    last = nc.tensor.transpose(ps[0:H, b0, 0:P], l2[:, :], ident[:, :])
                elif kind == "M":
                    pe.wait_ge(asq_ready, i + 1)
                    wait_used(pe, ("N", i))
                    mm(ps[:, b0, :], blockones[:, :], asq[:, :], start=True, stop=False)
                    for c in range(CT):
                        last = mm(ps[:, b0, P * c:P * (c + 1)], sel[:, c, :], l2T[:, :], start=False,
                                  stop=(c == CT - 1))
                elif kind == "W":
                    pe.wait_ge(aT_ready, i + 1)
                    if i == 0:
                        pe.wait_ge(wo_ready, 1)
                        pe.wait_ge(conv_done, CT)
                    for j in range(2):
                        for k in range(KT):
                            lhs = aT[:, k, :] if k < CT else conv[:, k - CT, P * i:P * (i + 1)]
                            last = mm(ps[:, b0 + j, :], lhs, wo[:, k, 512 * j:512 * (j + 1)],
                                      start=(k == 0), stop=(k == KT - 1))
                elif kind == "U":
                    pe.wait_ge(u2_ready, i + 1)
                    for k in range(KT):
                        last = nc.tensor.transpose(buf(job, D)[:, P * k:P * (k + 1)], u2[:, P * k:P * (k + 1)],
                                                   ident[:, :])
                else:
                    wait_used(pe, ("U", i))
                    for k in range(KT):
                        last = mm(ps[0:NG + NE, b0, 0:P], wr[:, k, :], u2T[:, k, :], start=(k == 0),
                                  stop=(k == KT - 1))
                done(job, last)

            pe.wait_ge(consts, 1)
            pe.wait_ge(params, 16 * NPAR)
            for n, t in enumerate(toks):
                turn_x(t, n)
            for t in toks[-2:]:
                wait_used(pe, ("T", t))
            for c in range(CT):
                wait_chunk(c)
                channels("C", c)
                channels("H", c)
                channels("B", c)
                if c:
                    conv_mean(c - 1)
            wait_chunk(CT)
            for n, t in enumerate(toks):
                tokens(("V", t), CT % 3, 2, VC)
                if n == 1:
                    conv_mean(CT - 1)
            job = ("CUM", 0)
            start(job)
            pe.wait_ge(lf_ready, 1)
            mm(ps[:, 3 * side(job), 0:(NT + 1) * H], tri[:, :], lf[:, :, :].rearrange("p t h -> p (t h)"),
               start=True, stop=False)
            done(job, mm(ps[:, 3 * side(job), 0:(NT + 1) * H], ones[:, :],
                         facc[:, :, :].rearrange("p t h -> p (t h)"), start=False, stop=True))
            n_turned = 0
            for job in JOBS:
                if job[0] in ("K", "Q"):
                    if job == ("K", NT):
                        wait_chunk(CT + 1)
                    if job == ("Q", 0):
                        wait_chunk(CT + 2)
                    tokens(job, (CT + 1 if job[0] == "K" else CT + 2) % 3, 1, AW)
                elif job[0] in ("KT", "QT"):
                    turn_heads(job, n_turned)
                    n_turned += 1
            wait_used(pe, ("KT", NT - 1))
            wait_used(pe, ("QT", NT - 1))
            wait_used(pe, ("QT", NT - 2))
            pe.wait_ge(consts, 2)
            for n in range(NH + 2):
                if n < NH:
                    if n == ONE_BANK + 1:
                        no = group_no(n - 2, len(groups(heads[n - 2][0])) - 1)
                        for m in (no - 1, no):
                            pe.wait_ge(pt_out[m % 2], m // 2 + 1)
                    scores(n)
                parts = len(groups(heads[n - 1][0])) if 1 <= n <= NH else 1
                for g in range(parts):
                    if 1 <= n <= NH:
                        turn(n - 1, g)
                    if n >= 2:
                        times_v(n - 2, g, parts)
                if n < NH and heads[n][0] and heads[n][1] in EXTRA:
                    extra(EXTRA[heads[n][1]], heads[n][0] - 1)
            for kind in ("N", "M", "W", "U", "L"):
                extra(kind, NT - 1)
            job = ("LT", 0)
            start(job)
            for t in (NT - 2, NT - 1):
                wait_used(pe, ("L", t))
            for t in range(NT):
                last = nc.tensor.transpose(ps[:, 3 * side(job), (NG + NE) * t:(NG + NE) * (t + 1)],
                                           lT[0:NG + NE, P * t:P * (t + 1)], ident[0:NG + NE, 0:NG + NE])
            done(job, last)
            job = ("RANK", 0)
            start(job)
            pe.wait_ge(gate_ask, 2)
            b0 = 3 * side(job)
            mm(ps[:, b0, 0:NT * NE], tris[:, :], both[:, :, :].rearrange("p t e -> p (t e)"), start=True, stop=False)
            mm(ps[:, b0, 0:NT * NE], ones[:, :], prev[:, 0:NT, :].rearrange("p t e -> p (t e)"),
               start=False, stop=True)
            done(job, mm(ps[:, b0, NT * NE:(NT + 1) * NE], ones[:, :], prev[:, NT, :], start=True, stop=True))
            job = ("TABLE", 0)
            start(job)
            pe.wait_ge(gate_ask, 3)
            for m in range(2 * NT):
                last = mm(ps[:, 3 * side(job), 0:COLS], rowhot[:, m, :], colhot[:, m, :],
                          start=(m == 0), stop=(m == 2 * NT - 1))
            done(job, last)
            pe.wait_ge(route_ready, 1)
            nb = pe.value_load(nblocks[0:1, 0:1], min_val=NE, max_val=NE + MAX_OVER)
            with pe.Fori(0, nb, 2) as i:
                for s in range(2):
                    pair = i // 2 + 1
                    pe.wait_ge(xg_in[s], 16 * pair)
                    for k in range(KT):
                        last = nc.tensor.transpose(big[:, P * k:P * (k + 1)], xg[:, s, P * k:P * (k + 1)], ident[:, :])
                    last.then_inc(x_turned, 1)
                    pe.wait_ge(wg_in[s], 16 * pair)
                    pe.wait_ge(xT_dve, i + s + 1)
                    pe.wait_ge(xT_act, i + s + 1)
                    for k in range(KT):
                        last = mm(ps[:, 2, :], xT[:, k, :], wg[:, s, k, :], start=(k == 0), stop=(k == KT - 1))
                    last.then_inc(g_done, 1)
                    pe.wait_ge(wu_in[s], 16 * pair)
                    for k in range(KT):
                        last = mm(ps[:, 3, :], xT[:, k, :], wu[:, s, k, :], start=(k == 0), stop=(k == KT - 1))
                    last.then_inc(u_done, 1)
                    pe.wait_ge(hid_ready, i + s + 1)
                    for k in range(FT):
                        last = nc.tensor.transpose(ps[:, 4, P * k:P * (k + 1)], hid[:, P * k:P * (k + 1)], ident[:, :])
                    last.then_inc(hid_turned, 1)
                    pe.wait_ge(wd_in[s], 16 * pair)
                    pe.wait_ge(hidT_ready, i + s + 1)
                    pe.wait_ge(yb_dve, i + s + 1)
                    pe.wait_ge(yb_act, i + s + 1)
                    for j in range(2):
                        for k in range(FT):
                            last = mm(ps[:, 5 + j, :], hidT[:, k, :], wd[:, s, k, 512 * j:512 * (j + 1)],
                                      start=(k == 0), stop=(k == FT - 1))
                    last.then_inc(y_done[s], 1)

        @block.scalar
        def _(act):
            count = [0]
            A = nc.scalar.activation

            def then(ins):
                count[0] += 1
                ins.then_inc(act_step, 1)
                act.wait_ge(act_step, count[0])

            def inv_root(dst, src, scale):
                then(A(dst, src, ACT.Ln, bias=eps_b[0:dst.shape[0], :], scale=scale))
                return A(dst, dst, ACT.Exp, scale=-0.5)

            nc.scalar.preload_act_table_set("natural_log_exp_and_others")
            act.wait_ge(consts, 1)
            for n, t in enumerate(toks):
                r = rows(t)
                act.wait_ge(x_in[n % 2], 16 * (n // 2 + 1))
                if n >= 2:
                    act.wait_ge(hn_ready, n - 1)
                then(A(sqj[0:r, :], xin[0:r, n % 2, :], ACT.Square, accum_out=ms[0:r, n % 2:n % 2 + 1]))
                inv_root(ms[0:r, n % 2:n % 2 + 1], ms[0:r, n % 2:n % 2 + 1], 1.0 / D).then_inc(rs_ready, 1)

            def conv_root(c):
                wait_made(act, ("R", c))
                if c:
                    act.wait_ge(conv_done, c)
                count[0] += 1
                A(rsb[:, :], buf(("R", c), T), ACT.Ln, bias=eps_b[:, :]).then_inc(used[side(("R", c))], 1)
                wait_used(act, ("R", c))
                count[0] -= 1
                A(rsb[:, :], rsb[:, :], ACT.Exp, scale=-0.5).then_inc(rsb_ready, 1)

            for c in range(CT):
                job = ("C", c)
                wait_made(act, job)
                if c:
                    wait_used(act, ("H", c - 1))
                b0 = 3 * side(job)
                A(csb[:, :].rearrange("p (j n) -> p j n", j=3), ps[:, b0:b0 + 3, 0:(T + 2) // 3],
                  ACT.Copy).then_inc(used[side(job)], 1)
                wait_used(act, ("B", c))
                if c:
                    wait_made(act, ("R", c - 1))
                    conv_root(c - 1)
                A(ysq[:, :], conv[:, c, :], ACT.Square).then_inc(ysq_ready, 1)
            for n, t in enumerate(toks):
                job, r = ("V", t), rows(t)
                wait_made(act, job)
                b0 = 3 * side(job)
                A(v[0:r, t, 0:VC], ps[0:r, b0, 0:VC], ACT.Copy)
                A(v[0:r, t, VC:], ps[0:r, b0 + 1, 0:AW - VC], ACT.Copy)
                A(fz[0:r, t, :], ps[0:r, b0 + 1, AW - VC:VC], ACT.Copy).then_inc(used[side(job)], 1)
                if n == 1:
                    conv_root(CT - 1)
            act.wait_ge(f_ready, 1)
            then(A(fe[:, :, :], fe[:, :, :], ACT.Exp, scale=-1.0))
            A(fe[:, :, :], fe[:, :, :], ACT.Ln, bias=one_b[:, :]).then_inc(fe_ready, 1)

            n = 0
            for job in JOBS:
                kind, t = job[0], job[1]
                if kind in ("K", "Q"):
                    r = rows(t)
                    wait_made(act, job)
                    if n:
                        act.wait_ge(ss_ready, n)
                    A(sq[0:r, :], ps[0:r, 3 * side(job), :], ACT.Square).then_inc(sq_ready, 1)
                    act.wait_ge(ss_ready, n + 1)
                    inv_root(stat[0:r, n % 2, :], stat[0:r, n % 2, :], 1.0 / HD).then_inc(rk_ready, 1)
                    n += 1
                elif kind in ("KT", "QT"):
                    r = rows(t)
                    wait_made(act, job)
                    if job == ("KT", NT):
                        act.wait_ge(conv_done, CT)
                    dst = kT[0:AUG, :, slice(*u_cols(t))] if kind == "KT" else qT[0:AUG, :, P * t:P * (t + 1)]
                    A(dst, buf(job, H * P)[0:AUG, :].rearrange("p (h n) -> p h n", h=H)[:, :, 0:r],
                      ACT.Copy).then_inc(used[side(job)], 1)

            def evict(n):
                for g, js in enumerate(groups(heads[n][0])):
                    no = group_no(n, g)
                    if no % 2:
                        act.wait_ge(pt_made, no + 1)
                        if n >= 2:
                            act.wait_ge(pv_done, n - 1)
                        A(pT[:, n % 2, P * js[0]:P * (js[-1] + 1)], ps[:, pt_bank(n, no), 0:P * len(js)],
                          ACT.Copy).then_inc(pt_out[1], 1)

            def extra(kind, i):
                if kind == "ASQ":
                    act.wait_ge(o_taken, i + 1)
                    if i:
                        wait_made(act, ("M", i - 1))
                    A(asq[:, :], ot[:, :], ACT.Square).then_inc(asq_ready, 1)
                elif kind == "ARS":
                    job = ("M", i)
                    wait_made(act, job)
                    if i:
                        act.wait_ge(aT_ready, i)
                    A(rsa[:, :], ps[:, 3 * side(job), :], ACT.Ln).then_inc(used[side(job)], 1)
                    wait_used(act, job)
                    A(rsa[:, :], rsa[:, :], ACT.Exp, scale=-0.5).then_inc(rsa_ready, 1)
                elif kind == "URS":
                    wait_used(act, ("W", i))
                    then(A(u2sq[:, :], h1b[:, :], ACT.Square, accum_out=ms[:, 2:3]))
                    inv_root(ms[:, 2:3], ms[:, 2:3], 1.0 / D).then_inc(u2rs_ready, 1)
                else:
                    job = ("U", i)
                    wait_made(act, job)
                    if i:
                        wait_made(act, ("L", i - 1))
                    A(u2T[:, :, :].rearrange("p k n -> p (k n)"), buf(job, D), ACT.Copy).then_inc(used[side(job)], 1)

            extras = {1: "ASQ", 3: "ARS", 5: "URS", 6: "U"}
            for n, (i, h) in enumerate(heads):
                if n:
                    evict(n - 1)
                act.wait_ge(max_ready, n + 1)
                if n >= 2:
                    last = len(groups(heads[n - 2][0])) - 1
                    act.wait_ge(pt_made, group_no(n - 2, last) + 1)
                job = ("S", i, h)
                A(probs[:, n % 2, 0:width(i)].rearrange("p (b n) -> p b n", b=banks(i)),
                  score_buf(i, h), ACT.Exp, bias=negmax[:, n % 2:n % 2 + 1],
                  accum_out=rowsum[:, i % 2, h:h + 1]).then_inc(used[side(job)], 1)
                if i and h in extras:
                    extra(extras[h], i - 1)
            evict(NH - 1)
            for kind in ("ASQ", "ARS", "URS", "U"):
                extra(kind, NT - 1)
            act.wait_ge(gate_ask, 1)
            A(r4[0][:, :, :], r4[0][:, :, :], ACT.Exp)
            A(r8[0][:, 0, :], r8[0][:, 0, :], ACT.Exp).then_inc(gate_exp, 1)
            act.wait_ge(route_ready, 1)
            nc.scalar.sem_inc(yb_act, 1)
            nb = act.value_load(nblocks[0:1, 0:1], min_val=NE, max_val=NE + MAX_OVER)
            with act.Fori(0, nb, 2) as i:
                for s in range(2):
                    act.wait_ge(x_turned, i + s + 1)
                    A(xT[:, KT // 2:, :].rearrange("p k n -> p (k n)"), ps[:, 1, :], ACT.Copy).then_inc(xT_act, 1)
                    act.wait_ge(g_done, i + s + 1)
                    A(sil[:, :], ps[:, 2, :], ACT.Silu).then_inc(sil_ready, 1)
                    act.wait_ge(hid_turned, i + s + 1)
                    A(hidT[:, :, :].rearrange("p k n -> p (k n)"), ps[:, 4, :], ACT.Copy).then_inc(hidT_ready, 1)
                    act.wait_ge(y_done[s], i // 2 + 1)
                    act.wait_ge(yb_free, i + s + 1)
                    A(yb[:, s, 512:], ps[:, 6, :], ACT.Copy).then_inc(yb_act, 1)
            for t in range(NT):
                act.wait_ge(fin_ready, t + 1)
                act.dma_start(out[P * t:P * (t + 1), :], h1t[:, t % 2, :]).then_inc(fin_out[t % 2], 16)
            for s in range(2):
                act.wait_ge(fin_out[s], 16 * (NT // 2))

        @block.vector
        def _(dve):
            count = [0]
            V = nc.vector

            def then(ins):
                count[0] += 1
                ins.then_inc(dve_step, 1)
                dve.wait_ge(dve_step, count[0])

            def bc(ap, shape):
                return ap.unsqueeze(2).broadcast_to(shape)

            dve.wait_ge(consts, 1)
            dve.wait_ge(params, 16 * NPAR)

            dve.wait_ge(gmix_in, 16)

            def take_turned(t):
                job, r = ("T", t), rows(t)
                wait_made(dve, job)
                a, b = u_cols(t)
                V.tensor_tensor(uT[:, :, a:b], buf(job, KT * P).rearrange("p (k n) -> p k n", k=KT)[:, :, 0:r],
                                bc(gmixT[:, :], [P, KT, r]), ALU.mult).then_inc(used[side(job)], 1)

            for n, t in enumerate(toks):
                r = rows(t)
                dve.wait_ge(rs_ready, n + 1)
                if n >= 2:
                    wait_made(dve, ("T", toks[n - 2]))
                V.tensor_scalar(hn[0:r, n % 2, :], xin[0:r, n % 2, :], ms[0:r, n % 2:n % 2 + 1], None,
                                ALU.mult).then_inc(hn_ready, 1)
                if n:
                    take_turned(toks[n - 1])
            take_turned(toks[-1])
            then(V.tensor_scalar(gqk_b[:, 0, :], gqk_b[:, 0, :], HD ** -0.5, None, ALU.mult))
            then(V.tensor_tensor(gqk_b[:, 0, :], gqk_b[:, 0, :], gqk_b[:, 1, :], ALU.mult))

            def conv_norm(c):
                dve.wait_ge(rsb_ready, c + 1)
                V.scalar_tensor_tensor(conv[:, c, :], conv[:, c, :], gconvT[:, c:c + 1], rsb[:, :],
                                       ALU.mult, ALU.mult).then_inc(conv_done, 1)

            for c in range(CT):
                job = ("H", c)
                wait_made(dve, job)
                wait_used(dve, ("C", c))
                b0 = 3 * side(job)
                V.tensor_tensor(uc[:, :].rearrange("p (j n) -> p j n", j=3), ps[:, b0:b0 + 3, 0:(T + 2) // 3],
                                csb[:, :].rearrange("p (j n) -> p j n", j=3), ALU.mult).then_inc(used[side(job)], 1)
                wait_used(dve, job)
                y = conv[:, c, :]
                then(V.tensor_scalar(y, uc[:, 0:T], convwT[:, 0, c:c + 1], None, ALU.mult))
                for n in (1, 2):
                    then(V.scalar_tensor_tensor(y, uc[:, n:n + T], convwT[:, n, c:c + 1], y, ALU.mult, ALU.add))
                job = ("B", c)
                wait_made(dve, job)
                V.tensor_tensor(y, y, buf(job, T), ALU.mult).then_inc(used[side(job)], 1)
                if c:
                    conv_norm(c - 1)
            conv_norm(CT - 1)
            for t in toks[-2:]:
                wait_used(dve, ("V", t))
            then(V.tensor_tensor(fz[:, :, :], fz[:, :, :], bf_b[:, :].unsqueeze(1).broadcast_to([P, NT + 1, H]),
                                 ALU.add))
            V.scalar_tensor_tensor(fe[:, :, :], fz[:, :, :], -1.0, fz[:, :, :], ALU.mult, ALU.max).then_inc(f_ready, 1)
            dve.wait_ge(fe_ready, 1)
            for r, a, b in ((P, 0, NT), (META, NT, NT + 1)):
                ins = V.scalar_tensor_tensor(lf[0:r, a:b, :], fz[0:r, a:b, :], 0.0, fe[0:r, a:b, :],
                                             ALU.min, ALU.subtract)
            then(ins)
            V.memset(facc[:, NT, :], 0.0)
            then(V.tensor_copy(facc[:, 0, :], lf[:, NT, :]))
            for t in range(1, NT):
                ins = V.tensor_tensor(facc[:, t, :], facc[:, t - 1, :], lf[:, t - 1, :], ALU.add)
                if t < NT - 1:
                    then(ins)
            ins.then_inc(lf_ready, 1)
            job = ("CUM", 0)
            wait_made(dve, job)
            V.tensor_copy(cum[:, :, :].rearrange("p t h -> p (t h)"),
                          buf(job, (NT + 1) * H)).then_inc(used[side(job)], 1)
            wait_used(dve, job)

            n = 0
            turns = ["KT"] * (NT + 1) + ["QT"] * NT
            for kind, t in [j for j in JOBS if j[0] in ("K", "Q")]:
                job, r = (kind, t), rows(t)
                dve.wait_ge(sq_ready, n + 1)
                if n >= 2:
                    dve.wait_ge(rk_ready, n - 1)
                V.tensor_reduce(stat[0:r, n % 2, :], sq[0:r, :].rearrange("p (h d) -> p h d", h=H), AX.X,
                                ALU.add).then_inc(ss_ready, 1)
                at = toks.index(t) if kind == "K" else t
                dst = (kn if kind == "K" else qn)[0:r, at % 2, :, :]
                if at >= 2:
                    wait_made(dve, ("KT", toks[at - 2]) if kind == "K" else ("QT", at - 2))
                if kind == "K":
                    V.tensor_scalar(dst[:, :, HD], cum[0:r, t, :], -1.0, None, ALU.mult)
                else:
                    V.tensor_copy(dst[:, :, HD + 1], cum[0:r, t, :])
                dve.wait_ge(rk_ready, n + 1)
                src = ps[0:r, 3 * side(job), :].rearrange("p (h d) -> p h d", h=H)
                V.tensor_tensor(dst[:, :, 0:HD], src, bc(stat[0:r, n % 2, :], [r, H, HD]),
                                ALU.mult).then_inc(used[side(job)], 1)
                wait_used(dve, job)
                if kind == "Q":
                    V.tensor_tensor(dst[:, :, 0:HD], dst[:, :, 0:HD],
                                    gqk_b[:, 0, :].unsqueeze(1).broadcast_to([P, H, HD]),
                                    ALU.mult).then_inc(kn_ready, 1)
                else:
                    dve.sem_inc(kn_ready, 1)
                n += 1

            def extra(kind, i):
                if kind == "O":
                    dve.wait_ge(pv_done, H * (i + 1))
                    if i:
                        dve.wait_ge(aT_ready, i)
                    V.tensor_copy(ot[:, :], ps[:, OB, :]).then_inc(o_taken, 1)
                    V.tensor_tensor(l2[:, :], rowsum[:, i % 2, :], rowsum[:, i % 2, :],
                                    ALU.mult).then_inc(l2_ready, 1)
                elif kind == "N":
                    job = ("N", i)
                    wait_made(dve, job)
                    V.tensor_copy(l2T[:, :], ps[0:H, 3 * side(job), 0:P]).then_inc(used[side(job)], 1)
                elif kind == "M":
                    dve.wait_ge(rsa_ready, i + 1)
                    if i:
                        wait_made(dve, ("W", i - 1))
                    V.tensor_tensor(aT[:, :, :].rearrange("p k n -> p (k n)"), ot[:, :], rsa[:, :],
                                    ALU.mult).then_inc(aT_ready, 1)
                elif kind == "W":
                    job = ("W", i)
                    wait_made(dve, job)
                    dve.wait_ge(xr_in, 16 * (i + 1))
                    if i:
                        dve.wait_ge(h1_out, 16 * i)
                    V.tensor_tensor(h1b[:, :], buf(job, D), xr[:, :], ALU.add).then_inc(used[side(job)], 1)
                elif kind == "U2":
                    dve.wait_ge(u2rs_ready, i + 1)
                    if i:
                        dve.wait_ge(rows_out, 16 * i)
                        wait_made(dve, ("U", i - 1))
                    V.scalar_tensor_tensor(u2[:, :], h1b[:, :], ms[:, 2:3], gffn_b[:, :], ALU.mult,
                                           ALU.mult).then_inc(u2_ready, 1)
                else:
                    job = ("L", i)
                    wait_made(dve, job)
                    V.tensor_scalar(lT[0:NG + NE, P * i:P * (i + 1)], ps[0:NG + NE, 3 * side(job), 0:P],
                                    br_c[:, :], None, ALU.add).then_inc(used[side(job)], 1)

            def evict(n):
                for g, js in enumerate(groups(heads[n][0])):
                    no = group_no(n, g)
                    if no % 2 == 0:
                        dve.wait_ge(pt_made, no + 1)
                        if n >= 2:
                            dve.wait_ge(pv_done, n - 1)
                        V.tensor_copy(pT[:, n % 2, P * js[0]:P * (js[-1] + 1)],
                                      ps[:, pt_bank(n, no), 0:P * len(js)]).then_inc(pt_out[0], 1)

            extras = {1: ("O",), 2: ("N",), 3: ("M",), 4: ("W",), 5: ("U2",), 7: ("L",)}
            dve.wait_ge(wo_in, 32)
            for k in range(CT):
                ins = V.tensor_scalar(wo[:, k, :], wo[:, k, :], gattnT[:, k:k + 1], None, ALU.mult)
            ins.then_inc(wo_ready, 1)
            for n, (i, h) in enumerate(heads):
                job = ("S", i, h)
                wait_made(dve, job)
                if n >= 2:
                    wait_used(dve, ("S", *heads[n - 2]))
                V.tensor_reduce(negmax[:, n % 2:n % 2 + 1], score_buf(i, h), AX.XY, ALU.max,
                                negate=True).then_inc(max_ready, 1)
                if n:
                    evict(n - 1)
                if i and h in extras:
                    for kind in extras[h]:
                        extra(kind, i - 1)
            evict(NH - 1)
            for kind in ("O", "N", "M", "W", "U2", "L"):
                extra(kind, NT - 1)

            job = ("LT", 0)
            wait_made(dve, job)
            V.tensor_copy(logits[:, :, :].rearrange("p t g -> p (t g)"),
                          buf(job, NT * (NG + NE))).then_inc(used[side(job)], 1)
            wait_used(dve, job)
            gl, e_l = logits[:, :, 0:NG], logits[:, :, NG:]
            gmax, gidx = r8[1][:, 0, :], r8[1][:, 1, :]
            iota_g = iota128[:, 0:NG].unsqueeze(1).broadcast_to([P, NT, NG])
            iota_e = iota128[:, 0:NE].unsqueeze(1).broadcast_to([P, NT, NE])

            def first_max(dst_max, dst_idx, src, scratch, iota, n):
                then(V.tensor_reduce(dst_max, src, AX.X, ALU.max))
                then(V.tensor_tensor(scratch, src, bc(dst_max, [P, NT, n]), ALU.is_equal))
                then(V.scalar_tensor_tensor(scratch, scratch, -100.0, iota, ALU.mult, ALU.add))
                then(V.tensor_reduce(dst_idx, scratch, AX.X, ALU.min))
                then(V.tensor_scalar(dst_idx, dst_idx, 100.0, None, ALU.add))

            first_max(gmax, gidx, gl, r4[0][:, :, :], iota_g, NG)
            then(V.tensor_tensor(r4[1][:, :, :], iota_g, bc(gidx, [P, NT, NG]), ALU.is_equal))
            oh = r4[1][:, :, :].rearrange("p t g -> p (t g)").unsqueeze(2).broadcast_to([P, NT * NG, EG])
            e4 = et[:, :, :].rearrange("p t (g e) -> p (t g) e", g=NG)
            then(V.tensor_copy(e4, oh))
            then(V.tensor_tensor(el[:, :, :], e_l, et[:, :, :], ALU.mult))
            then(V.tensor_scalar(et[:, :, :], et[:, :, :], 1.0, -NEG, ALU.subtract, ALU.mult))
            then(V.tensor_tensor(el[:, :, :], el[:, :, :], et[:, :, :], ALU.add))
            m0, x0 = r8[2][:, 0, :], r8[3][:, 0, :]
            m1, x1 = r8[2][:, 1, :], r8[3][:, 1, :]
            first_max(m0, x0, el[:, :, :], et[:, :, :], iota_e, NE)
            then(V.tensor_tensor(one0[:, :, :], iota_e, bc(x0, [P, NT, NE]), ALU.is_equal))
            then(V.scalar_tensor_tensor(el[:, :, :], one0[:, :, :], 2 * NEG, el[:, :, :], ALU.mult, ALU.add))
            first_max(m1, x1, el[:, :, :], et[:, :, :], iota_e, NE)
            then(V.tensor_tensor(one1[:, :, :], iota_e, bc(x1, [P, NT, NE]), ALU.is_equal))
            then(V.tensor_tensor(r8[0][:, 0, :], m1, m0, ALU.subtract))
            V.tensor_tensor(r4[0][:, :, :], gl, bc(gmax, [P, NT, NG]), ALU.subtract).then_inc(gate_ask, 1)
            then(V.tensor_tensor(both[:, :, :], one0[:, :, :], one1[:, :, :], ALU.add))
            then(V.memset(prev[:, 0, :], 0.0))
            for t in range(1, NT + 1):
                ins = V.tensor_tensor(prev[:, t, :], prev[:, t - 1, :], both[:, t - 1, :], ALU.add)
                if t < NT:
                    then(ins)
            ins.then_inc(gate_ask, 1)
            dve.wait_ge(gate_exp, 1)
            then(V.tensor_reduce(r8[4][:, 0, :], r4[0][:, :, :], AX.X, ALU.add))
            then(V.tensor_scalar(r8[4][:, 1, :], r8[0][:, 0, :], 1.0, None, ALU.add))
            then(V.tensor_tensor(r8[4][:, 0, :], r8[4][:, 0, :], r8[4][:, 1, :], ALU.mult))
            then(V.reciprocal(gates[:, 0, :], r8[4][:, 0, :]))
            then(V.tensor_tensor(gates[:, 1, :], gates[:, 0, :], r8[0][:, 0, :], ALU.mult))
            job = ("RANK", 0)
            wait_made(dve, job)
            b0 = 3 * side(job)
            V.tensor_copy(cnt[:, :], ps[:, b0, NT * NE:(NT + 1) * NE])
            V.tensor_copy(ranks[:, :, :].rearrange("p t e -> p (t e)"), ps[:, b0, 0:NT * NE]).then_inc(used[side(job)], 1)
            wait_used(dve, job)
            rank, jblk, row, col, ovs, gt0 = (r8[n][:, :, :] for n in (4, 5, 6, 7, 8, 9))
            for k, one in ((0, one0), (1, one1)):
                then(V.tensor_tensor(et[:, :, :], one[:, :, :], ranks[:, :, :], ALU.mult))
                then(V.tensor_reduce(rank[:, k, :], et[:, :, :], AX.X, ALU.add))
            lim = t256[:, 0, 0:7]
            then(V.tensor_scalar(lim, iota128[:, 1:8], float(P), None, ALU.mult))
            c7 = cmp7[:, :, 0:7]
            then(V.tensor_tensor(c7, bc(cnt[:, :], [P, NE, 7]), lim.unsqueeze(1).broadcast_to([P, NE, 7]), ALU.is_gt))
            then(V.tensor_reduce(nover[:, :], c7, AX.X, ALU.add))
            then(V.tensor_copy(over[:, 0, :], nover[:, :]))
            cur = 0
            for d in (1, 2, 4, 8, 16):
                then(V.tensor_copy(over[:, 1 - cur, 0:d], over[:, cur, 0:d]))
                then(V.tensor_tensor(over[:, 1 - cur, d:], over[:, cur, d:], over[:, cur, 0:NE - d], ALU.add))
                cur = 1 - cur
            end = over[:, cur, :]
            begin = over[:, 1 - cur, :]
            NX = COLS - NE
            then(V.tensor_tensor(bcmp[:, 0:NX, :], end.unsqueeze(1).broadcast_to([P, NX, NE]),
                                 bc(iota128[:, 0:NX], [P, NX, NE]), ALU.is_le))
            then(V.tensor_reduce(tabf[0][:, 0:NX], bcmp[:, 0:NX, :], AX.X, ALU.add))
            V.tensor_scalar(bexp[:, NE:], tabf[0][:, 0:NX], float(NE - 1), None, ALU.min)
            V.tensor_copy(bexp[:, 0:NE], iota128[:, 0:NE])
            V.tensor_scalar(nblocks[:, :], end[:, NE - 1:NE], float(NE), None, ALU.add)
            then(V.tensor_tensor(begin, end, nover[:, :], ALU.subtract))
            for k, one in ((0, one0), (1, one1)):
                then(V.tensor_tensor(et[:, :, :], one[:, :, :], begin.unsqueeze(1).broadcast_to([P, NT, NE]), ALU.mult))
                then(V.tensor_reduce(ovs[:, k, :], et[:, :, :], AX.X, ALU.add))
            lim1 = lim.unsqueeze(1).broadcast_to([P, 16, 7])
            c16 = t256[:, :, 8:15]
            flat = r8[4][:, :, :].rearrange("p k t -> p (k t)")
            then(V.tensor_tensor(c16, bc(flat, [P, 16, 7]), lim1, ALU.is_ge))
            then(V.tensor_reduce(r8[5][:, :, :].rearrange("p k t -> p (k t)"), c16, AX.X, ALU.add))
            then(V.scalar_tensor_tensor(row, jblk, -float(P), rank, ALU.mult, ALU.add))
            then(V.tensor_scalar(gt0, jblk, 0.0, None, ALU.is_gt))
            then(V.scalar_tensor_tensor(col, jblk, float(NE - 1), ovs, ALU.add, ALU.add))
            then(V.tensor_tensor(col, col, r8[3][:, :, :], ALU.subtract))
            then(V.tensor_tensor(col, col, gt0, ALU.mult))
            then(V.tensor_tensor(col, col, r8[3][:, :, :], ALU.add))
            code = r8[0][:, :, :]
            V.tensor_copy(code[:, 0, :], tokcode[:, :])
            then(V.tensor_scalar(code[:, 1, :], tokcode[:, :], float(T), None, ALU.add))
            for k in range(2):
                for t in range(NT):
                    m = NT * k + t
                    V.tensor_scalar(rowhot[:, m, :], iota128[:, :], row[:, k, t:t + 1], None, ALU.is_equal)
                    ins = V.tensor_scalar(colhot[:, m, :], iota128[:, 0:COLS], col[:, k, t:t + 1],
                                          code[:, k, t:t + 1], ALU.is_equal, ALU.mult)
            ins.then_inc(gate_ask, 1)
            job = ("TABLE", 0)
            wait_made(dve, job)
            c, pad, hi = (tabf[n][:, :] for n in range(3))
            V.tensor_copy(c, buf(job, COLS)).then_inc(used[side(job)], 1)
            wait_used(dve, job)
            then(V.tensor_scalar(pad, c, 0.5, float(NOWHERE), ALU.is_lt, ALU.mult))
            then(V.scalar_tensor_tensor(pad, c, -1.0, pad, ALU.add, ALU.add))
            V.tensor_copy(stab[:, :], pad)
            then(V.tensor_scalar(hi, c, T + 0.5, -float(T), ALU.is_gt, ALU.mult))
            V.tensor_tensor(gtab[:, :], pad, hi, ALU.add).then_inc(route_ready, 1)

            dve.wait_ge(route_ready, 1)
            dve.sem_inc(yb_dve, 1)
            nb = dve.value_load(nblocks[0:1, 0:1], min_val=NE, max_val=NE + MAX_OVER)
            with dve.Fori(0, nb, 2) as i:
                for s in range(2):
                    dve.wait_ge(x_turned, i + s + 1)
                    V.tensor_copy(xT[:, 0:KT // 2, :].rearrange("p k n -> p (k n)"), ps[:, 0, :]).then_inc(xT_dve, 1)
                    dve.wait_ge(sil_ready, i + s + 1)
                    dve.wait_ge(u_done, i + s + 1)
                    V.tensor_tensor(hid[:, :], sil[:, :], ps[:, 3, :], ALU.mult).then_inc(hid_ready, 1)
                    dve.wait_ge(y_done[s], i // 2 + 1)
                    dve.wait_ge(yb_free, i + s + 1)
                    V.tensor_copy(yb[:, s, 0:512], ps[:, 5, :]).then_inc(yb_dve, 1)

            for t in range(NT):
                s = t % 2
                dve.wait_ge(y_in[s], 48 * (t // 2 + 1))
                then(V.scalar_tensor_tensor(h1t[:, s, :], y0[:, s, :], gates[:, 0, t:t + 1], h1t[:, s, :],
                                            ALU.mult, ALU.add))
                V.scalar_tensor_tensor(h1t[:, s, :], y1[:, s, :], gates[:, 1, t:t + 1], h1t[:, s, :],
                                       ALU.mult, ALU.add).then_inc(fin_ready, 1)


_ORDER = ["x", "meta_tokens", "norm_mix_g", "w_in", "b_forget", "q_norm_g", "k_norm_g", "conv_w", "attn_out_g",
          "conv_out_g", "w_out", "norm_ffn_g", "w_router_group", "b_router_group", "w_router_expert",
          "b_router_expert", "w_gate", "w_up", "w_down"]


def kernel(**inputs):
    import numpy as _np
    import concourse.bacc as _bacc
    from concourse import mybir as _mybir
    from concourse.bass_utils import run_bass_kernel_spmd as _run

    nc = _bacc.Bacc("TRN2", target_bir_lowering=False, num_devices=1)
    arrays, args = {}, []
    for name in _ORDER:
        a = _np.ascontiguousarray(inputs[name])
        if name != "meta_tokens":
            a = a[0]
        arrays[f"in_{name}"] = a
        args.append(nc.dram_tensor(f"in_{name}", a.shape, _mybir.dt.from_np(a.dtype), kind="ExternalInput").ap())
    args.append(nc.dram_tensor("out_0", (T, D), F32, kind="ExternalOutput").ap())
    build(nc, *args)
    r = _run(nc, [arrays], core_ids=[0])
    return r.results[0]["out_0"].reshape(1, T, D)
```

```python
import concourse.bass as bass
from concourse import mybir
from contextlib import ExitStack

F32 = mybir.dt.float32
BF16 = mybir.dt.bfloat16
I32 = mybir.dt.int32
U32 = mybir.dt.uint32
F32R = mybir.dt.float32r
ALU = mybir.AluOpType
ACT = mybir.ActivationFunctionType
AX = mybir.AxisListType

P = 128
D = 1024
KT = D // P
T = 1024
NT = T // P
META = 16
KEYS = T + META
KPAD = KEYS + META
H = 8
HD = 64
AW = H * HD
CW = D - AW
CT = CW // P
AUG = HD + 2
NG = 4
NE = 32
EG = NE // NG
F = 512
FT = F // P
EPS = 1e-6
NEG = -1e30
MAX_OVER = 2 * T // P - 1
COLS = NE + MAX_OVER + 7
NOWHERE = 1 << 20

VC = (AW + H) // 2
HH = H // 2

COL_V = 2 * AW
COL_B = 3 * AW + H
COL_C, COL_H = COL_B + CW, COL_B + 2 * CW

BASE = 16512


class Plan:

    def __init__(self, nc, at, end):
        self.nc, self.at, self.end = nc, at, end

    def __call__(self, name, shape, dt=F32):
        n = 1
        for s in shape[1:]:
            n *= s
        size = n * (2 if dt == BF16 else 4)
        t = self.nc.alloc_sbuf_tensor_at(name, list(shape), dt, offset=self.at)
        self.at += -(-size // 32) * 32
        assert self.at <= self.end, (name, self.at, self.end)
        return t


EXTRA = {2: "N", 3: "M", 4: "W", 6: "U", 7: "L"}


def ring_jobs():
    jobs = [("T", NT)] + [("T", t) for t in range(NT)]
    for c in range(CT):
        jobs += [("C", c), ("H", c), ("B", c)]
        if c:
            jobs.append(("R", c - 1))
    toks = [NT] + list(range(NT))
    jobs += [("V", NT, 1), ("V", 0, 1), ("R", CT - 1)] + [("V", t, 1) for t in range(1, NT)]
    jobs += [("Z", t, part) for part in range(2) for t in range(NT)]
    jobs += [("V", t, 0) for t in toks]
    jobs.append(("CUM", 0))
    jobs += [("K", t, part) for part in range(2) for t in toks]
    jobs += [("Q", t, part) for part in range(2) for t in range(NT)]
    for i in range(NT):
        for h in range(H):
            jobs.append(("S", i, h))
            if i and h in EXTRA:
                jobs.append((EXTRA[h], i - 1))
    jobs += [(k, NT - 1) for k in ("N", "M", "W", "U", "L")]
    jobs += [("LT", 0), ("RANK", 0), ("TABLE", 0)]
    return jobs


JOBS = ring_jobs()
TURN = {job: n for n, job in enumerate(JOBS)}


def side(job):
    return TURN[job] % 2


def uses(job):
    return TURN[job] // 2 + 1


def groups(i):
    blocks = list(range(i + 2))
    n = -(-len(blocks) // 4)
    if n == 1 and len(blocks) > 2:
        n = 2
    cuts = [len(blocks) * g // n for g in range(n + 1)]
    return [blocks[a:b] for a, b in zip(cuts, cuts[1:])]


GROUPS = {}
for _i in range(NT):
    for _h in range(H):
        for _g in range(len(groups(_i))):
            GROUPS[(_i, _h, _g)] = len(GROUPS)


def build(nc, x, meta, g_mix, w_in, b_forget, gq, gk, conv_w, g_attn, g_conv, w_out, g_ffn,
          w_rg, b_rg, w_re, b_re, w_gate, w_up, w_down, out):
    ctx = ExitStack()
    with ctx:
        def sem(name):
            return ctx.enter_context(nc.semaphore(name))

        top = BASE + 212800
        small = Plan(nc, BASE, BASE + 20000)
        ident = small("ident", [P, P])
        identb = small("identb", [P, P], BF16)
        maskb = small("maskb", [P, P + META], BF16)
        tri = small("tri", [P, P])
        tris = small("tris", [P, P])
        ones = small("ones", [P, P])
        blockones = small("blockones", [P, P])
        iota128 = small("iota128", [P, P])
        ones64 = small("ones64", [P, P], F32R)
        selr = small("selr", [H, CT, P], F32R)
        l2 = small("l2", [P, H])
        l2Th = small("l2Th", [H, P], F32R)
        l2Tl = small("l2Tl", [H, P], F32R)
        wrh = small("wrh", [P, KT, NG + NE], F32R)
        wrl = small("wrl", [P, KT, NG + NE], F32R)
        gattnT = small("gattnT", [P, CT])
        gconvT = small("gconvT", [P, CT])
        convwT = small("convwT", [P, 3, CT])
        bf_b = small("bf_b", [P, H])
        gqk_b = small("gqk_b", [P, 2, HD])
        br_c = small("br_c", [NG + NE, 1])
        stat = small("stat", [P, 2, H])
        ms = small("ms", [P, 4])
        negmax = small("negmax", [P, 2])
        rowsum = small("rowsum", [P, 2, H])
        logits = small("logits", [P, NT, NG + NE])
        tokcode = small("tokcode", [P, NT])
        gates = small("gates", [P, 2, NT])
        eps_b = small("eps_b", [P, 1])
        one_b = small("one_b", [P, 1])
        gtab = small("gtab", [P, COLS], I32)
        stab = small("stab", [P, COLS], I32)
        bexp = small("bexp", [P, COLS], I32)
        last_pair = small("last_pair", [P, 1], I32)
        idxg = small("idxg", [P, 2], I32)
        idxs = small("idxs", [P, 2], I32)

        A0 = small.at

        p = Plan(nc, A0, top)
        uh = p("uh", [P, KT, KEYS], F32R)
        ul = p("ul", [P, KT, KEYS], F32R)
        x_at = p.at
        raw_a = p("raw_a", [P, KT, 3 * P])
        p.at = x_at + 4 * KT * AW
        conv_at = p.at
        conv = p("conv", [P, CT, T])
        v_at = p.at
        v = p("v", [P, NT + 1, AW])
        raw_b = Plan(nc, v_at, p.at)("raw_b", [P, KT, 3 * P])
        qT_at = p.at
        qT = p("qT", [P, H, T])
        kT = p("kT", [P, H, KPAD])
        kn_at = p.at
        c_ = Plan(nc, qT_at, kn_at)
        xin = c_("xin", [P, NT + 1, D])
        hn = c_("hn", [P, 2, D])
        sqj = c_("sqj", [P, D])
        part_end = c_.at
        gmix_b = Plan(nc, c_.at, kn_at)("gmix_b", [P, D])
        csb = c_("csb", [P, T + 2])
        early = Plan(nc, c_.at, kn_at)
        wr = early("wr", [P, KT, NG + NE])
        sel = early("sel", [H, CT, P])
        uc = c_("uc", [P, T + 2])
        ysq = c_("ysq", [P, T])
        rsb = c_("rsb", [P, T])
        c_ = Plan(nc, qT_at, part_end)
        conv_parts = [[c_(f"w_{n}_{s}", [P, KT, 3 * P], F32R) for n in ("high", "low")] for s in range(2)]
        c_ = Plan(nc, qT_at, qT_at + 4 * H * T)
        k_parts = [[c_(f"wk_{n}_{s}", [P, KT, AW // 2], F32R) for n in ("high", "low")] for s in range(2)]
        c_ = Plan(nc, x_at, conv_at)
        q_parts = [c_(f"wq_{n}", [P, KT, AW // 2], F32R) for n in ("high", "low")]
        m_ = Plan(nc, kn_at, top)
        kn = m_("kn", [P, 2, HH, AUG])
        fz = m_("fz", [P, NT + 1, H])
        fe = m_("fe", [P, NT + 1, H])
        lf = m_("lf", [P, NT + 1, H])
        facc = m_("facc", [P, NT + 1, H])
        cum = m_("cum", [P, NT + 1, H])
        sq = m_("sq", [P, AW // 2])
        lT = Plan(nc, m_.at, top)("lT", [P, T])
        y_ = Plan(nc, kn_at, m_.at)
        ot = y_("ot", [P, AW])
        rsa = y_("rsa", [P, AW])
        y_ = Plan(nc, m_.at + 4 * D, top)
        asqh = y_("asqh", [P, AW], F32R)
        asql = y_("asql", [P, AW], F32R)
        raw_at = m_.at
        raw_c = m_("raw_c", [P, KT, VC])
        raw_z = Plan(nc, raw_at, top)("raw_z", [P, CT, D // 2])
        conv_h = Plan(nc, x_at, conv_at)("conv_h", [P, CT, T], F32R)
        conv_l = Plan(nc, part_end, kn_at)("conv_l", [P, CT, T], F32R)
        z_parts = [[Plan(nc, qT_at + 4 * KT * 3 * P * (2 * s + m), kn_at)(f"wz_{n}_{s}", [P, CT, D // 2], F32R)
                    for m, n in enumerate(("high", "low"))] for s in range(2)]
        zx = Plan(nc, conv_at, v_at)("zx", [P, NT, D // 2])
        Z0, VB, K0, Q0 = CT + 1, CT + 3, CT + 4, CT + 6
        n_chunks = CT + 8
        chunk_raw = [(raw_a, raw_b)[u % 2] for u in range(CT + 1)] + [raw_z] * 2 + [raw_c] * 5
        chunk_parts = ([conv_parts[u % 2] for u in range(CT + 1)] + [z_parts[1], z_parts[0], conv_parts[1]] +
                       k_parts + [q_parts] * 2)
        a_ = Plan(nc, A0, conv_at)
        h1b = a_("h1b", [P, D])
        u2 = a_("u2", [P, D])
        gffn_b = a_("gffn_b", [P, D])
        u2sq = a_("u2sq", [P, D])
        woh = a_("woh", [P, CT, D], F32R)
        wol = a_("wol", [P, CT, D], F32R)
        wo = Plan(nc, conv_at, v_at)("wo", [P, CT, D])
        probs = a_("probs", [P, 2, KPAD])
        pT = a_("pT", [P, 2, (NT + 1) * P])
        aT = Plan(nc, a_.at, conv_at)("aT", [P, CT, P])
        asq = a_("asq", [P, AW])
        aTh = a_("aTh", [P, CT, P], F32R)
        aTl = a_("aTl", [P, CT, P], F32R)
        u2Th = a_("u2Th", [P, KT, P], F32R)
        u2Tl = a_("u2Tl", [P, KT, P], F32R)
        q_ = Plan(nc, A0, A0 + 4 * 4 * D)
        rowhot = q_("rowhot", [P, 2 * NT, P], F32R)
        one_at = q_.at
        one0 = q_("one0", [P, NT, NE])
        one1 = q_("one1", [P, NT, NE])
        both = q_("both", [P, NT, NE])
        prev = q_("prev", [P, NT + 1, NE])
        ranks = q_("ranks", [P, NT, NE])
        el = q_("el", [P, NT, NE])
        et = q_("et", [P, NT, NE])
        q_ = Plan(nc, one_at, q_.at)
        hot = q_("hot", [P, 2 * NT, COLS])
        bcmp = q_("bcmp", [P, COLS - NE, NE])
        oc = Plan(nc, conv_at - 1024, v_at - 4 * 2 * D)
        cmp7 = oc("cmp7", [P, NE, 8])
        t256 = oc("t256", [P, 16, 16])
        colhot = oc("colhot", [P, 2 * NT, COLS], F32R)
        over = oc("over", [P, 2, NE])
        nover = oc("nover", [P, NE])
        cnt = oc("cnt", [P, NE])
        r8 = [oc(f"r8_{n}", [P, 2, NT]) for n in range(10)]
        r4 = [oc(f"r4_{n}", [P, NT, NG]) for n in range(2)]
        tabf = [oc(f"tabf_{n}", [P, COLS]) for n in range(3)]
        w_ = Plan(nc, v_at, top)
        wg = w_("wg", [P, 2, KT, F])
        wu = w_("wu", [P, 2, KT, F])
        wd = w_("wd", [P, 2, FT, D])
        raw = {"g": wg, "u": wu, "d": wd}
        f_ = Plan(nc, A0, v_at - 4 * (2 * 2 * D))
        sil = f_("sil", [P, F])
        hid = f_("hid", [P, F])
        xh = f_("xh", [P, KT, P], F32R)
        xl = f_("xl", [P, KT, P], F32R)
        hh = f_("hh", [P, FT, P], F32R)
        hl = f_("hl", [P, FT, P], F32R)
        wh = f_("wh", [P, 2, KT, F], F32R)
        wl = f_("wl", [P, 2, KT, F], F32R)
        e_ = Plan(nc, v_at - 4 * (2 * 2 * D), v_at)
        yb = e_("yb", [P, 2, D])
        xg = e_("xg", [P, 2, D])
        l_ = Plan(nc, v_at, top)
        h1t = l_("h1t", [P, NT, D])
        y0 = l_("y0", [P, NT, D])
        y1 = l_("y1", [P, NT, D])

        ps = ctx.enter_context(nc.psum_tensor("ps", [P, 8, 512], F32))
        OB = 7

        NH = H * NT
        ONE_BANK = NH - H - 1

        def pt_bank(n, no):
            return 6 if no % 2 == 0 or n >= ONE_BANK else 2
        big = ps[:, :, :].rearrange("p b n -> p (b n)")

        def buf(job, width, rows=P):
            at = 3 * 512 * side(job)
            return big[0:rows, at:at + width]

        def turned_heads(n):
            return ps[0:AUG, 6 + n % 2, :]

        dram_u2 = nc.dram_tensor("u2_rows", [T, D], F32).ap()
        dram_part = nc.dram_tensor("conv_part_rows", [T, D], F32).ap()
        dram_h1 = nc.dram_tensor("h1_rows", [T, D], F32).ap()
        ys = nc.dram_tensor("expert_rows", [2 * T, D], F32).ap()

        made = [sem("ring_made_0"), sem("ring_made_1")]
        used = [sem("ring_used_0"), sem("ring_used_1")]
        consts = sem("consts")
        gmix_in = sem("gmix_in")
        params = sem("params")
        x_in = [sem(f"x_in_{n}") for n in range(NT + 1)]
        win_in = [sem(f"win_in_{u}") for u in range(n_chunks)]
        chunk_high = sem("chunk_high_parts")
        chunk_low = sem("chunk_low_parts")
        uh_ready = sem("uh_ready")
        conv_h_ready = sem("conv_h_ready")
        conv_l_ready = sem("conv_l_ready")
        zx_in = [[sem(f"zx_in_{part}_{n}") for n in range(2)] for part in range(2)]
        z_out = [[sem(f"z_out_{part}_{n}") for n in range(2)] for part in range(2)]
        woh_ready = sem("woh_ready")
        wol_ready = sem("wol_ready")
        aTh_ready = sem("aTh_ready")
        aTl_ready = sem("aTl_ready")
        rs_ready = sem("rs_ready")
        hn_ready = sem("hn_ready")
        act_step = sem("act_step")
        dve_step = sem("dve_step")
        pool_step = sem("pool_step")
        ysq_ready = sem("ysq_ready")
        rsb_ready = sem("rsb_ready")
        conv_done = sem("conv_done")
        f_ready = sem("f_ready")
        fe_ready = sem("fe_ready")
        lf_ready = sem("lf_ready")
        sq_ready = sem("sq_ready")
        ss_ready = sem("ss_ready")
        rk_ready = sem("rk_ready")
        kn_ready = sem("kn_ready")
        heads_turned = sem("heads_turned")
        heads_out = sem("heads_out")
        max_ready = sem("max_ready")
        pt_made = sem("pt_made")
        pt_out = [sem("pt_out_even"), sem("pt_out_odd")]
        pv_done = sem("pv_done")
        o_taken = sem("o_taken")
        asqh_ready = sem("asqh_ready")
        asql_ready = sem("asql_ready")
        exact_ready = sem("exact_ready")
        wrl_ready = sem("wrl_ready")
        u2Th_ready = sem("u2Th_ready")
        l2_ready = sem("l2_ready")
        rsa_ready = sem("rsa_ready")
        aT_ready = sem("aT_ready")
        wo_ready = sem("wo_ready")
        wo_in = sem("wo_in")
        xr_in = sem("xr_in")
        u2rs_ready = sem("u2rs_ready")
        u2_ready = sem("u2_ready")
        rows_out = sem("u2_rows_out")
        h1_out = sem("h1_rows_out")
        route_ready = sem("route_ready")
        gate_ask = sem("gate_ask")
        gate_exp = sem("gate_exp")
        wg_in = [sem("wg_in_0"), sem("wg_in_1")]
        wu_in = [sem("wu_in_0"), sem("wu_in_1")]
        wd_in = [sem("wd_in_0"), sem("wd_in_1")]
        xg_in = [sem("xg_in_0"), sem("xg_in_1")]
        x_turned = sem("x_turned")
        xh_ready = sem("xh_ready")
        xl_ready = sem("xl_ready")
        w_high = {m: sem(f"high_parts_{m}") for m in "gud"}
        w_low = {m: sem(f"low_parts_{m}") for m in "gud"}
        w_used = sem("halves_used")
        sil_ready = sem("sil_ready")
        hid_ready = sem("hid_ready")
        hid_turned = sem("hid_turned")
        hh_ready = sem("hh_ready")
        hl_ready = sem("hl_ready")
        y_taken = sem("y_taken")
        ys_out = [sem("ys_out_0"), sem("ys_out_1")]
        idx_ready = sem("idx_ready")
        pool_pass = sem("pool_pass")
        yb_free = sem("yb_free")
        all_out = sem("all_expert_rows_out")
        y_in = [sem(f"y_in_{t}") for t in range(NT)]
        fin_ready = sem("fin_ready")
        fin_out = sem("fin_out")

        def wait_made(eng, job):
            eng.wait_ge(made[side(job)], uses(job))

        def wait_used(eng, job):
            eng.wait_ge(used[side(job)], uses(job))

        toks = [NT] + list(range(NT))

        def rows(t):
            return META if t == NT else P

        def u_cols(t):
            return (0, META) if t == NT else (META + P * t, META + P * (t + 1))

        w_in_sems = {"g": wg_in, "u": wu_in, "d": wd_in}

        def used_after(m, b):
            if m == "last d":
                return 6 * b + 6
            if isinstance(b, int) and b == 0 and m != "d":
                return {"g": 2, "u": 4}[m]
            return 6 * b + {"g": 0, "u": 2, "d": 10}[m]

        def half(t, s, n):
            size = KT * F // 2
            k = t[:, s, :, :].rearrange("p k f -> p (k f)")
            return k[:, size * n:size * (n + 1)]

        heads = [(i, h) for i in range(NT) for h in range(H)]
        qk = [job for job in JOBS if job[0] in ("K", "Q")]
        next_chunk = {1: K0 + 1, NT + 2: Q0, qk.index(("Q", NT - 1, 0)): Q0 + 1}
        last_job = {u: ("B", u) for u in range(CT)}
        last_job.update({CT: ("V", NT - 1, 1), Z0: ("Z", NT - 1, 0), Z0 + 1: ("Z", NT - 1, 1),
                         VB: ("V", NT - 1, 0), K0: ("K", NT - 1, 0), K0 + 1: ("K", NT - 1, 1),
                         Q0: ("Q", NT - 1, 0), Q0 + 1: ("Q", NT - 1, 1)})

        def chunk_cols(u):
            if u in (CT, VB):
                a = COL_V + (VC if u == CT else 0)
                return a, a + VC
            n = u - K0
            a = (AW if n < 2 else 0) + AW // 2 * (n % 2)
            return a, a + AW // 2

        def chunk_half(t, u, n):
            if u in (Z0, Z0 + 1):
                return t[:, CT // 2 * n:CT // 2 * (n + 1), :]
            size = 3 * P if u < CT else chunk_cols(u)[1] - chunk_cols(u)[0]
            return t[:, KT // 2 * n:KT // 2 * (n + 1), 0:size]

        NPAR = 12

        def width(i):
            return KPAD if i == NT - 1 else META + P * (i + 1)

        def banks(i):
            return -(-width(i) // 512)

        def score_buf(i, h):
            b0, n = 3 * side(("S", i, h)), banks(i)
            return ps[:, b0:b0 + n, 0:width(i) // n]

        def group_no(n, g):
            return GROUPS[(*heads[n], g)]

        block = ctx.enter_context(nc.Block())

        @block.sync
        def _(sp):
            w_in_k = w_in.rearrange("(k p) c -> p k c", p=P)

            def load_x(n):
                t = toks[n]
                src = meta[:, :] if t == NT else x[P * t:P * (t + 1), :]
                sp.dma_start(xin[0:rows(t), n, :], src).then_inc(x_in[n], 16)

            def load_chunk(u):
                if u in (2, 3, 4):
                    sp.wait_ge(chunk_low, 2 * (u - 1))
                if u > Z0:
                    sp.wait_ge(chunk_low, 2 * u)
                if u < CT:
                    for n, col in enumerate((COL_B, COL_C, COL_H)):
                        sp.dma_start(chunk_raw[u][:, :, P * n:P * (n + 1)],
                                     w_in_k[:, :, col + P * u:col + P * (u + 1)]).then_inc(win_in[u], 16)
                elif u in (Z0, Z0 + 1):
                    sp.dma_start(raw_z[:, :, :], w_out[AW:, :].rearrange("(k p) c -> p k c", p=P)[
                        :, :, D // 2 * (u - Z0):D // 2 * (u - Z0 + 1)]).then_inc(win_in[u], 16)
                else:
                    a, b = chunk_cols(u)
                    sp.dma_start(chunk_raw[u][:, :, 0:b - a], w_in_k[:, :, a:b]).then_inc(win_in[u], 16)

            load_x(0)
            load_x(1)
            sp.dma_start(gmix_b[:, :], g_mix.partition_broadcast(P)).then_inc(gmix_in, 16)
            for n in range(2, NT + 1):
                load_x(n)
            for u in range(n_chunks):
                load_chunk(u)
            wait_made(sp, ("Q", NT - 1, 1))
            for part in range(2):
                for n in range(2):
                    sp.wait_ge(z_out[part][n], 16 * NT // 2)
            sp.dma_start(wo[:, :, :], w_out[0:AW, :].rearrange("(k p) c -> p k c", p=P)).then_inc(wo_in, 16)
            sp.dma_start(gffn_b[:, :], g_ffn.partition_broadcast(P)).then_inc(wo_in, 16)
            for i in range(NT):
                if i:
                    sp.wait_ge(h1_out, 16 * i)
                    sp.wait_ge(u2_ready, i)
                sp.dma_start(h1b[:, :], dram_part[P * i:P * (i + 1), :]).then_inc(xr_in, 16)
            sp.wait_ge(pv_done, NH)

            def load_expert(e, s):
                sp.dma_start(wg[:, s, :, :], w_gate[e].rearrange("(k p) f -> p k f", p=P)).then_inc(wg_in[s], 16)
                sp.dma_start(wu[:, s, :, :], w_up[e].rearrange("(k p) f -> p k f", p=P)).then_inc(wu_in[s], 16)
                sp.dma_start(wd[:, s, :, :], w_down[e].rearrange("(k p) f -> p k f", p=P)).then_inc(wd_in[s], 16)

            load_expert(0, 0)
            sp.wait_ge(rows_out, 16 * NT)
            wait_made(sp, ("LT", 0))
            load_expert(1, 1)

            def load_next(m, src, e, b, s):
                sp.wait_ge(w_low[m], 2 * b - 2)
                sp.dma_start(raw[m][:, s, :, :], src[e].rearrange("o (k p) f -> p (o k) f", p=P)
                             ).then_inc(w_in_sems[m][s], 16)

            load_next("g", w_gate, slice(2, 3), 2, 0)
            load_next("u", w_up, slice(2, 3), 2, 0)
            load_next("g", w_gate, slice(3, 4), 3, 1)
            load_next("u", w_up, slice(3, 4), 3, 1)
            load_next("d", w_down, slice(2, 3), 2, 0)
            sp.wait_ge(route_ready, 1)
            last = sp.value_load(last_pair[0:1, 0:1], min_val=NE - 2, max_val=NE + MAX_OVER - 1)

            def expert_of(b):
                return bass.ds(sp.value_load(bexp[0:1, bass.ds(b, 1)], min_val=0, max_val=NE - 1), 1)

            with sp.Fori(4, last + 2, 2) as i:
                for s in range(2):
                    e = expert_of(i + s)
                    load_next("g", w_gate, e, i + s, s)
                    load_next("u", w_up, e, i + s, s)
                    load_next("d", w_down, expert_of(i + s - 1), i + s - 1, 1 - s)
            load_next("d", w_down, expert_of(last + 1), last + 1, 1)
            sp.wait_ge(w_low["g"], 2 * last + 4)
            sp.wait_ge(h1_out, 16 * NT)
            for t in range(NT):
                sp.dma_start(h1t[:, t, :], dram_h1[P * t:P * (t + 1), :]).then_inc(y_in[t], 16)
            sp.wait_ge(all_out, 1)
            for t in range(NT):
                for dst, src in ((y0, ys[P * t:P * (t + 1), :]),
                                 (y1, ys[T + P * t:T + P * (t + 1), :])):
                    sp.dma_start(dst[:, t, :], src).then_inc(y_in[t], 16)

        @block.gpsimd
        def _(pool):
            count = [0]

            def then(ins):
                count[0] += 1
                ins.then_inc(pool_step, 1)
                pool.wait_ge(pool_step, count[0])

            then(nc.gpsimd.memset(eps_b[:], EPS))
            then(nc.gpsimd.memset(ident[:], 0.0))
            nc.gpsimd.affine_select(out=ident[:], in_=ident[:], compare_op=ALU.not_equal, fill=1.0, base=0,
                                    pattern=[[-1, P]], channel_multiplier=1).then_inc(consts, 1)
            for tile_, value in ((identb, 0.0), (maskb, 0.0), (tri, 1.0), (tris, 1.0),
                                 (ones, 1.0), (sel, 0.0), (one_b, 1.0), (blockones, 0.0),
                                 (lf, 0.0), (fz, 0.0), (kn, 1.0)):
                then(nc.gpsimd.memset(tile_[:], value))
            then(nc.gpsimd.affine_select(out=identb[:], in_=identb[:], compare_op=ALU.not_equal, fill=1.0, base=0,
                                         pattern=[[-1, P]], channel_multiplier=1))
            then(nc.gpsimd.affine_select(out=maskb[:], in_=maskb[:], compare_op=ALU.is_ge, fill=NEG, base=0,
                                         pattern=[[-1, P + META]], channel_multiplier=1))
            then(nc.gpsimd.affine_select(out=sel[:].rearrange("h c (r d) -> h c r d", r=2),
                                         in_=sel[:].rearrange("h c (r d) -> h c r d", r=2),
                                         compare_op=ALU.not_equal, fill=1.0, base=0,
                                         pattern=[[-2, CT], [-1, 2], [0, HD]], channel_multiplier=1))
            then(nc.gpsimd.affine_select(out=tri[:], in_=tri[:], compare_op=ALU.is_ge, fill=0.0, base=0,
                                         pattern=[[1, P]], channel_multiplier=-1))
            then(nc.gpsimd.affine_select(out=tris[:], in_=tris[:], compare_op=ALU.is_gt, fill=0.0, base=0,
                                         pattern=[[1, P]], channel_multiplier=-1))
            for n in range(2):
                then(nc.gpsimd.memset(blockones[HD * n:HD * (n + 1), HD * n:HD * (n + 1)], 1.0 / HD))
            then(nc.gpsimd.iota(iota128[:], pattern=[[1, P]], base=0, channel_multiplier=0,
                                allow_small_or_imprecise_dtypes=True))
            nc.gpsimd.iota(tokcode[:], pattern=[[P, NT]], base=1, channel_multiplier=1,
                           allow_small_or_imprecise_dtypes=True).then_inc(consts, 1)
            slow = dict(allow_slow_non_contiguous=True)
            pool.dma_start(wr[:, :, 0:NG], w_rg.rearrange("(k p) c -> p k c", p=P), **slow).then_inc(params, 16)
            pool.dma_start(wr[:, :, NG:], w_re.rearrange("(k p) c -> p k c", p=P), **slow).then_inc(params, 16)
            pool.dma_start(gattnT[:, :], g_attn.rearrange("(k p) -> p k", p=P), **slow).then_inc(params, 16)
            pool.dma_start(gconvT[:, :], g_conv.rearrange("(k p) -> p k", p=P), **slow).then_inc(params, 16)
            for n in range(3):
                pool.dma_start(convwT[:, n, :], conv_w[n].rearrange("(k p) -> p k", p=P),
                               **slow).then_inc(params, 16)
            pool.dma_start(bf_b[:, :], b_forget.partition_broadcast(P)).then_inc(params, 16)
            pool.dma_start(gqk_b[:, 0, :], gq.partition_broadcast(P)).then_inc(params, 16)
            pool.dma_start(gqk_b[:, 1, :], gk.partition_broadcast(P)).then_inc(params, 16)
            pool.dma_start(br_c[0:NG, :], b_rg.unsqueeze(1), **slow).then_inc(params, 16)
            pool.dma_start(br_c[NG:, :], b_re.unsqueeze(1), **slow).then_inc(params, 16)
            x_tiles = x.rearrange("(t p) c -> p t c", p=P)

            def load_zx(part, n):
                ts, cols = slice(NT // 2 * n, NT // 2 * (n + 1)), slice(D // 2 * part, D // 2 * (part + 1))
                pool.dma_start(zx[:, ts, :], x_tiles[:, ts, cols]).then_inc(zx_in[part][n], 16)

            pool.wait_ge(conv_l_ready, CT)
            load_zx(0, 0)
            load_zx(0, 1)
            for part in range(2):
                for t in range(NT):
                    n = t // (NT // 2)
                    wait_used(pool, ("Z", t, part))
                    pool.dma_start(dram_part[P * t:P * (t + 1), D // 2 * part:D // 2 * (part + 1)],
                                   zx[:, t, :]).then_inc(z_out[part][n], 16)
                    if part == 0 and t % (NT // 2) == NT // 2 - 1:
                        pool.wait_ge(z_out[0][n], 16 * NT // 2)
                        load_zx(1, n)
            wait_made(pool, ("V", NT - 1, 0))
            nc.gpsimd.memset(kT[:, :, KEYS:], 0.0).then_inc(consts, 1)
            for i in range(NT):
                wait_used(pool, ("W", i))
                pool.dma_start(dram_h1[P * i:P * (i + 1), :], h1b[:, :]).then_inc(h1_out, 16)
                pool.wait_ge(u2_ready, i + 1)
                pool.dma_start(dram_u2[P * i:P * (i + 1), :], u2[:, :]).then_inc(rows_out, 16)
            nc.gpsimd.memset(xg[:], 0.0).then_inc(pool_step, 1)
            count[0] += 1
            pool.wait_ge(pool_step, count[0])
            wait_made(pool, ("LT", 0))
            for m, slot in (("g", 0), ("u", 1)):
                for n in range(2):
                    pool.wait_ge(w_high[m], n + 1)
                    nc.gpsimd.tensor_tensor(half(wl, slot, n), half(raw[m], 0, n), half(wh, slot, n).bitcast(F32),
                                            ALU.subtract).then_inc(w_low[m], 1)
            pool.wait_ge(rows_out, 16 * NT)
            pool.wait_ge(route_ready, 1)
            last_token, last_row = pool.to_reg(T - 1), pool.to_reg(2 * T - 1)
            for s in range(2):
                nc.gpsimd.tensor_copy(idxg[:, s:s + 1], gtab[:, s:s + 1]).then_inc(idx_ready, 1)
                pool.wait_ge(idx_ready, s + 1)
                nc.gpsimd.indirect_dma_start(
                    out=xg[:, s, :], out_offset=None, in_=dram_u2[:, :],
                    in_offset=bass.IndirectOffsetOnAxis(ap=idxg[:, s:s + 1].bitcast(U32), axis=0),
                    bounds_check=last_token, oob_is_err=False).then_inc(xg_in[s], 16)
                pool.sem_inc(yb_free, 1)
            last = pool.value_load(last_pair[0:1, 0:1], min_val=NE - 2, max_val=NE + MAX_OVER - 1)

            def gather(b, s, n_idx):
                pool.wait_ge(x_turned, b - 1)
                nc.gpsimd.tensor_copy(idxg[:, s:s + 1], gtab[:, bass.ds(b, 1)]).then_inc(idx_ready, 1)
                pool.wait_ge(idx_ready, n_idx)
                pool.sem_inc(pool_pass, 1)
                nc.gpsimd.indirect_dma_start(
                    out=xg[:, s, :], out_offset=None, in_=dram_u2[:, :],
                    in_offset=bass.IndirectOffsetOnAxis(ap=idxg[:, s:s + 1].bitcast(U32), axis=0),
                    bounds_check=last_token, oob_is_err=False).then_inc(xg_in[s], 16)

            def scatter(b, s, n_idx):
                nc.gpsimd.tensor_copy(idxs[:, s:s + 1], stab[:, bass.ds(b, 1)]).then_inc(idx_ready, 1)
                pool.wait_ge(idx_ready, n_idx)
                pool.wait_ge(y_taken, b + 2)
                pool.sem_inc(pool_pass, 1)
                nc.gpsimd.indirect_dma_start(
                    out=ys[:, :], in_=yb[:, s, :], in_offset=None,
                    out_offset=bass.IndirectOffsetOnAxis(ap=idxs[:, s:s + 1].bitcast(U32), axis=0),
                    bounds_check=last_row, oob_is_err=False).then_inc(ys_out[s], 16)

            def free_result(s, n):
                pool.wait_ge(ys_out[s], 16 * n)
                pool.sem_inc(yb_free, 1)

            gather(2, 0, 3)
            gather(3, 1, 4)
            gather(4, 0, 5)
            scatter(0, 0, 6)
            gather(5, 1, 7)
            scatter(1, 1, 8)
            free_result(0, 1)
            with pool.Fori(2, last, 2) as i:
                for s in range(2):
                    gather(i + s + 4, s, 2 * (i + s) + 5)
                    scatter(i + s, s, 2 * (i + s) + 6)
                    free_result(1 - s, i // 2 + s)
            for s in range(2):
                scatter(last + s, s, 2 * last + 5 + s)
                if s == 0:
                    free_result(1, last // 2)
            for s in range(2):
                pool.wait_ge(ys_out[s], 16 * (last // 2 + 1))
                pool.wait_ge(xg_in[s], 16 * (last // 2 + 2))
            pool.wait_ge(h1_out, 16 * NT)
            pool.sem_inc(all_out, 1)

        @block.tensor
        def _(pe):
            mm = nc.tensor.matmul

            def start(job):
                if uses(job) > 1:
                    pe.wait_ge(used[side(job)], uses(job) - 1)

            def done(job, last):
                last.then_inc(made[side(job)], 1)

            def turn_x(t, n):
                job = ("T", t)
                start(job)
                pe.wait_ge(hn_ready, n + 1)
                r = rows(t)
                for k in range(KT):
                    last = nc.tensor.transpose(buf(job, KT * P)[:, P * k:P * k + r],
                                               hn[0:r, n % 2, P * k:P * (k + 1)], ident[0:r, 0:r])
                done(job, last)

            def three(o, lhs, rhs, k, last=KT - 1):
                (a_high, a_low), (b_high, b_low) = lhs, rhs
                mm(o, a_high, b_high, start=(k == 0), stop=False)
                mm(o, a_high, b_low, start=False, stop=False)
                return mm(o, a_low, b_high, start=False, stop=(k == last))

            def wait_half(u, k):
                if k % (KT // 2) == 0:
                    pe.wait_ge(chunk_low, 2 * u + k // (KT // 2) + 1)

            def channels(kind, c):
                job = (kind, c)
                start(job)
                sect = {"B": 0, "C": 1, "H": 2}[kind]
                n_chunk, size, at = (2, 512, META) if kind == "B" else (3, (T + 2) // 3, META - 2)
                for j in range(n_chunk):
                    for k in range(KT):
                        if kind == "C" and j == 0:
                            wait_half(c, k)
                        last = three(ps[:, 3 * side(job) + j, 0:size],
                                     [w[:, k, P * sect:P * (sect + 1)] for w in chunk_parts[c]],
                                     [u[:, k, at + size * j:at + size * (j + 1)] for u in (uh, ul)], k)
                done(job, last)

            def conv_mean(c):
                job = ("R", c)
                start(job)
                pe.wait_ge(ysq_ready, c + 1)
                for j in range(2):
                    last = mm(ps[:, 3 * side(job) + j, :], blockones[:, :], ysq[:, 512 * j:512 * (j + 1)],
                              start=True, stop=True)
                done(job, last)

            def tokens(job, u):
                t = job[1]
                a = u_cols(t)[0]
                start(job)
                for k in range(KT):
                    if t == (0 if job[0] == "Q" else NT):
                        wait_half(u, k)
                    n = chunk_cols(u)[1] - chunk_cols(u)[0]
                    last = three(ps[:, 3 * side(job), 0:n], [x_[:, k, a:a + P] for x_ in (uh, ul)],
                                 [w[:, k, 0:n] for w in chunk_parts[u]], k)
                done(job, last)

            def turn_heads(n):
                kind, t, part = qk[n]
                if n >= 2:
                    pe.wait_ge(heads_out, n - 1)
                pe.wait_ge(kn_ready, n + 1)
                r = rows(t)
                for h in range(HH):
                    last = nc.tensor.transpose(turned_heads(n)[:, P * h:P * h + r], kn[0:r, n % 2, h, :],
                                               ident[0:r, 0:r])
                last.then_inc(heads_turned, 1)

            def scores(n):
                i, h = heads[n]
                job = ("S", i, h)
                start(job)
                q = qT[0:AUG, h, P * i:P * (i + 1)]
                b0 = 3 * side(job)
                size = width(i) // banks(i)
                for b in range(banks(i)):
                    diag = b == banks(i) - 1
                    mm(ps[:, b0 + b, 0:size], q, kT[0:AUG, h, size * b:size * (b + 1)], start=True, stop=not diag)
                at = META + P * i - size * b
                done(job, mm(ps[:, b0 + b, at:size], identb[:, :], maskb[:, 0:size - at], start=False, stop=True))

            def turn(n, g):
                no = group_no(n, g)
                if g == 0:
                    wait_used(pe, ("S", *heads[n]))
                if no >= 2:
                    pe.wait_ge(pt_out[no % 2], no // 2)
                if n >= ONE_BANK:
                    pe.wait_ge(pt_out[(no - 1) % 2], (no - 1) // 2 + 1)
                for m, j in enumerate(groups(heads[n][0])[g]):
                    at = max(0, META + P * (j - 1))
                    last = nc.tensor.transpose(ps[:, pt_bank(n, no), P * m:P * (m + 1)],
                                               probs[:, n % 2, at:at + P], ident[:, :])
                last.then_inc(pt_made, 1)

            def times_v(n, part, parts):
                i, h = heads[n]
                gs = groups(i)
                if part == 0 and h == 0 and i:
                    pe.wait_ge(o_taken, i)
                blocks = [(g, j) for g, js in enumerate(gs) for j in js]
                for g, j in blocks[len(blocks) * part // parts:len(blocks) * (part + 1) // parts]:
                    no = group_no(n, g)
                    if j == gs[g][0]:
                        pe.wait_ge(pt_out[no % 2], no // 2 + 1)
                    r, t = (META, NT) if j == 0 else (P, j - 1)
                    a = HD * (h % 2)
                    last = mm(ps[a:a + HD, OB, P * (h // 2):P * (h // 2 + 1)], v[0:r, t, HD * h:HD * (h + 1)],
                              pT[0:r, n % 2, P * j:P * (j + 1)], start=(j == 0), stop=(j == i + 1))
                    if j == i + 1:
                        last.then_inc(pv_done, 1)

            def extra(kind, i):
                job = (kind, i)
                start(job)
                b0 = 3 * side(job)
                if kind == "N":
                    pe.wait_ge(l2_ready, i + 1)
                    last = nc.tensor.transpose(ps[0:H, b0, 0:P], l2[:, :], ident[:, :])
                elif kind == "M":
                    pe.wait_ge(asql_ready, i + 1)
                    wait_used(pe, ("N", i))
                    mm(ps[:, b0, :], ones64[:, :], asqh[:, :], start=True, stop=False)
                    mm(ps[:, b0, :], ones64[:, :], asql[:, :], start=False, stop=False)
                    for c in range(CT):
                        o = ps[:, b0, P * c:P * (c + 1)]
                        mm(o, selr[:, c, :], l2Th[:, :], start=False, stop=False)
                        last = mm(o, selr[:, c, :], l2Tl[:, :], start=False, stop=(c == CT - 1))
                elif kind == "W":
                    pe.wait_ge(aTl_ready, i + 1)
                    if i == 0:
                        pe.wait_ge(wol_ready, CT)
                        pe.wait_ge(wrl_ready, 1)
                    for j in range(2):
                        for k in range(CT):
                            last = three(ps[:, b0 + j, :], [a[:, k, :] for a in (aTh, aTl)],
                                         [w[:, k, 512 * j:512 * (j + 1)] for w in (woh, wol)], k, CT - 1)
                elif kind == "U":
                    pe.wait_ge(u2_ready, i + 1)
                    for k in range(KT):
                        last = nc.tensor.transpose(buf(job, D)[:, P * k:P * (k + 1)], u2[:, P * k:P * (k + 1)],
                                                   ident[:, :])
                else:
                    wait_used(pe, ("U", i))
                    for k in range(KT):
                        last = three(ps[0:NG + NE, b0, 0:P], [w[:, k, :] for w in (wrh, wrl)],
                                     [u[:, k, :] for u in (u2Th, u2Tl)], k)
                done(job, last)

            pe.wait_ge(consts, 1)
            for n, t in enumerate(toks):
                turn_x(t, n)
            for t in toks[-2:]:
                wait_used(pe, ("T", t))
            pe.wait_ge(consts, 2)
            pe.wait_ge(params, 16 * NPAR)
            for c in range(CT):
                channels("C", c)
                channels("H", c)
                channels("B", c)
                if c:
                    conv_mean(c - 1)
            for n, t in enumerate(toks):
                tokens(("V", t, 1), CT)
                if n == 1:
                    conv_mean(CT - 1)
            pe.wait_ge(conv_l_ready, CT)
            for part in range(2):
                for t in range(NT):
                    job = ("Z", t, part)
                    start(job)
                    for k in range(CT):
                        if t == 0 and k % (CT // 2) == 0:
                            pe.wait_ge(chunk_low, 2 * (Z0 + part) + k // (CT // 2) + 1)
                        last = three(ps[:, 3 * side(job), :],
                                     [c_[:, k, P * t:P * (t + 1)] for c_ in (conv_h, conv_l)],
                                     [w[:, k, :] for w in chunk_parts[Z0 + part]], k, CT - 1)
                    done(job, last)
            for t in toks:
                tokens(("V", t, 0), VB)
            job = ("CUM", 0)
            start(job)
            pe.wait_ge(lf_ready, 1)
            mm(ps[:, 3 * side(job), 0:(NT + 1) * H], tri[:, :], lf[:, :, :].rearrange("p t h -> p (t h)"),
               start=True, stop=False)
            done(job, mm(ps[:, 3 * side(job), 0:(NT + 1) * H], ones[:, :],
                         facc[:, :, :].rearrange("p t h -> p (t h)"), start=False, stop=True))
            for n, job in enumerate(qk):
                tokens(job, (K0 if job[0] == "K" else Q0) + job[2])
                if n:
                    turn_heads(n - 1)
            turn_heads(len(qk) - 1)
            pe.wait_ge(heads_out, len(qk))
            pe.wait_ge(consts, 3)
            for n in range(NH + 2):
                if n < NH:
                    if n == ONE_BANK + 1:
                        no = group_no(n - 2, len(groups(heads[n - 2][0])) - 1)
                        for m in (no - 1, no):
                            pe.wait_ge(pt_out[m % 2], m // 2 + 1)
                    scores(n)
                parts = len(groups(heads[n - 1][0])) if 1 <= n <= NH else 1
                for g in range(parts):
                    if 1 <= n <= NH:
                        turn(n - 1, g)
                    if n >= 2:
                        times_v(n - 2, g, parts)
                if n < NH and heads[n][0] and heads[n][1] in EXTRA:
                    extra(EXTRA[heads[n][1]], heads[n][0] - 1)
            for kind in ("N", "M", "W", "U", "L"):
                extra(kind, NT - 1)
            job = ("LT", 0)
            start(job)
            for t in (NT - 2, NT - 1):
                wait_used(pe, ("L", t))
            for t in range(NT):
                last = nc.tensor.transpose(ps[:, 3 * side(job), (NG + NE) * t:(NG + NE) * (t + 1)],
                                           lT[0:NG + NE, P * t:P * (t + 1)], ident[0:NG + NE, 0:NG + NE])
            done(job, last)
            job = ("RANK", 0)
            start(job)
            pe.wait_ge(gate_ask, 2)
            b0 = 3 * side(job)
            mm(ps[:, b0, 0:NT * NE], tris[:, :], both[:, :, :].rearrange("p t e -> p (t e)"), start=True, stop=False)
            mm(ps[:, b0, 0:NT * NE], ones[:, :], prev[:, 0:NT, :].rearrange("p t e -> p (t e)"),
               start=False, stop=True)
            done(job, mm(ps[:, b0, NT * NE:(NT + 1) * NE], ones[:, :], prev[:, NT, :], start=True, stop=True))
            job = ("TABLE", 0)
            start(job)
            pe.wait_ge(gate_ask, 3)
            for m in range(2 * NT):
                last = mm(ps[:, 3 * side(job), 0:COLS], rowhot[:, m, :], colhot[:, m, :],
                          start=(m == 0), stop=(m == 2 * NT - 1))
            done(job, last)
            pe.wait_ge(route_ready, 1)
            final = pe.value_load(last_pair[0:1, 0:1], min_val=NE - 2, max_val=NE + MAX_OVER - 1)

            def turn_tokens(b, s):
                pe.wait_ge(xg_in[s], 16 * ((b - s) // 2 + 1))
                for k in range(KT):
                    last = nc.tensor.transpose(big[:, P * k:P * (k + 1)], xg[:, s, P * k:P * (k + 1)], ident[:, :])
                last.then_inc(x_turned, 1)

            def product(m, b, slot, first):
                if first:
                    pe.wait_ge(xl_ready, b + 1)
                for n in range(2):
                    pe.wait_ge(w_low[m], 2 * b + n + 1)
                    for k in range(KT // 2 * n, KT // 2 * (n + 1)):
                        o = ps[:, 2 if m == "g" else 3, :]
                        mm(o, xh[:, k, :], wh[:, slot, k, :], start=(k == 0), stop=False)
                        mm(o, xh[:, k, :], wl[:, slot, k, :], start=False, stop=False)
                        last = mm(o, xl[:, k, :], wh[:, slot, k, :], start=False, stop=(k == KT - 1))
                    last.then_inc(w_used, 1)

            def turn_hidden(b):
                pe.wait_ge(hid_ready, b + 1)
                for k in range(FT):
                    last = nc.tensor.transpose(ps[:, 4, P * k:P * (k + 1)], hid[:, P * k:P * (k + 1)], ident[:, :])
                last.then_inc(hid_turned, 1)

            def down(b, slot):
                pe.wait_ge(hl_ready, b + 1)
                pe.wait_ge(y_taken, b + 1)
                for n in range(2):
                    pe.wait_ge(w_low["d"], 2 * b + n + 1)
                    for k in range(FT // 2 * n, FT // 2 * (n + 1)):
                        for j in range(2):
                            o, r = ps[:, 5 + j, :], 2 * k + j
                            mm(o, hh[:, k, :], wh[:, slot, r, :], start=(k == 0), stop=False)
                            mm(o, hh[:, k, :], wl[:, slot, r, :], start=False, stop=False)
                            last = mm(o, hl[:, k, :], wh[:, slot, r, :], start=False, stop=(k == FT - 1))
                    last.then_inc(w_used, 1)

            def blocks(b, s, more):
                pe.wait_ge(sil_ready, b + 1)
                product("g", b + 1, s, True)
                turn_hidden(b)
                product("u", b + 1, 1 - s, False)
                if more:
                    turn_tokens(b + 2, s)
                down(b, s)

            turn_tokens(0, 0)
            product("g", 0, 0, True)
            product("u", 0, 1, False)
            turn_tokens(1, 1)
            with pe.Fori(0, final, 2) as i:
                for s in range(2):
                    blocks(i + s, s, True)
            blocks(final, 0, False)
            turn_hidden(final + 1)
            down(final + 1, 1)

        @block.scalar
        def _(act):
            count = [0]
            A = nc.scalar.activation

            def then(ins):
                count[0] += 1
                ins.then_inc(act_step, 1)
                act.wait_ge(act_step, count[0])

            def inv_root(dst, src, scale):
                then(A(dst, src, ACT.Ln, bias=eps_b[0:dst.shape[0], :], scale=scale))
                return A(dst, dst, ACT.Exp, scale=-0.5)

            nc.scalar.preload_act_table_set("natural_log_exp_and_others")
            def high_chunk(u):
                act.wait_ge(win_in[u], 16 * (3 if u < CT else 1))
                if u == 0:
                    act.wait_ge(hn_ready, 6)
                elif u == 1:
                    wait_used(act, ("T", NT - 1))
                elif u == Q0:
                    wait_made(act, last_job[Z0 + 1])
                elif u in (K0 + 1, Q0 + 1):
                    wait_made(act, last_job[VB if u == K0 + 1 else Q0])
                else:
                    wait_made(act, last_job[u - 2])
                for n in range(2):
                    A(chunk_half(chunk_parts[u][0], u, n), chunk_half(chunk_raw[u], u, n),
                      ACT.Copy).then_inc(chunk_high, 1)

            def high_u(t):
                job, r = ("T", t), rows(t)
                wait_made(act, job)
                a, b = u_cols(t)
                A(uh[:, :, a:b], buf(job, KT * P).rearrange("p (k n) -> p k n", k=KT)[:, :, 0:r],
                  ACT.Copy).then_inc(uh_ready, 1)

            act.wait_ge(consts, 1)
            for n, t in enumerate(toks):
                r = rows(t)
                act.wait_ge(x_in[n], 16)
                if n >= 2:
                    act.wait_ge(hn_ready, n - 1)
                then(A(sqj[0:r, :], xin[0:r, n, :], ACT.Square, accum_out=ms[0:r, n % 2:n % 2 + 1]))
                inv_root(ms[0:r, n % 2:n % 2 + 1], ms[0:r, n % 2:n % 2 + 1], 1.0 / D).then_inc(rs_ready, 1)
                if n:
                    high_u(toks[n - 1])
            high_u(toks[-1])
            high_chunk(0)
            high_chunk(1)
            act.wait_ge(consts, 2)
            act.wait_ge(params, 16 * NPAR)
            A(ones64[:, :], blockones[:, :], ACT.Copy).then_inc(exact_ready, 1)
            A(selr[:, :, :], sel[:, :, :], ACT.Copy).then_inc(exact_ready, 1)
            A(wrh[:, :, :], wr[:, :, :], ACT.Copy).then_inc(exact_ready, 1)
            act.wait_ge(consts, 2)

            def conv_root(c):
                wait_made(act, ("R", c))
                if c:
                    act.wait_ge(conv_done, c)
                count[0] += 1
                A(rsb[:, :], buf(("R", c), T), ACT.Ln, bias=eps_b[:, :]).then_inc(used[side(("R", c))], 1)
                wait_used(act, ("R", c))
                count[0] -= 1
                A(rsb[:, :], rsb[:, :], ACT.Exp, scale=-0.5).then_inc(rsb_ready, 1)

            for c in range(CT):
                job = ("C", c)
                wait_made(act, job)
                if c:
                    wait_used(act, ("H", c - 1))
                b0 = 3 * side(job)
                A(csb[:, :].rearrange("p (j n) -> p j n", j=3), ps[:, b0:b0 + 3, 0:(T + 2) // 3],
                  ACT.Copy).then_inc(used[side(job)], 1)
                wait_used(act, ("B", c))
                if c:
                    wait_made(act, ("R", c - 1))
                    conv_root(c - 1)
                A(ysq[:, :], conv[:, c, :], ACT.Square).then_inc(ysq_ready, 1)
                high_chunk(c + 2)
            for n, t in enumerate(toks):
                job, r = ("V", t, 1), rows(t)
                wait_made(act, job)
                b0 = 3 * side(job)
                A(v[0:r, t, VC:], ps[0:r, b0, 0:AW - VC], ACT.Copy)
                A(fz[0:r, t, :], ps[0:r, b0, AW - VC:VC], ACT.Copy).then_inc(used[side(job)], 1)
                if n == 1:
                    conv_root(CT - 1)
                if n == 3:
                    act.wait_ge(chunk_low, 2 * (CT + 1))
                    act.wait_ge(conv_done, CT)
                    for c in range(CT):
                        A(conv_h[:, c, :], conv[:, c, :], ACT.Copy).then_inc(conv_h_ready, 1)
            high_chunk(Z0 + 1)
            act.wait_ge(f_ready, 1)
            then(A(fe[:, :, :], fe[:, :, :], ACT.Exp, scale=-1.0))
            A(fe[:, :, :], fe[:, :, :], ACT.Ln, bias=one_b[:, :]).then_inc(fe_ready, 1)
            high_chunk(VB)
            high_chunk(K0)
            for n, t in enumerate(toks):
                job, r = ("V", t, 0), rows(t)
                wait_made(act, job)
                A(v[0:r, t, 0:VC], ps[0:r, 3 * side(job), 0:VC], ACT.Copy).then_inc(used[side(job)], 1)

            def copy_heads(n):
                kind, t, part = qk[n]
                r = rows(t)
                act.wait_ge(heads_turned, n + 1)
                if n == 0:
                    act.wait_ge(conv_done, CT)
                own = slice(HH * part, HH * (part + 1))
                dst = kT[0:AUG, own, slice(*u_cols(t))] if kind == "K" else qT[0:AUG, own, P * t:P * (t + 1)]
                A(dst, turned_heads(n).rearrange("p (h n) -> p h n", h=HH)[:, :, 0:r],
                  ACT.Copy).then_inc(heads_out, 1)

            for n, job in enumerate(qk):
                r = rows(job[1])
                wait_made(act, job)
                if n:
                    act.wait_ge(ss_ready, n)
                A(sq[0:r, :], ps[0:r, 3 * side(job), 0:AW // 2], ACT.Square).then_inc(sq_ready, 1)
                if n in next_chunk:
                    high_chunk(next_chunk[n])
                act.wait_ge(ss_ready, n + 1)
                inv_root(stat[0:r, n % 2, 0:HH], stat[0:r, n % 2, 0:HH], 1.0 / HD).then_inc(rk_ready, 1)
                if n:
                    copy_heads(n - 1)
            copy_heads(len(qk) - 1)

            def evict(n):
                for g, js in enumerate(groups(heads[n][0])):
                    no = group_no(n, g)
                    if no % 2:
                        act.wait_ge(pt_made, no + 1)
                        if n >= 2:
                            act.wait_ge(pv_done, n - 1)
                        A(pT[:, n % 2, P * js[0]:P * (js[-1] + 1)], ps[:, pt_bank(n, no), 0:P * len(js)],
                          ACT.Copy).then_inc(pt_out[1], 1)

            def extra(kind, i):
                if kind == "ASQ":
                    act.wait_ge(o_taken, i + 1)
                    if i:
                        wait_made(act, ("M", i - 1))
                    then(A(asq[:, :], ot[:, :], ACT.Square))
                    A(asqh[:, :], asq[:, :], ACT.Copy).then_inc(asqh_ready, 1)
                elif kind == "ARS":
                    job = ("M", i)
                    wait_made(act, job)
                    if i:
                        act.wait_ge(aT_ready, i)
                    A(rsa[:, :], ps[:, 3 * side(job), :], ACT.Ln).then_inc(used[side(job)], 1)
                    wait_used(act, job)
                    A(rsa[:, :], rsa[:, :], ACT.Exp, scale=-0.5).then_inc(rsa_ready, 1)
                elif kind == "AH":
                    act.wait_ge(aT_ready, i + 1)
                    if i:
                        wait_made(act, ("W", i - 1))
                    A(aTh[:, :, :], aT[:, :, :], ACT.Copy).then_inc(aTh_ready, 1)
                elif kind == "URS":
                    wait_used(act, ("W", i))
                    then(A(u2sq[:, :], h1b[:, :], ACT.Square, accum_out=ms[:, 2:3]))
                    inv_root(ms[:, 2:3], ms[:, 2:3], 1.0 / D).then_inc(u2rs_ready, 1)
                else:
                    job = ("U", i)
                    wait_made(act, job)
                    if i:
                        wait_made(act, ("L", i - 1))
                    A(u2Th[:, :, :].rearrange("p k n -> p (k n)"), buf(job, D), ACT.Copy).then_inc(u2Th_ready, 1)

            extras = {1: "ASQ", 3: "ARS", 5: "URS", 6: "U"}
            for n, (i, h) in enumerate(heads):
                if n:
                    evict(n - 1)
                act.wait_ge(max_ready, n + 1)
                if n >= 2:
                    last = len(groups(heads[n - 2][0])) - 1
                    act.wait_ge(pt_made, group_no(n - 2, last) + 1)
                job = ("S", i, h)
                A(probs[:, n % 2, 0:width(i)].rearrange("p (b n) -> p b n", b=banks(i)),
                  score_buf(i, h), ACT.Exp, bias=negmax[:, n % 2:n % 2 + 1],
                  accum_out=rowsum[:, i % 2, h:h + 1]).then_inc(used[side(job)], 1)
                if 8 <= n < 8 + CT:
                    act.wait_ge(wo_ready, n - 7)
                    A(woh[:, n - 8, :], wo[:, n - 8, :], ACT.Copy).then_inc(woh_ready, 1)
                if i and h in extras:
                    extra(extras[h], i - 1)
                    if h == 3:
                        extra("AH", i - 1)
            evict(NH - 1)
            for kind in ("ASQ", "ARS", "AH", "URS", "U"):
                extra(kind, NT - 1)
            def high(m, b, s, slot, after):
                act.wait_ge(w_in_sems[m][s], 16 * ((b - s) // 2 + 1))
                for n in range(2):
                    if after is not None:
                        act.wait_ge(w_used, after - 5 + n)
                    A(half(wh, slot, n), half(raw[m], s, n), ACT.Copy).then_inc(w_high[m], 1)

            high("g", 0, 0, 0, None)
            high("u", 0, 0, 1, None)
            act.wait_ge(gate_ask, 1)
            A(r4[0][:, :, :], r4[0][:, :, :], ACT.Exp)
            A(r8[0][:, 0, :], r8[0][:, 0, :], ACT.Exp).then_inc(gate_exp, 1)
            act.wait_ge(route_ready, 1)
            nc.scalar.sem_inc(y_taken, 1)
            last = act.value_load(last_pair[0:1, 0:1], min_val=NE - 2, max_val=NE + MAX_OVER - 1)

            def high_x(b):
                act.wait_ge(x_turned, b + 1)
                A(xh[:, :, :].rearrange("p k n -> p (k n)"), big[:, 0:D], ACT.Copy).then_inc(xh_ready, 1)

            def silu(b):
                act.wait_ge(w_used, used_after("g", b))
                A(sil[:, :], ps[:, 2, :], ACT.Silu).then_inc(sil_ready, 1)

            def high_hidden(b):
                act.wait_ge(hid_turned, b + 1)
                A(hh[:, :, :].rearrange("p k n -> p (k n)"), ps[:, 4, :], ACT.Copy).then_inc(hh_ready, 1)

            def take_y(b, s, after):
                act.wait_ge(w_used, after)
                act.wait_ge(yb_free, b + 1)
                A(yb[:, s, :], big[:, 5 * 512:7 * 512], ACT.Copy).then_inc(y_taken, 1)

            def blocks(b, s, more):
                high("u", b + 1, 1 - s, 1 - s, used_after("u", b + 1))
                high_hidden(b)
                silu(b + 1)
                high("d", b, s, s, used_after("d", b))
                if more:
                    high_x(b + 2)
                    high("g", b + 2, s, 1 - s, used_after("g", b + 2))
                take_y(b, s, used_after("d", b))

            high_x(0)
            high("g", 1, 1, 0, used_after("g", 1))
            silu(0)
            high_x(1)
            with act.Fori(0, last, 2) as i:
                for s in range(2):
                    blocks(i + s, s, True)
            blocks(last, 0, False)
            high_hidden(last + 1)
            high("d", last + 1, 1, 1, used_after("last d", last + 1))
            take_y(last + 1, 1, used_after("last d", last + 1))
            for t in range(NT):
                act.wait_ge(fin_ready, t + 1)
                act.dma_start(out[P * t:P * (t + 1), :], h1t[:, t, :]).then_inc(fin_out, 16)
            act.wait_ge(fin_out, 16 * NT)

        @block.vector
        def _(dve):
            count = [0]
            V = nc.vector

            def then(ins):
                count[0] += 1
                ins.then_inc(dve_step, 1)
                dve.wait_ge(dve_step, count[0])

            def bc(ap, shape):
                return ap.unsqueeze(2).broadcast_to(shape)

            def low_chunk(u):
                for n in range(2):
                    dve.wait_ge(chunk_high, 2 * u + n + 1)
                    V.tensor_tensor(chunk_half(chunk_parts[u][1], u, n), chunk_half(chunk_raw[u], u, n),
                                    chunk_half(chunk_parts[u][0], u, n).bitcast(F32),
                                    ALU.subtract).then_inc(chunk_low, 1)

            def low_u(t, n):
                job, r = ("T", t), rows(t)
                dve.wait_ge(uh_ready, n + 1)
                a, b = u_cols(t)
                V.tensor_tensor(ul[:, :, a:b], buf(job, KT * P).rearrange("p (k n) -> p k n", k=KT)[:, :, 0:r],
                                uh[:, :, a:b].bitcast(F32), ALU.subtract).then_inc(used[side(job)], 1)

            dve.wait_ge(gmix_in, 16)
            for n, t in enumerate(toks):
                r = rows(t)
                dve.wait_ge(rs_ready, n + 1)
                if n >= 2:
                    wait_made(dve, ("T", toks[n - 2]))
                V.scalar_tensor_tensor(hn[0:r, n % 2, :], xin[0:r, n, :], ms[0:r, n % 2:n % 2 + 1],
                                       gmix_b[0:r, :], ALU.mult, ALU.mult).then_inc(hn_ready, 1)
                if n:
                    low_u(toks[n - 1], n - 1)
            low_u(toks[-1], NT)
            low_chunk(0)
            low_chunk(1)
            dve.wait_ge(consts, 2)
            dve.wait_ge(params, 16 * NPAR)
            dve.wait_ge(exact_ready, 3)
            V.tensor_tensor(wrl[:, :, :], wr[:, :, :], wrh[:, :, :].bitcast(F32), ALU.subtract).then_inc(wrl_ready, 1)
            then(V.tensor_scalar(gqk_b[:, 0, :], gqk_b[:, 0, :], HD ** -0.5, None, ALU.mult))
            then(V.tensor_tensor(gqk_b[:, 0, :], gqk_b[:, 0, :], gqk_b[:, 1, :], ALU.mult))

            def conv_norm(c):
                dve.wait_ge(rsb_ready, c + 1)
                V.scalar_tensor_tensor(conv[:, c, :], conv[:, c, :], gconvT[:, c:c + 1], rsb[:, :],
                                       ALU.mult, ALU.mult).then_inc(conv_done, 1)

            for c in range(CT):
                job = ("H", c)
                wait_made(dve, job)
                wait_used(dve, ("C", c))
                b0 = 3 * side(job)
                V.tensor_tensor(uc[:, :].rearrange("p (j n) -> p j n", j=3), ps[:, b0:b0 + 3, 0:(T + 2) // 3],
                                csb[:, :].rearrange("p (j n) -> p j n", j=3), ALU.mult).then_inc(used[side(job)], 1)
                wait_used(dve, job)
                y = conv[:, c, :]
                then(V.tensor_scalar(y, uc[:, 0:T], convwT[:, 0, c:c + 1], None, ALU.mult))
                for n in (1, 2):
                    then(V.scalar_tensor_tensor(y, uc[:, n:n + T], convwT[:, n, c:c + 1], y, ALU.mult, ALU.add))
                job = ("B", c)
                wait_made(dve, job)
                V.tensor_tensor(y, y, buf(job, T), ALU.mult).then_inc(used[side(job)], 1)
                if c:
                    conv_norm(c - 1)
                low_chunk(c + 2)
            conv_norm(CT - 1)
            for c in range(CT):
                dve.wait_ge(conv_h_ready, c + 1)
                V.tensor_tensor(conv_l[:, c, :], conv[:, c, :], conv_h[:, c, :].bitcast(F32),
                                ALU.subtract).then_inc(conv_l_ready, 1)
            for t in toks[-2:]:
                wait_used(dve, ("V", t, 1))
            then(V.tensor_tensor(fz[:, :, :], fz[:, :, :], bf_b[:, :].unsqueeze(1).broadcast_to([P, NT + 1, H]),
                                 ALU.add))
            V.scalar_tensor_tensor(fe[:, :, :], fz[:, :, :], -1.0, fz[:, :, :], ALU.mult, ALU.max).then_inc(f_ready, 1)
            low_chunk(Z0 + 1)
            dve.wait_ge(fe_ready, 1)
            for r, a, b in ((P, 0, NT), (META, NT, NT + 1)):
                ins = V.scalar_tensor_tensor(lf[0:r, a:b, :], fz[0:r, a:b, :], 0.0, fe[0:r, a:b, :],
                                             ALU.min, ALU.subtract)
            then(ins)
            V.memset(facc[:, NT, :], 0.0)
            then(V.tensor_copy(facc[:, 0, :], lf[:, NT, :]))
            for t in range(1, NT):
                ins = V.tensor_tensor(facc[:, t, :], facc[:, t - 1, :], lf[:, t - 1, :], ALU.add)
                if t < NT - 1:
                    then(ins)
            ins.then_inc(lf_ready, 1)
            for part in range(2):
                for t in range(NT):
                    job, n = ("Z", t, part), t // (NT // 2)
                    wait_made(dve, job)
                    dve.wait_ge(zx_in[part][n], 16)
                    V.tensor_tensor(zx[:, t, :], zx[:, t, :], ps[:, 3 * side(job), :],
                                    ALU.add).then_inc(used[side(job)], 1)
                low_chunk(VB + part)
            job = ("CUM", 0)
            wait_made(dve, job)
            V.tensor_copy(cum[:, :, :].rearrange("p t h -> p (t h)"),
                          buf(job, (NT + 1) * H)).then_inc(used[side(job)], 1)
            wait_used(dve, job)

            for n, job in enumerate(qk):
                kind, t, part = job
                r = rows(t)
                dve.wait_ge(sq_ready, n + 1)
                if n >= 2:
                    dve.wait_ge(rk_ready, n - 1)
                V.tensor_reduce(stat[0:r, n % 2, 0:HH], sq[0:r, :].rearrange("p (h d) -> p h d", h=HH), AX.X,
                                ALU.add).then_inc(ss_ready, 1)
                dst = kn[0:r, n % 2, :, :]
                if n >= 2:
                    dve.wait_ge(heads_turned, n - 1)
                own = cum[0:r, t, HH * part:HH * (part + 1)]
                if kind == "K":
                    V.tensor_scalar(dst[:, :, HD], own, -1.0, None, ALU.mult)
                else:
                    V.memset(dst[:, :, HD], 1.0)
                    V.tensor_copy(dst[:, :, HD + 1], own)
                dve.wait_ge(rk_ready, n + 1)
                src = ps[0:r, 3 * side(job), 0:AW // 2].rearrange("p (h d) -> p h d", h=HH)
                V.tensor_tensor(dst[:, :, 0:HD], src, bc(stat[0:r, n % 2, 0:HH], [r, HH, HD]),
                                ALU.mult).then_inc(used[side(job)], 1)
                wait_used(dve, job)
                if kind == "Q":
                    V.tensor_tensor(dst[:, :, 0:HD], dst[:, :, 0:HD],
                                    gqk_b[:, 0, :].unsqueeze(1).broadcast_to([P, HH, HD]),
                                    ALU.mult).then_inc(kn_ready, 1)
                else:
                    dve.sem_inc(kn_ready, 1)
                if n in next_chunk:
                    low_chunk(next_chunk[n])

            def extra(kind, i):
                if kind == "O":
                    dve.wait_ge(pv_done, H * (i + 1))
                    if i:
                        dve.wait_ge(aT_ready, i)
                    V.tensor_copy(ot[:, :], ps[:, OB, :]).then_inc(o_taken, 1)
                    V.scalar_tensor_tensor(l2[:, :], rowsum[:, i % 2, :], EPS, rowsum[:, i % 2, :], ALU.mult,
                                           ALU.mult).then_inc(l2_ready, 1)
                elif kind == "N":
                    job = ("N", i)
                    wait_made(dve, job)
                    then(V.tensor_copy(l2Th[:, :], ps[0:H, 3 * side(job), 0:P]))
                    V.tensor_tensor(l2Tl[:, :], ps[0:H, 3 * side(job), 0:P], l2Th[:, :].bitcast(F32),
                                    ALU.subtract).then_inc(used[side(job)], 1)
                    dve.wait_ge(asqh_ready, i + 1)
                    V.tensor_tensor(asql[:, :], asq[:, :], asqh[:, :].bitcast(F32),
                                    ALU.subtract).then_inc(asql_ready, 1)
                elif kind == "M":
                    dve.wait_ge(rsa_ready, i + 1)
                    if i:
                        wait_made(dve, ("W", i - 1))
                    V.tensor_tensor(aT[:, :, :].rearrange("p k n -> p (k n)"), ot[:, :], rsa[:, :],
                                    ALU.mult).then_inc(aT_ready, 1)
                elif kind == "AL":
                    dve.wait_ge(aTh_ready, i + 1)
                    V.tensor_tensor(aTl[:, :, :], aT[:, :, :], aTh[:, :, :].bitcast(F32),
                                    ALU.subtract).then_inc(aTl_ready, 1)
                elif kind == "W":
                    job = ("W", i)
                    wait_made(dve, job)
                    dve.wait_ge(xr_in, 16 * (i + 1))
                    V.tensor_tensor(h1b[:, :], buf(job, D), h1b[:, :], ALU.add).then_inc(used[side(job)], 1)
                elif kind == "U2":
                    dve.wait_ge(u2rs_ready, i + 1)
                    if i:
                        dve.wait_ge(rows_out, 16 * i)
                        wait_made(dve, ("U", i - 1))
                    V.scalar_tensor_tensor(u2[:, :], h1b[:, :], ms[:, 2:3], gffn_b[:, :], ALU.mult,
                                           ALU.mult).then_inc(u2_ready, 1)
                elif kind == "U":
                    job = ("U", i)
                    dve.wait_ge(u2Th_ready, i + 1)
                    V.tensor_tensor(u2Tl[:, :, :].rearrange("p k n -> p (k n)"), buf(job, D),
                                    u2Th[:, :, :].rearrange("p k n -> p (k n)").bitcast(F32),
                                    ALU.subtract).then_inc(used[side(job)], 1)
                else:
                    job = ("L", i)
                    wait_made(dve, job)
                    V.tensor_scalar(lT[0:NG + NE, P * i:P * (i + 1)], ps[0:NG + NE, 3 * side(job), 0:P],
                                    br_c[:, :], None, ALU.add).then_inc(used[side(job)], 1)

            def evict(n):
                for g, js in enumerate(groups(heads[n][0])):
                    no = group_no(n, g)
                    if no % 2 == 0:
                        dve.wait_ge(pt_made, no + 1)
                        if n >= 2:
                            dve.wait_ge(pv_done, n - 1)
                        V.tensor_copy(pT[:, n % 2, P * js[0]:P * (js[-1] + 1)],
                                      ps[:, pt_bank(n, no), 0:P * len(js)]).then_inc(pt_out[0], 1)

            extras = {1: ("O",), 2: ("N",), 3: ("M",), 4: ("AL", "W"), 5: ("U2",), 6: ("U",), 7: ("L",)}
            for n, (i, h) in enumerate(heads):
                job = ("S", i, h)
                wait_made(dve, job)
                if n >= 2:
                    wait_used(dve, ("S", *heads[n - 2]))
                V.tensor_reduce(negmax[:, n % 2:n % 2 + 1], score_buf(i, h), AX.XY, ALU.max,
                                negate=True).then_inc(max_ready, 1)
                if n:
                    evict(n - 1)
                if 9 <= n < 9 + CT:
                    dve.wait_ge(woh_ready, n - 8)
                    V.tensor_tensor(wol[:, n - 9, :], wo[:, n - 9, :], woh[:, n - 9, :].bitcast(F32),
                                    ALU.subtract).then_inc(wol_ready, 1)
                if 8 <= n < 8 + CT:
                    k = n - 8
                    if k == 0:
                        dve.wait_ge(wo_in, 32)
                    V.tensor_scalar(wo[:, k, :], wo[:, k, :], gattnT[:, k:k + 1], None,
                                    ALU.mult).then_inc(wo_ready, 1)
                if i and h in extras:
                    for kind in extras[h]:
                        extra(kind, i - 1)
            evict(NH - 1)
            for kind in ("O", "N", "M", "AL", "W", "U2", "U", "L"):
                extra(kind, NT - 1)

            dve.wait_ge(h1_out, 16 * NT)
            dve.wait_ge(rows_out, 16 * NT)
            job = ("LT", 0)
            wait_made(dve, job)
            V.tensor_copy(logits[:, :, :].rearrange("p t g -> p (t g)"),
                          buf(job, NT * (NG + NE))).then_inc(used[side(job)], 1)
            wait_used(dve, job)
            gl, e_l = logits[:, :, 0:NG], logits[:, :, NG:]
            gmax, gidx = r8[1][:, 0, :], r8[1][:, 1, :]
            iota_g = iota128[:, 0:NG].unsqueeze(1).broadcast_to([P, NT, NG])
            iota_e = iota128[:, 0:NE].unsqueeze(1).broadcast_to([P, NT, NE])

            def first_max(dst_max, dst_idx, src, scratch, iota, n):
                then(V.tensor_reduce(dst_max, src, AX.X, ALU.max))
                then(V.tensor_tensor(scratch, src, bc(dst_max, [P, NT, n]), ALU.is_equal))
                then(V.scalar_tensor_tensor(scratch, scratch, -100.0, iota, ALU.mult, ALU.add))
                then(V.tensor_reduce(dst_idx, scratch, AX.X, ALU.min))
                then(V.tensor_scalar(dst_idx, dst_idx, 100.0, None, ALU.add))

            first_max(gmax, gidx, gl, r4[0][:, :, :], iota_g, NG)
            then(V.tensor_tensor(r4[1][:, :, :], iota_g, bc(gidx, [P, NT, NG]), ALU.is_equal))
            oh = r4[1][:, :, :].rearrange("p t g -> p (t g)").unsqueeze(2).broadcast_to([P, NT * NG, EG])
            e4 = et[:, :, :].rearrange("p t (g e) -> p (t g) e", g=NG)
            then(V.tensor_copy(e4, oh))
            then(V.tensor_tensor(el[:, :, :], e_l, et[:, :, :], ALU.mult))
            then(V.tensor_scalar(et[:, :, :], et[:, :, :], 1.0, -NEG, ALU.subtract, ALU.mult))
            then(V.tensor_tensor(el[:, :, :], el[:, :, :], et[:, :, :], ALU.add))
            m0, x0 = r8[2][:, 0, :], r8[3][:, 0, :]
            m1, x1 = r8[2][:, 1, :], r8[3][:, 1, :]
            first_max(m0, x0, el[:, :, :], et[:, :, :], iota_e, NE)
            then(V.tensor_tensor(one0[:, :, :], iota_e, bc(x0, [P, NT, NE]), ALU.is_equal))
            then(V.scalar_tensor_tensor(el[:, :, :], one0[:, :, :], 2 * NEG, el[:, :, :], ALU.mult, ALU.add))
            first_max(m1, x1, el[:, :, :], et[:, :, :], iota_e, NE)
            then(V.tensor_tensor(one1[:, :, :], iota_e, bc(x1, [P, NT, NE]), ALU.is_equal))
            then(V.tensor_tensor(r8[0][:, 0, :], m1, m0, ALU.subtract))
            V.tensor_tensor(r4[0][:, :, :], gl, bc(gmax, [P, NT, NG]), ALU.subtract).then_inc(gate_ask, 1)
            then(V.tensor_tensor(both[:, :, :], one0[:, :, :], one1[:, :, :], ALU.add))
            then(V.memset(prev[:, 0, :], 0.0))
            for t in range(1, NT + 1):
                ins = V.tensor_tensor(prev[:, t, :], prev[:, t - 1, :], both[:, t - 1, :], ALU.add)
                if t < NT:
                    then(ins)
            ins.then_inc(gate_ask, 1)
            dve.wait_ge(gate_exp, 1)
            then(V.tensor_reduce(r8[4][:, 0, :], r4[0][:, :, :], AX.X, ALU.add))
            then(V.tensor_scalar(r8[4][:, 1, :], r8[0][:, 0, :], 1.0, None, ALU.add))
            then(V.tensor_tensor(r8[4][:, 0, :], r8[4][:, 0, :], r8[4][:, 1, :], ALU.mult))
            then(V.reciprocal(gates[:, 0, :], r8[4][:, 0, :]))
            then(V.tensor_tensor(gates[:, 1, :], gates[:, 0, :], r8[0][:, 0, :], ALU.mult))
            job = ("RANK", 0)
            wait_made(dve, job)
            b0 = 3 * side(job)
            V.tensor_copy(cnt[:, :], ps[:, b0, NT * NE:(NT + 1) * NE])
            V.tensor_copy(ranks[:, :, :].rearrange("p t e -> p (t e)"), ps[:, b0, 0:NT * NE]).then_inc(used[side(job)], 1)
            wait_used(dve, job)
            rank, jblk, row, col, ovs, gt0 = (r8[n][:, :, :] for n in (4, 5, 6, 7, 8, 9))
            for k, one in ((0, one0), (1, one1)):
                then(V.tensor_tensor(et[:, :, :], one[:, :, :], ranks[:, :, :], ALU.mult))
                then(V.tensor_reduce(rank[:, k, :], et[:, :, :], AX.X, ALU.add))
            lim = t256[:, 0, 0:7]
            then(V.tensor_scalar(lim, iota128[:, 1:8], float(P), None, ALU.mult))
            c7 = cmp7[:, :, 0:7]
            then(V.tensor_tensor(c7, bc(cnt[:, :], [P, NE, 7]), lim.unsqueeze(1).broadcast_to([P, NE, 7]), ALU.is_gt))
            then(V.tensor_reduce(nover[:, :], c7, AX.X, ALU.add))
            then(V.tensor_copy(over[:, 0, :], nover[:, :]))
            cur = 0
            for d in (1, 2, 4, 8, 16):
                then(V.tensor_copy(over[:, 1 - cur, 0:d], over[:, cur, 0:d]))
                then(V.tensor_tensor(over[:, 1 - cur, d:], over[:, cur, d:], over[:, cur, 0:NE - d], ALU.add))
                cur = 1 - cur
            end = over[:, cur, :]
            begin = over[:, 1 - cur, :]
            then(V.tensor_tensor(begin, end, nover[:, :], ALU.subtract))
            for k, one in ((0, one0), (1, one1)):
                then(V.tensor_tensor(et[:, :, :], one[:, :, :], begin.unsqueeze(1).broadcast_to([P, NT, NE]), ALU.mult))
                then(V.tensor_reduce(ovs[:, k, :], et[:, :, :], AX.X, ALU.add))
            lim1 = lim.unsqueeze(1).broadcast_to([P, 16, 7])
            c16 = t256[:, :, 8:15]
            flat = r8[4][:, :, :].rearrange("p k t -> p (k t)")
            then(V.tensor_tensor(c16, bc(flat, [P, 16, 7]), lim1, ALU.is_ge))
            then(V.tensor_reduce(r8[5][:, :, :].rearrange("p k t -> p (k t)"), c16, AX.X, ALU.add))
            then(V.scalar_tensor_tensor(row, jblk, -float(P), rank, ALU.mult, ALU.add))
            then(V.tensor_scalar(gt0, jblk, 0.0, None, ALU.is_gt))
            then(V.scalar_tensor_tensor(col, jblk, float(NE - 1), ovs, ALU.add, ALU.add))
            then(V.tensor_tensor(col, col, r8[3][:, :, :], ALU.subtract))
            then(V.tensor_tensor(col, col, gt0, ALU.mult))
            then(V.tensor_tensor(col, col, r8[3][:, :, :], ALU.add))
            code = r8[0][:, :, :]
            V.tensor_copy(code[:, 0, :], tokcode[:, :])
            then(V.tensor_scalar(code[:, 1, :], tokcode[:, :], float(T), None, ALU.add))
            flat_col, flat_code = (a.rearrange("p k t -> p (k t)") for a in (col, code))
            then(V.tensor_tensor(hot[:, :, :], iota128[:, 0:COLS].unsqueeze(1).broadcast_to([P, 2 * NT, COLS]),
                                 bc(flat_col, [P, 2 * NT, COLS]), ALU.is_equal))
            V.tensor_tensor(colhot[:, :, :], hot[:, :, :], bc(flat_code, [P, 2 * NT, COLS]), ALU.mult)
            V.tensor_tensor(rowhot[:, :, :], iota128[:, :].unsqueeze(1).broadcast_to([P, 2 * NT, P]),
                            bc(row.rearrange("p k t -> p (k t)"), [P, 2 * NT, P]), ALU.is_equal).then_inc(gate_ask, 1)
            NX = COLS - NE
            then(V.tensor_tensor(bcmp[:, 0:NX, :], end.unsqueeze(1).broadcast_to([P, NX, NE]),
                                 bc(iota128[:, 0:NX], [P, NX, NE]), ALU.is_le))
            then(V.tensor_reduce(tabf[0][:, 0:NX], bcmp[:, 0:NX, :], AX.X, ALU.add))
            V.tensor_scalar(bexp[:, NE:], tabf[0][:, 0:NX], float(NE - 1), None, ALU.min)
            V.tensor_copy(bexp[:, 0:NE], iota128[:, 0:NE])
            then(V.tensor_scalar(last_pair[:, :], end[:, NE - 1:NE], float(NE - 1), None, ALU.add))
            V.tensor_scalar(last_pair[:, :], last_pair[:, :], -2, None, ALU.bitwise_and)
            job = ("TABLE", 0)
            wait_made(dve, job)
            c, pad, hi = (tabf[n][:, :] for n in range(3))
            V.tensor_copy(c, buf(job, COLS)).then_inc(used[side(job)], 1)
            wait_used(dve, job)
            then(V.tensor_scalar(pad, c, 0.5, float(NOWHERE), ALU.is_lt, ALU.mult))
            then(V.scalar_tensor_tensor(pad, c, -1.0, pad, ALU.add, ALU.add))
            V.tensor_copy(stab[:, :], pad)
            then(V.tensor_scalar(hi, c, T + 0.5, -float(T), ALU.is_gt, ALU.mult))
            V.tensor_tensor(gtab[:, :], pad, hi, ALU.add).then_inc(route_ready, 1)

            dve.wait_ge(route_ready, 1)
            last = dve.value_load(last_pair[0:1, 0:1], min_val=NE - 2, max_val=NE + MAX_OVER - 1)

            def rest(dst, src, high_part):
                return V.tensor_tensor(dst, src, high_part.bitcast(F32), ALU.subtract)

            def low_x(b):
                dve.wait_ge(xh_ready, b + 1)
                rest(xl[:, :, :].rearrange("p k n -> p (k n)"), big[:, 0:D],
                     xh[:, :, :].rearrange("p k n -> p (k n)")).then_inc(xl_ready, 1)

            def low(m, b, s, slot):
                for n in range(2):
                    dve.wait_ge(w_high[m], 2 * b + n + 1)
                    rest(half(wl, slot, n), half(raw[m], s, n), half(wh, slot, n)).then_inc(w_low[m], 1)

            def hidden(b):
                dve.wait_ge(sil_ready, b + 1)
                dve.wait_ge(w_used, used_after("u", b))
                V.tensor_tensor(hid[:, :], sil[:, :], ps[:, 3, :], ALU.mult).then_inc(hid_ready, 1)

            def low_hidden(b):
                dve.wait_ge(hh_ready, b + 1)
                rest(hl[:, :, :].rearrange("p k n -> p (k n)"), ps[:, 4, :],
                     hh[:, :, :].rearrange("p k n -> p (k n)")).then_inc(hl_ready, 1)

            def blocks(b, s, more):
                low("u", b + 1, 1 - s, 1 - s)
                low_hidden(b)
                low("d", b, s, s)
                hidden(b + 1)
                if more:
                    low_x(b + 2)
                    low("g", b + 2, s, 1 - s)

            low_x(0)
            low("g", 1, 1, 0)
            hidden(0)
            low_x(1)
            with dve.Fori(0, last, 2) as i:
                for s in range(2):
                    blocks(i + s, s, True)
            blocks(last, 0, False)
            low_hidden(last + 1)
            low("d", last + 1, 1, 1)

            for t in range(NT):
                dve.wait_ge(y_in[t], 48)
                then(V.scalar_tensor_tensor(h1t[:, t, :], y0[:, t, :], gates[:, 0, t:t + 1], h1t[:, t, :],
                                            ALU.mult, ALU.add))
                V.scalar_tensor_tensor(h1t[:, t, :], y1[:, t, :], gates[:, 1, t:t + 1], h1t[:, t, :],
                                       ALU.mult, ALU.add).then_inc(fin_ready, 1)


_ORDER = ["x", "meta_tokens", "norm_mix_g", "w_in", "b_forget", "q_norm_g", "k_norm_g", "conv_w", "attn_out_g",
          "conv_out_g", "w_out", "norm_ffn_g", "w_router_group", "b_router_group", "w_router_expert",
          "b_router_expert", "w_gate", "w_up", "w_down"]


def kernel(**inputs):
    import numpy as _np
    import concourse.bacc as _bacc
    from concourse import mybir as _mybir
    from concourse.bass_utils import run_bass_kernel_spmd as _run

    nc = _bacc.Bacc("TRN2", target_bir_lowering=False, num_devices=1)
    arrays, args = {}, []
    for name in _ORDER:
        a = _np.ascontiguousarray(inputs[name])
        if name != "meta_tokens":
            a = a[0]
        arrays[f"in_{name}"] = a
        args.append(nc.dram_tensor(f"in_{name}", a.shape, _mybir.dt.from_np(a.dtype), kind="ExternalInput").ap())
    args.append(nc.dram_tensor("out_0", (T, D), F32, kind="ExternalOutput").ap())
    build(nc, *args)
    r = _run(nc, [arrays], core_ids=[0])
    return r.results[0]["out_0"].reshape(1, T, D)
```
